# Optimizing a Trainium2 kernel written in Bass

```python
import math
import jax, jax.numpy as jnp
from jax import lax
import numpy as np

D_MODEL = 1024
BATCH = 1
SEQ = 256
DEPTH = 2

GRID_W = 64
CTX_LEN = 256
Q_BLOCK = 128
ROPE_THETA = 10000.0
EPS = 1e-6

MLA_HEADS = 4
MLA_Q_LORA = 256
MLA_KV_LORA = 128
MLA_NOPE = 64
MLA_ROPE = 32
MLA_V = 64
MLA_QK = MLA_NOPE + MLA_ROPE
MLA_IN = MLA_Q_LORA + MLA_KV_LORA + MLA_ROPE

GQA_Q_HEADS = 4
GQA_KV_HEADS = 2
GQA_GROUP = GQA_Q_HEADS // GQA_KV_HEADS
GQA_HEAD_DIM = 64
GQA_IN = (GQA_Q_HEADS + 2 * GQA_KV_HEADS) * GQA_HEAD_DIM

ML_HEADS = 4
ML_HEAD_DIM = 64
ML_WIDTH = ML_HEADS * ML_HEAD_DIM
ML_CHUNK = 64
ML_IN = 4 * ML_WIDTH + 4 * ML_HEADS

HY_WIDTH = 256
HY_ORDER = 2
HY_BANDS = 16
HY_FEAT = 1 + 2 * HY_BANDS
HY_HIDDEN = 64
HY_IN = (HY_ORDER + 1) * HY_WIDTH
HY_DECAY_TARGET = 1e-2
HY_SHORT_PCT = 0.3
HY_LONG_PCT = 1.5

N_BRANCH = 4
BRANCH_W = 256
GATE_IN = N_BRANCH * D_MODEL
IN_OFFSETS = (MLA_IN, MLA_IN + GQA_IN, MLA_IN + GQA_IN + ML_IN, MLA_IN + GQA_IN + ML_IN + HY_IN)
D_IN = MLA_IN + GQA_IN + ML_IN + HY_IN + GATE_IN

PEER_HEADS = 8
PEER_NKEYS = 128
PEER_EXPERTS = PEER_NKEYS * PEER_NKEYS
PEER_DK = 256
PEER_TOPK = 16
PEER_BLOCK = 128

kernel_name = "hybrid_prefix_dit_mla_gqa_mlstm_hyena_peer"

def rms_norm(x, g):
    xf = x.astype(jnp.float32)
    y = xf * lax.rsqrt(jnp.mean(xf * xf, axis=-1, keepdims=True) + EPS)
    return (y * g.astype(jnp.float32)).astype(x.dtype)

def modulate(x, g, shift, scale):
    return rms_norm(x, g) * (1.0 + scale) + shift

def axial_rope_tables(rows, cols, d_rot):
    m = d_rot // 2
    inv = ROPE_THETA ** (-jnp.arange(0, m, 2, dtype=jnp.float32) / m)
    ar = rows.astype(jnp.float32)[:, None] * inv
    ac = cols.astype(jnp.float32)[:, None] * inv
    return (jnp.cos(ar), jnp.sin(ar), jnp.cos(ac), jnp.sin(ac))

def _rotate(x, cos, sin):
    x1, x2 = jnp.split(x, 2, axis=-1)
    return jnp.concatenate([x1 * cos - x2 * sin, x2 * cos + x1 * sin], axis=-1)

def apply_axial_rope(x, tables):
    extra = x.ndim - 3
    t = [a.reshape((a.shape[0],) + (1,) * extra + (a.shape[1],)) for a in tables]
    xr, xc = jnp.split(x.astype(jnp.float32), 2, axis=-1)
    out = jnp.concatenate([_rotate(xr, t[0], t[1]), _rotate(xc, t[2], t[3])], axis=-1)
    return out.astype(x.dtype)

def attend(q, k, v, scale):
    s = jnp.einsum('bqhgd,bkhd->bhgqk', q, k, preferred_element_type=jnp.float32) * scale
    p = jax.nn.softmax(s, axis=-1).astype(v.dtype)
    return jnp.einsum('bhgqk,bkhd->bqhgd', p, v)

def latent_attention(q_lat, k_ctx, v_ctx, k_lat, v_lat, scale):
    k_all = jnp.concatenate([k_ctx, k_lat], axis=1)
    v_all = jnp.concatenate([v_ctx, v_lat], axis=1)
    B, S = q_lat.shape[:2]
    qb = jnp.moveaxis(q_lat.reshape((B, S // Q_BLOCK, Q_BLOCK) + q_lat.shape[2:]), 1, 0)
    ob = lax.map(lambda qi: attend(qi, k_all, v_all, scale), qb)
    return jnp.moveaxis(ob, 0, 1).reshape(B, S, -1)

def mla_qkv(u, q_norm, kv_norm, w_uq, w_ukv, qk_norm_q, qk_norm_k, rope):
    B, L = u.shape[:2]
    c_q = u[..., :MLA_Q_LORA]
    c_kv = u[..., MLA_Q_LORA:MLA_Q_LORA + MLA_KV_LORA]
    k_pe = u[..., MLA_Q_LORA + MLA_KV_LORA:]
    q = (rms_norm(c_q, q_norm) @ w_uq).reshape(B, L, MLA_HEADS, MLA_QK)
    kv = (rms_norm(c_kv, kv_norm) @ w_ukv).reshape(B, L, MLA_HEADS, MLA_NOPE + MLA_V)
    k = jnp.concatenate([kv[..., :MLA_NOPE],
                         jnp.broadcast_to(k_pe[:, :, None, :], (B, L, MLA_HEADS, MLA_ROPE))], axis=-1)
    v = kv[..., MLA_NOPE:]
    q = rms_norm(q, qk_norm_q)
    k = rms_norm(k, qk_norm_k)
    if rope is not None:
        q = jnp.concatenate([q[..., :MLA_NOPE], apply_axial_rope(q[..., MLA_NOPE:], rope)], axis=-1)
        k = jnp.concatenate([k[..., :MLA_NOPE], apply_axial_rope(k[..., MLA_NOPE:], rope)], axis=-1)
    return q[:, :, :, None, :], k, v

def gqa_qkv(u, qk_norm_q, qk_norm_k, rope):
    B, L = u.shape[:2]
    nq = GQA_Q_HEADS * GQA_HEAD_DIM
    nk = GQA_KV_HEADS * GQA_HEAD_DIM
    q = rms_norm(u[..., :nq].reshape(B, L, GQA_KV_HEADS, GQA_GROUP, GQA_HEAD_DIM), qk_norm_q)
    k = rms_norm(u[..., nq:nq + nk].reshape(B, L, GQA_KV_HEADS, GQA_HEAD_DIM), qk_norm_k)
    v = u[..., nq + nk:].reshape(B, L, GQA_KV_HEADS, GQA_HEAD_DIM)
    if rope is not None:
        q = apply_axial_rope(q, rope)
        k = apply_axial_rope(k, rope)
    return q, k, v

def mlstm_scan(q, k, v, log_i, log_f, state):
    B, L, H, d = q.shape
    nc = L // ML_CHUNK
    f32 = jnp.float32

    def to_chunks(a):
        return jnp.moveaxis(a.reshape((B, nc, ML_CHUNK) + a.shape[2:]), 1, 0)

    xs = (to_chunks(q.astype(f32)), to_chunks(k.astype(f32) * (d ** -0.5)), to_chunks(v.astype(f32)),
          to_chunks(log_i), to_chunks(log_f))
    lower = jnp.tril(jnp.ones((ML_CHUNK, ML_CHUNK), dtype=bool))

    def step(carry, inp):
        C, n, m = carry
        qc, kc, vc, ic, fc = inp
        b = jnp.cumsum(fc, axis=1).transpose(0, 2, 1)
        ih = ic.transpose(0, 2, 1)
        dmat = jnp.where(lower, b[..., :, None] - b[..., None, :] + ih[..., None, :], -jnp.inf)
        inter = b + m[..., None]
        m_t = jnp.maximum(inter, jnp.max(dmat, axis=-1))
        w_intra = jnp.exp(dmat - m_t[..., None])
        w_state = jnp.exp(inter - m_t)
        a = w_intra * jnp.einsum('bthd,bshd->bhts', qc, kc)
        num = (jnp.einsum('bhts,bshd->bthd', a, vc)
               + jnp.einsum('bht,bthk,bhkv->bthv', w_state, qc, C))
        den = jnp.sum(a, axis=-1) + w_state * jnp.einsum('bthk,bhk->bht', qc, n)
        h = num / jnp.maximum(jnp.abs(den), jnp.exp(-m_t)).transpose(0, 2, 1)[..., None]
        b_last = b[..., -1]
        g = b_last[..., None] - b + ih
        m_new = jnp.maximum(b_last + m, jnp.max(g, axis=-1))
        w_s = jnp.exp(g - m_new[..., None])
        w_c = jnp.exp(b_last + m - m_new)
        C = w_c[..., None, None] * C + jnp.einsum('bhs,bshk,bshv->bhkv', w_s, kc, vc)
        n = w_c[..., None] * n + jnp.einsum('bhs,bshk->bhk', w_s, kc)
        return (C, n, m_new), h

    state, hs = lax.scan(step, state, xs)
    return jnp.moveaxis(hs, 0, 1).reshape(B, L, H, d), state

def mlstm_inputs(u, gate_b):
    B, L = u.shape[:2]
    q, k, v, o = [a.reshape(B, L, ML_HEADS, ML_HEAD_DIM) for a in jnp.split(u[..., :4 * ML_WIDTH], 4, axis=-1)]
    gates = u[..., 4 * ML_WIDTH:].astype(jnp.float32).reshape(B, L, 4, ML_HEADS) + gate_b.astype(jnp.float32)
    return (q, k, v, o, gates[:, :, 0], gates[:, :, 1],
            jax.nn.log_sigmoid(gates[:, :, 2]), jax.nn.log_sigmoid(gates[:, :, 3]))

def bidir_mlstm(q, k, v, i_f, i_b, lf_f, lf_b, st_f, st_b):
    h_f, st_f = mlstm_scan(q, k, v, i_f, lf_f, st_f)
    flip = lambda a: jnp.flip(a, axis=1)
    h_b, st_b = mlstm_scan(flip(q), flip(k), flip(v), flip(i_b), flip(lf_b), st_b)
    return h_f + flip(h_b), st_f, st_b

def mlstm_mixer(u_ctx, u_lat, gate_b, norm_g, with_ctx):
    B = u_lat.shape[0]
    f32 = jnp.float32
    zero = (jnp.zeros((B, ML_HEADS, ML_HEAD_DIM, ML_HEAD_DIM), f32),
            jnp.zeros((B, ML_HEADS, ML_HEAD_DIM), f32), jnp.zeros((B, ML_HEADS), f32))
    qc, kc, vc, oc, icf, icb, fcf, fcb = mlstm_inputs(u_ctx, gate_b)
    h_c, st_f, st_b = bidir_mlstm(qc, kc, vc, icf, icb, fcf, fcb, zero, zero)
    ql, kl, vl, ol, ilf, ilb, flf, flb = mlstm_inputs(u_lat, gate_b)
    h_l, _, _ = bidir_mlstm(ql, kl, vl, ilf, ilb, flf, flb, st_f, st_b)

    def out(h, o):
        Bq, L = o.shape[:2]
        y = jax.nn.sigmoid(o.astype(f32)) * rms_norm(h, norm_g)
        return y.reshape(Bq, L, ML_WIDTH).astype(o.dtype)

    return (out(h_c, oc) if with_ctx else None), out(h_l, ol)

def hyena_filters(L, w1, b1, freq, w2, b2, w3):
    f32 = jnp.float32
    t = jnp.arange(L, dtype=f32) / L
    ang = 2.0 * math.pi * t[:, None] * jnp.arange(1, HY_BANDS + 1, dtype=f32)
    z = jnp.concatenate([t[:, None], jnp.sin(ang), jnp.cos(ang)], axis=-1)
    hdn = jnp.sin(freq[0].astype(f32) * (z @ w1.astype(f32) + b1.astype(f32)))
    hdn = jnp.sin(freq[1].astype(f32) * (hdn @ w2.astype(f32) + b2.astype(f32)))
    filt = (hdn @ w3.astype(f32)).reshape(L, HY_ORDER, 2, HY_WIDTH)
    log_target = math.log(HY_DECAY_TARGET)
    alpha = jnp.linspace(-log_target / HY_LONG_PCT, -log_target / HY_SHORT_PCT, HY_WIDTH, dtype=f32)
    filt = filt * jnp.exp(-t[:, None] * alpha)[:, None, None, :]
    return filt * lax.rsqrt(jnp.sum(filt * filt, axis=(0, 2), keepdims=True) + EPS)

def two_sided_fftconv(z, h_fwd, h_bwd):
    L, C = h_fwd.shape
    h_circ = jnp.concatenate([h_fwd, jnp.zeros((1, C), h_fwd.dtype), h_bwd[:0:-1]], axis=0)
    hf = jnp.fft.rfft(h_circ, n=2 * L, axis=0)
    zf = jnp.fft.rfft(z.astype(jnp.float32), n=2 * L, axis=1)
    y = jnp.fft.irfft(zf * hf[None], n=2 * L, axis=1)[:, :L]
    return y.astype(z.dtype)

def short_conv3(u, w):
    up = jnp.pad(u, ((0, 0), (1, 1), (0, 0)))
    return up[:, :-2] * w[0] + up[:, 1:-1] * w[1] + up[:, 2:] * w[2]

def hyena_mixer(u, conv_w, filt, bias):
    u = short_conv3(u, conv_w)
    v, x1, x2 = jnp.split(u, 3, axis=-1)
    z = v
    for order, gate in enumerate((x1, x2)):
        z = gate * (two_sided_fftconv(z, filt[:, order, 0], filt[:, order, 1]) + z * bias[order])
    return z

def merge_branches(ys, gate_logits, w_branch, w_out):
    B, L = gate_logits.shape[:2]
    gl = gate_logits.reshape(B, L, N_BRANCH, -1)
    acc = jax.nn.sigmoid(gl[:, :, 0]) * (ys[0] @ w_branch[0])
    for i in range(1, N_BRANCH):
        acc = acc + jax.nn.sigmoid(gl[:, :, i]) * (ys[i] @ w_branch[i])
    return acc @ w_out

def peer(h, wq, subkeys, u_tab, v_tab):
    T, D = h.shape
    q = (h @ wq).reshape(T, PEER_HEADS, 2, PEER_DK // 2)
    s = jnp.einsum('thcd,hcnd->thcn', q, subkeys, preferred_element_type=jnp.float32)
    sv, si = lax.top_k(s, PEER_TOPK)
    cand = (sv[:, :, 0, :, None] + sv[:, :, 1, None, :]).reshape(T, PEER_HEADS, PEER_TOPK * PEER_TOPK)
    cidx = (si[:, :, 0, :, None] * PEER_NKEYS + si[:, :, 1, None, :]).reshape(T, PEER_HEADS, PEER_TOPK * PEER_TOPK)
    best, pos = lax.top_k(cand, PEER_TOPK)
    idx = jnp.take_along_axis(cidx, pos, axis=-1)
    g = jax.nn.softmax(best, axis=-1)
    nb = T // PEER_BLOCK

    def block(args):
        hb, ib, gb = args
        act = jax.nn.gelu(jnp.einsum('thkd,td->thk', u_tab[ib], hb, preferred_element_type=jnp.float32))
        return jnp.einsum('thk,thkd->td', (gb * act).astype(v_tab.dtype), v_tab[ib])

    out = lax.map(block, (h.reshape(nb, PEER_BLOCK, D),
                          idx.reshape(nb, PEER_BLOCK, PEER_HEADS, PEER_TOPK),
                          g.reshape(nb, PEER_BLOCK, PEER_HEADS, PEER_TOPK)))
    return out.reshape(T, D).astype(h.dtype)

def trunk_layer(xc, xl, mod_c, mod_l, rope_a, rope_b, with_ctx, norm1, norm2, w_in,
                mla_q_norm, mla_kv_norm, mla_w_uq, mla_w_ukv, mla_qk_norm_q, mla_qk_norm_k,
                gqa_qk_norm_q, gqa_qk_norm_k, ml_gate_b, ml_norm,
                hy_conv, hy_w1, hy_b1, hy_freq, hy_w2, hy_b2, hy_w3, hy_bias,
                w_branch, w_out, peer_wq, peer_subkeys, peer_u, peer_v):
    D = xl.shape[-1]
    sh1_c, sc1_c, g1_c, sh2_c, sc2_c, g2_c = jnp.split(mod_c, 6, axis=-1)
    sh1_l, sc1_l, g1_l, sh2_l, sc2_l, g2_l = [a[:, None, :] for a in jnp.split(mod_l, 6, axis=-1)]

    pc = modulate(xc, norm1, sh1_c, sc1_c) @ w_in
    pl = modulate(xl, norm1, sh1_l, sc1_l) @ w_in
    a_c, b_c, m_c, h_c, gate_c = jnp.split(pc, IN_OFFSETS, axis=-1)
    a_l, b_l, m_l, h_l, gate_l = jnp.split(pl, IN_OFFSETS, axis=-1)

    qa_c, ka_c, va_c = mla_qkv(a_c, mla_q_norm, mla_kv_norm, mla_w_uq, mla_w_ukv, mla_qk_norm_q, mla_qk_norm_k, None)
    qa_l, ka_l, va_l = mla_qkv(a_l, mla_q_norm, mla_kv_norm, mla_w_uq, mla_w_ukv, mla_qk_norm_q, mla_qk_norm_k, rope_a)
    ya_l = latent_attention(qa_l, ka_c, va_c, ka_l, va_l, MLA_QK ** -0.5)
    qb_c, kb_c, vb_c = gqa_qkv(b_c, gqa_qk_norm_q, gqa_qk_norm_k, None)
    qb_l, kb_l, vb_l = gqa_qkv(b_l, gqa_qk_norm_q, gqa_qk_norm_k, rope_b)
    yb_l = latent_attention(qb_l, kb_c, vb_c, kb_l, vb_l, GQA_HEAD_DIM ** -0.5)
    yc_c, yc_l = mlstm_mixer(m_c, m_l, ml_gate_b, ml_norm, with_ctx)
    filt_l = hyena_filters(xl.shape[1], hy_w1, hy_b1, hy_freq, hy_w2, hy_b2, hy_w3)
    yd_l = hyena_mixer(h_l, hy_conv, filt_l, hy_bias)

    xl = xl + g1_l * merge_branches([ya_l, yb_l, yc_l, yd_l], gate_l, w_branch, w_out)
    if with_ctx:
        Bc, Lc = xc.shape[:2]
        ya_c = attend(qa_c, ka_c, va_c, MLA_QK ** -0.5).reshape(Bc, Lc, -1)
        yb_c = attend(qb_c, kb_c, vb_c, GQA_HEAD_DIM ** -0.5).reshape(Bc, Lc, -1)
        filt_c = hyena_filters(Lc, hy_w1, hy_b1, hy_freq, hy_w2, hy_b2, hy_w3)
        yd_c = hyena_mixer(h_c, hy_conv, filt_c, hy_bias)
        xc = xc + g1_c * merge_branches([ya_c, yb_c, yc_c, yd_c], gate_c, w_branch, w_out)

    h2l = modulate(xl, norm2, sh2_l, sc2_l)
    if with_ctx:
        h2c = modulate(xc, norm2, sh2_c, sc2_c)
        n_ctx = xc.shape[0] * xc.shape[1]
        f = peer(jnp.concatenate([h2c.reshape(-1, D), h2l.reshape(-1, D)], axis=0), peer_wq, peer_subkeys, peer_u, peer_v)
        xc = xc + g2_c * f[:n_ctx].reshape(xc.shape)
        xl = xl + g2_l * f[n_ctx:].reshape(xl.shape)
    else:
        xl = xl + g2_l * peer(h2l.reshape(-1, D), peer_wq, peer_subkeys, peer_u, peer_v).reshape(xl.shape)
    return xc, xl

def setup_inputs(seed: int = 0) -> dict:
    key = jax.random.key(seed)
    keys = iter(jax.random.split(key, 48))
    f32 = jnp.float32

    def nrm(shape, scale):
        return jax.random.normal(next(keys), shape, f32) * scale

    def gain(shape):
        return 1.0 + nrm(shape, 0.02)

    L, D = DEPTH, D_MODEL
    forget_bias = jnp.linspace(3.0, 6.0, ML_HEADS, dtype=f32)
    return {
        "x": nrm((BATCH, SEQ, D), 1.0),
        "c": nrm((BATCH, D), 1.0),
        "ctx": nrm((BATCH, CTX_LEN, D), 1.0),
        "c_ctx": nrm((D,), 1.0),
        "ada_w": nrm((L, D, 6 * D), 0.5 * D ** -0.5),
        "ada_b": nrm((L, 6 * D), 0.02),
        "norm1": gain((L, D)),
        "norm2": gain((L, D)),
        "w_in": nrm((L, D, D_IN), D ** -0.5),
        "mla_q_norm": gain((L, MLA_Q_LORA)),
        "mla_kv_norm": gain((L, MLA_KV_LORA)),
        "mla_w_uq": nrm((L, MLA_Q_LORA, MLA_HEADS * MLA_QK), MLA_Q_LORA ** -0.5),
        "mla_w_ukv": nrm((L, MLA_KV_LORA, MLA_HEADS * (MLA_NOPE + MLA_V)), MLA_KV_LORA ** -0.5),
        "mla_qk_norm_q": gain((L, MLA_QK)),
        "mla_qk_norm_k": gain((L, MLA_QK)),
        "gqa_qk_norm_q": gain((L, GQA_HEAD_DIM)),
        "gqa_qk_norm_k": gain((L, GQA_HEAD_DIM)),
        "ml_gate_b": jnp.concatenate([nrm((L, 2, ML_HEADS), 0.1), forget_bias + nrm((L, 2, ML_HEADS), 0.1)], axis=1),
        "ml_norm": gain((L, ML_HEADS, ML_HEAD_DIM)),
        "hy_conv": nrm((L, 3, HY_IN), 3 ** -0.5),
        "hy_w1": nrm((L, HY_FEAT, HY_HIDDEN), HY_FEAT ** -0.5),
        "hy_b1": nrm((L, HY_HIDDEN), 0.1),
        "hy_freq": gain((L, 2, HY_HIDDEN)),
        "hy_w2": nrm((L, HY_HIDDEN, HY_HIDDEN), HY_HIDDEN ** -0.5),
        "hy_b2": nrm((L, HY_HIDDEN), 0.1),
        "hy_w3": nrm((L, HY_HIDDEN, HY_ORDER * 2 * HY_WIDTH), HY_HIDDEN ** -0.5),
        "hy_bias": nrm((L, HY_ORDER, HY_WIDTH), 0.5),
        "w_branch": nrm((L, N_BRANCH, BRANCH_W, D), BRANCH_W ** -0.5),
        "w_out": nrm((L, D, D), D ** -0.5),
        "peer_wq": nrm((L, D, PEER_HEADS * PEER_DK), D ** -0.5),
        "peer_subkeys": nrm((L, PEER_HEADS, 2, PEER_NKEYS, PEER_DK // 2), (PEER_DK // 2) ** -0.5),
        "peer_u": nrm((L, PEER_EXPERTS, D), D ** -0.5),
        "peer_v": nrm((L, PEER_EXPERTS, D), PEER_HEADS ** -0.5),
    }

def reference(x, c, ctx, c_ctx, ada_w, ada_b, norm1, norm2, w_in,
              mla_q_norm, mla_kv_norm, mla_w_uq, mla_w_ukv, mla_qk_norm_q, mla_qk_norm_k,
              gqa_qk_norm_q, gqa_qk_norm_k, ml_gate_b, ml_norm,
              hy_conv, hy_w1, hy_b1, hy_freq, hy_w2, hy_b2, hy_w3, hy_bias,
              w_branch, w_out, peer_wq, peer_subkeys, peer_u, peer_v):
    B, S, D = x.shape
    ROWS = S // GRID_W
    rows = jnp.broadcast_to(jnp.arange(ROWS, dtype=jnp.int32)[:, None], (ROWS, GRID_W)).reshape(-1)
    cols = jnp.broadcast_to(jnp.arange(GRID_W, dtype=jnp.int32)[None, :], (ROWS, GRID_W)).reshape(-1)
    rope_a = axial_rope_tables(rows, cols, MLA_ROPE)
    rope_b = axial_rope_tables(rows, cols, GQA_HEAD_DIM)
    s_lat = jax.nn.silu(c)
    s_ctx = jax.nn.silu(c_ctx)
    xc, xl = ctx, x
    for l in range(DEPTH):
        mod_l = s_lat @ ada_w[l] + ada_b[l]
        mod_c = s_ctx @ ada_w[l] + ada_b[l]
        xc, xl = trunk_layer(
            xc, xl, mod_c, mod_l, rope_a, rope_b, l < DEPTH - 1, norm1[l], norm2[l], w_in[l],
            mla_q_norm[l], mla_kv_norm[l], mla_w_uq[l], mla_w_ukv[l], mla_qk_norm_q[l], mla_qk_norm_k[l],
            gqa_qk_norm_q[l], gqa_qk_norm_k[l], ml_gate_b[l], ml_norm[l],
            hy_conv[l], hy_w1[l], hy_b1[l], hy_freq[l], hy_w2[l], hy_b2[l], hy_w3[l], hy_bias[l],
            w_branch[l], w_out[l], peer_wq[l], peer_subkeys[l], peer_u[l], peer_v[l])
    return xl


_drawn_inputs = setup_inputs


def setup_inputs(seed=0):
    import zlib

    import numpy as np

    out = dict(_drawn_inputs(seed))
    spreads = {}
    factors = {'norm1': 2.75,
     'norm2': 14.361,
     'mla_q_norm': 8.0,
     'mla_kv_norm': 8.0,
     'mla_qk_norm_q': 8.0,
     'mla_qk_norm_k': 8.0,
     'gqa_qk_norm_q': 8.0,
     'gqa_qk_norm_k': 8.0,
     'ml_norm': 45.942,
     'hy_freq': 3.362}
    for name, (base, spread) in spreads.items():
        noise = np.random.default_rng([zlib.crc32(name.encode()), seed]).standard_normal(out[name].shape)
        drawn = base * np.exp(spread * noise) if base else spread * noise
        out[name] = __import__('jax').numpy.asarray(drawn.astype(out[name].dtype))
    for name, factor in factors.items():
        out[name] = (out[name] * factor).astype(out[name].dtype)
    return out
```

```python
from contextlib import ExitStack, contextmanager

import concourse.bass as bass
from concourse import mybir

F32 = mybir.dt.float32
U32 = mybir.dt.uint32
ALU = mybir.AluOpType
ACT = mybir.ActivationFunctionType
AX = mybir.AxisListType

P = 128
D = 1024
KD = D // P
CTX = 256
LAT = 256
TOK = CTX + LAT
NB = TOK // P
LAYERS = 2
EPS = 1e-6
BANK = 512
BANKS = 8

MLA_Q, MLA_KV, MLA_PE, MLA_NOPE, MLA_V, MLA_H = 256, 128, 32, 64, 64, 4
MLA_QK = MLA_NOPE + MLA_PE
GQA_Q, GQA_KV, HD = 4, 2, 64
ML_H = 4
ML_W = ML_H * HD
HY_W = 256
O_GQA = MLA_Q + MLA_KV + MLA_PE
O_ML = O_GQA + (GQA_Q + 2 * GQA_KV) * HD
O_HY = O_ML + 4 * ML_W + 4 * ML_H
O_GATE = O_HY + 3 * HY_W
N_BRANCH = 4

PH, NK, TOPK = 8, 128, 16
HC = 2 * PH

V_ADAB, V_N1, V_N2, V_CONV, V_HYB = 0, 48, 56, 64, 82
V_MQ, V_MKV, V_MLN, V_QKQ, V_QKK, V_GQ, V_GK = 86, 88, 89, 91, 92, 93, 94
V_B1, V_B2, V_FREQ, V_ROWS = 95, 96, 97, 99

(C_ID, C_ONES, C_BONES, C_TRI_F, C_TRI_B, C_STR_F, C_STR_B, C_NEG_F, C_NEG_B, C_ROT_M, C_ROT_G, C_IOTA,
 C_N) = range(13)


NUMBER = [0, 0]


@contextmanager
def stage(nc, *names):
    NUMBER[0] += 1
    sems = [nc.alloc_semaphore(f"{n}_{NUMBER[0]}") for n in names]
    with nc.Block() as block:
        yield (block, *sems)
    nc.clear_and_free_semaphores(sems)
    nc.all_engine_barrier()


def sbuf(nc, name, shape, dtype):
    NUMBER[1] += 1
    return nc.sbuf_tensor(f"{name}_{NUMBER[1]}", shape, dtype)


class Chain:

    def __init__(self, eng, sem):
        self.eng, self.sem, self.n = eng, sem, 0

    def step(self, ins):
        self.n += 1
        ins.then_inc(self.sem, 1)

    def meet(self):
        self.eng.wait_ge(self.sem, self.n)

    def link(self, ins):
        self.step(ins)
        self.meet()


class Mem:
    pass




def setup(nc, m, d):
    with ExitStack() as ctx:
        tok = ctx.enter_context(sbuf(nc, "tok", [P, NB, D], F32))
        crow = ctx.enter_context(sbuf(nc, "crow", [2 * KD, P], F32))
        craw = ctx.enter_context(sbuf(nc, "craw", [P, 2 * KD], F32))
        cexp = ctx.enter_context(sbuf(nc, "cexp", [P, 2 * KD], F32))
        (block, consts_in, tok_in, c_in, tok_turned, c_turned, resid_by_act, c_exp, c_copied, dve_own, act_own) = (
            ctx.enter_context(stage(nc, "consts_in", "tok_in", "c_in", "tok_turned", "c_turned", "resid_by_act",
                                    "c_exp", "c_copied", "dve_own", "act_own")))

        @block.sync
        def _(sp):
            sp.dma_start(m.sq[:, :, :], d["k_square"].rearrange("(c p) n -> p c n", p=P)).then_inc(consts_in, 16)
            sp.dma_start(tok[:, 0:2, :], d["ctx"][0].rearrange("(b p) n -> p b n", p=P)).then_inc(tok_in, 16)
            sp.dma_start(tok[:, 2:4, :], d["x"][0].rearrange("(b p) n -> p b n", p=P)).then_inc(tok_in, 16)
            sp.dma_start(crow[0:KD, :], d["c"].rearrange("o (k p) -> (o k) p", p=P)).then_inc(c_in, 16)
            sp.dma_start(crow[KD:, :], d["c_ctx"].rearrange("(k p) -> k p", p=P)).then_inc(c_in, 16)

        @block.tensor
        def _(pe):
            pe.wait_ge(consts_in, 16)
            pe.wait_ge(c_in, 32)
            nc.tensor.transpose(m.ps[:, 7, 0:2 * KD], crow[:, :], m.sq[0:2 * KD, C_ID, 0:2 * KD]).then_inc(c_turned, 1)
            pe.wait_ge(tok_in, 32)
            for k in range(KD):
                if k >= 4:
                    pe.wait_ge(resid_by_act, k - 3)
                for b in range(NB):
                    ins = nc.tensor.transpose(m.ps[:, k % 4, b * P:(b + 1) * P], tok[:, b, k * P:(k + 1) * P],
                                              m.sq[:, C_ID, :])
                ins.then_inc(tok_turned, 1)

        @block.scalar
        def _(act):
            act.wait_ge(c_turned, 1)
            act.wait_ge(c_copied, 1)
            nc.scalar.activation(cexp[:, :], craw[:, :], ACT.Exp, scale=-1.0).then_inc(c_exp, 1)
            for k in range(KD):
                act.wait_ge(tok_turned, k + 1)
                nc.scalar.copy(m.resid[:, k, :], m.ps[:, k % 4, :]).then_inc(resid_by_act, 1)

        @block.vector
        def _(dve):
            own = Chain(dve, dve_own)
            dve.wait_ge(c_turned, 1)
            nc.vector.tensor_copy(craw[:, :], m.ps[:, 7, 0:2 * KD]).then_inc(c_copied, 1)
            dve.wait_ge(c_copied, 1)
            dve.wait_ge(c_exp, 1)
            own.link(nc.vector.tensor_scalar(cexp[:, :], cexp[:, :], 1.0, None, ALU.add))
            own.link(nc.vector.reciprocal(cexp[:, :], cexp[:, :]))
            own.link(nc.vector.tensor_tensor(m.cond[:, :, :].rearrange("p k r -> p r k"),
                                             craw[:, :].rearrange("p (r k) -> p r k", r=2),
                                             cexp[:, :].rearrange("p (r k) -> p r k", r=2), ALU.mult))




def modulation(nc, m, d, l):
    CH = 512
    NCH = 6 * D // CH
    RING = 3
    with ExitStack() as ctx:
        vrow = ctx.enter_context(sbuf(nc, "vrow", [P, P], F32))
        wada = ctx.enter_context(sbuf(nc, "wada", [P, RING, KD, CH], F32))
        mrow = ctx.enter_context(sbuf(nc, "mrow", [2, 6 * D], F32))
        (block, zeroed, vecs_in, chunk_mult, row_out, vecs_turned, mods_turned, dve_own, *w_ins) = (
            ctx.enter_context(stage(nc, "zeroed", "vecs_in", "chunk_mult", "row_out", "vecs_turned",
                                    "mods_turned", "dve_own", *[f"w_in{r}" for r in range(RING)])))

        vecs = [
            (V_ADAB, 48, P, d["ada_b"][l].rearrange("(k p) -> k p", p=P), 0),
            (V_N1, 8, P, d["norm1"][l].rearrange("(k p) -> k p", p=P), 0),
            (V_N2, 8, P, d["norm2"][l].rearrange("(k p) -> k p", p=P), 0),
            (V_CONV, 18, P, d["hy_conv"][l].rearrange("j (k p) -> (j k) p", p=P), 0),
            (V_HYB, 4, P, d["hy_bias"][l].rearrange("j (k p) -> (j k) p", p=P), 0),
            (V_MQ, 2, P, d["mla_q_norm"][l].rearrange("(k p) -> k p", p=P), 0),
            (V_MKV, 1, P, d["mla_kv_norm"][l].rearrange("(k p) -> k p", p=P), 0),
            (V_MLN, 2, P, d["ml_norm"][l].rearrange("(a b) e -> a (b e)", b=2), 0),
            (V_QKQ, 1, MLA_QK, d["mla_qk_norm_q"][l:l + 1, :], 0),
            (V_QKK, 1, MLA_QK, d["mla_qk_norm_k"][l:l + 1, :], 0),
            (V_GQ, 1, HD, d["gqa_qk_norm_q"][l:l + 1, :], 0),
            (V_GQ, 1, HD, d["gqa_qk_norm_q"][l:l + 1, :], HD),
            (V_GK, 1, HD, d["gqa_qk_norm_k"][l:l + 1, :], 0),
            (V_GK, 1, HD, d["gqa_qk_norm_k"][l:l + 1, :], HD),
            (V_B1, 1, HD, d["hy_b1"][l:l + 1, :], 0),
            (V_B2, 1, HD, d["hy_b2"][l:l + 1, :], 0),
            (V_FREQ, 2, HD, d["hy_freq"][l], 0),
        ]

        @block.sync
        def _(sp):
            for c in range(NCH):
                if c >= RING:
                    sp.wait_ge(chunk_mult, c - RING + 1)
                sp.dma_start(wada[:, c % RING, :, :],
                             d["ada_w"][l].rearrange("(k p) n -> p k n", p=P)[:, :, c * CH:(c + 1) * CH]
                             ).then_inc(w_ins[c % RING], 16)

        @block.scalar
        def _(act):
            act.wait_ge(zeroed, 1)
            for at, n, w, src, c0 in vecs:
                act.dma_start(vrow[at:at + n, c0:c0 + w], src).then_inc(vecs_in, 16)
            for c in range(NCH):
                act.wait_ge(chunk_mult, c + 1)
                nc.scalar.copy(mrow[:, c * CH:(c + 1) * CH], m.ps[0:2, c % 2, :]).then_inc(row_out, 1)

        @block.tensor
        def _(pe):
            pe.wait_ge(vecs_in, 16 * len(vecs))
            nc.tensor.transpose(m.ps[:, 6, 0:P], vrow[:, :], m.sq[:, C_ID, :]).then_inc(vecs_turned, 1)

            def turn(c):
                pe.wait_ge(row_out, c + 1)
                for q in range(CH // P):
                    j = c * (CH // P) + q
                    ins = nc.tensor.transpose(m.ps[:, 7, 2 * j:2 * j + 2], mrow[:, j * P:(j + 1) * P],
                                              m.sq[0:2, C_ID, 0:2])
                ins.then_inc(mods_turned, 1)

            for c in range(NCH):
                pe.wait_ge(w_ins[c % RING], 16 * (c // RING + 1))
                if c >= 2:
                    pe.wait_ge(row_out, c - 1)
                for k in range(KD):
                    ins = nc.tensor.matmul(m.ps[0:2, c % 2, :], m.cond[:, k, :], wada[:, c % RING, k, :],
                                           start=(k == 0), stop=(k == KD - 1))
                ins.then_inc(chunk_mult, 1)
                if c >= 1:
                    turn(c - 1)
            turn(NCH - 1)

        @block.vector
        def _(dve):
            own = Chain(dve, dve_own)
            nc.vector.memset(vrow[:, :], 0.0).then_inc(zeroed, 1)
            dve.wait_ge(vecs_turned, 1)
            own.link(nc.vector.tensor_copy(m.vec[:, :], m.ps[:, 6, 0:V_ROWS]))
            dve.wait_ge(mods_turned, NCH)
            own.link(nc.vector.tensor_tensor(
                m.mod[:, :, :], m.ps[:, 7, 0:12 * KD].rearrange("p (j r) -> p j r", r=2),
                m.vec[:, V_ADAB:V_ADAB + 6 * KD].unsqueeze(2).to_broadcast([P, 6 * KD, 2]), ALU.add))
            for v, at in ((V_N1, KD), (V_N2, 4 * KD)):
                own.link(nc.vector.tensor_scalar(m.mod[:, at:at + KD, :], m.mod[:, at:at + KD, :], 1.0, None, ALU.add))
                own.link(nc.vector.tensor_tensor(m.mod[:, at:at + KD, :], m.mod[:, at:at + KD, :],
                                                 m.vec[:, v:v + KD].unsqueeze(2).to_broadcast([P, KD, 2]), ALU.mult))


def mod_norm(nc, m, hT, at, t0):
    T = TOK - t0
    halves = [(kind, lo, hi) for kind, lo, hi in ((1, 0, CTX), (0, CTX, TOK)) if lo >= t0]
    with ExitStack() as ctx:
        sq = ctx.enter_context(sbuf(nc, "sq", [P, 3, TOK], F32))
        rs = ctx.enter_context(sbuf(nc, "rs", [P, TOK], F32))
        (block, squared, summed, scaled, rooted, normed, dve_own) = ctx.enter_context(
            stage(nc, "squared", "summed", "scaled", "rooted", "normed", "dve_own"))

        @block.scalar
        def _(act):
            for k in range(KD):
                if k >= 3:
                    act.wait_ge(summed, k - 2)
                nc.scalar.activation(sq[:, k % 3, t0:], m.resid[:, k, t0:], ACT.Square).then_inc(squared, 1)
            act.wait_ge(scaled, 1)
            nc.scalar.activation(rs[:, t0:], rs[:, t0:], ACT.Sqrt).then_inc(rooted, 1)
            for k in range(KD):
                act.wait_ge(normed, k + 1)
                for kind, lo, hi in halves:
                    nc.scalar.activation(hT[:, k, lo:hi], hT[:, k, lo:hi], ACT.Identity,
                                         scale=m.mod[:, at + KD + k, kind:kind + 1],
                                         bias=m.mod[:, at + k, kind:kind + 1])

        @block.tensor
        def _(pe):
            for k in range(KD):
                pe.wait_ge(squared, k + 1)
                nc.tensor.matmul(m.ps[:, 0, 0:T], m.sq[:, C_ONES, :], sq[:, k % 3, t0:], start=(k == 0),
                                 stop=(k == KD - 1)).then_inc(summed, 1)

        @block.vector
        def _(dve):
            own = Chain(dve, dve_own)
            dve.wait_ge(summed, KD)
            nc.vector.tensor_scalar(rs[:, t0:], m.ps[:, 0, 0:T], 1.0 / D, EPS, ALU.mult, ALU.add).then_inc(scaled, 1)
            dve.wait_ge(rooted, 1)
            own.link(nc.vector.reciprocal(rs[:, t0:], rs[:, t0:]))
            for k in range(KD):
                nc.vector.tensor_tensor(hT[:, k, t0:], m.resid[:, k, t0:], rs[:, t0:], ALU.mult).then_inc(normed, 1)




def input_projection(nc, m, d, hT, t, l, q0):
    CH = 456
    NCH = O_GATE // CH
    assert NCH * CH == O_GATE
    fm = [
        (128, lambda w: w[:, 0:128], 128, 0, t.cq[:, 0, :], q0),
        (256, lambda w: w[:, 128:256], 128, 0, t.cq[:, 1, :], q0),
        (384, lambda w: w[:, 256:384], 128, 0, t.ckv[:, :], 0),
        (416, lambda w: w[:, 384:416], 32, 64, t.kpe[64:96, :], 0),
        (544, lambda w: w[:, O_GQA:O_GQA + 128], 128, 0, [t.gq[0:64, 0, :], t.gq[0:64, 1, :]], q0),
        (672, lambda w: w[:, O_GQA + 128:O_GQA + 256], 128, 0, [t.gq[64:128, 0, :], t.gq[64:128, 1, :]], q0),
        (800, lambda w: w[:, O_GQA + 256:O_GQA + 384], 128, 0, t.gk[:, :], 0),
        (O_ML + 128, lambda w: w[:, O_ML:O_ML + 128], 128, 0, t.mq[:, 0, :], q0),
        (O_ML + 256, lambda w: w[:, O_ML + 128:O_ML + 256], 128, 0, t.mq[:, 1, :], q0),
        (O_ML + 384, lambda w: w[:, O_ML + 256:O_ML + 384], 128, 0, t.mk[:, 0, :], 0),
        (O_ML + 512, lambda w: w[:, O_ML + 384:O_ML + 512], 128, 0, t.mk[:, 1, :], 0),
    ]
    hy = [(O_HY + 128 * (g + 1), (lambda g: lambda w: w[:, O_HY + 128 * g:O_HY + 128 * g + 128])(g), 128, 0,
           t.hy[:, g, :], q0) for g in range(6)]
    tm = []
    for b in range(NB):
        tm.append((O_ML + 1024, O_ML + 512, 512, t.mvo[:, b, :], b, False))
        tm.append((O_HY, O_HY - 16, 16, t.mg[:, b, :], b, True))
        tm.append((O_ML, O_ML - 128, 128, t.gv[:, b, :], b, False))
    groups = [("fm", *g) for g in fm] + [("tm", *g) for g in tm] + [("fm", *g) for g in hy]
    with ExitStack() as ctx:
        w = ctx.enter_context(sbuf(nc, "w_nongate", [P, KD, O_GATE], F32))
        gbias = ctx.enter_context(sbuf(nc, "gbias", [1, 16], F32))
        (block, bias_in, group_mult, act_out, dve_out, *w_ins) = ctx.enter_context(
            stage(nc, "bias_in", "group_mult", "act_out", "dve_out", *[f"w_in{c}" for c in range(NCH)]))

        @block.sync
        def _(sp):
            sp.dma_start(gbias[:, :], d["ml_gate_b"][l:l + 1].rearrange("o a h -> o (a h)")).then_inc(bias_in, 16)
            for c in range(NCH):
                sp.dma_start(w[:, :, c * CH:(c + 1) * CH],
                             d["w_in"][l].rearrange("(k p) n -> p k n", p=P)[:, :, c * CH:(c + 1) * CH]
                             ).then_inc(w_ins[c], 16)

        @block.tensor
        def _(pe):
            pe.wait_ge(bias_in, 16)
            seen = 0
            for g, grp in enumerate(groups):
                while seen < NCH and seen * CH < grp[1]:
                    pe.wait_ge(w_ins[seen], 16)
                    seen += 1
                if g >= BANKS:
                    pe.wait_ge(dve_out if g % 2 else act_out, (g - BANKS) // 2 + 1)
                if grp[0] == "fm":
                    _, _, cols, M, p0, dst, t0 = grp
                    out = m.ps[p0:p0 + M, g % BANKS, 0:TOK - t0]
                    for k in range(KD):
                        ins = nc.tensor.matmul(out, cols(w[:, k, :]), hT[:, k, t0:], start=(k == 0),
                                               stop=(k == KD - 1))
                else:
                    _, _, c0, M, dst, b, biased = grp
                    out = m.ps[:, g % BANKS, 0:M]
                    for k in range(KD):
                        ins = nc.tensor.matmul(out, hT[:, k, b * P:(b + 1) * P], w[:, k, c0:c0 + M],
                                               start=(k == 0), stop=(k == KD - 1) and not biased)
                    if biased:
                        ins = nc.tensor.matmul(out, m.sq[0:1, C_ONES, :], gbias[:, :], start=False, stop=True)
                ins.then_inc(group_mult, 1)

        def out_of(g):
            grp = groups[g]
            if grp[0] == "tm":
                return [(grp[4], m.ps[:, g % BANKS, 0:grp[3]])]
            _, _, _, M, p0, dst, t0 = grp
            if isinstance(dst, list):
                return [(x[:, t0:], m.ps[64 * i:64 * i + 64, g % BANKS, 0:TOK - t0]) for i, x in enumerate(dst)]
            return [(dst[:, t0:], m.ps[p0:p0 + M, g % BANKS, 0:TOK - t0])]

        @block.scalar
        def _(act):
            for g in range(0, len(groups), 2):
                act.wait_ge(group_mult, g + 1)
                for dst, src in out_of(g):
                    ins = nc.scalar.copy(dst, src)
                ins.then_inc(act_out, 1)

        @block.vector
        def _(dve):
            for g in range(1, len(groups), 2):
                dve.wait_ge(group_mult, g + 1)
                for dst, src in out_of(g):
                    ins = nc.vector.tensor_copy(dst, src)
                ins.then_inc(dve_out, 1)




def attention_heads(nc, m, d, t, l, q0):
    with ExitStack() as ctx:
        wuq = ctx.enter_context(sbuf(nc, "wuq", [P, 2, MLA_H * MLA_QK], F32))
        wukv = ctx.enter_context(sbuf(nc, "wukv", [P, MLA_H * (MLA_NOPE + MLA_V)], F32))
        rope = ctx.enter_context(sbuf(nc, "rope", [P, 4, TOK], F32))
        lat = ctx.enter_context(sbuf(nc, "lat", [P, 3, TOK], F32))
        sq = ctx.enter_context(sbuf(nc, "sq", [P, 3, TOK], F32))
        rs = ctx.enter_context(sbuf(nc, "rs", [P, 3, TOK], F32))
        xn = ctx.enter_context(sbuf(nc, "xn", [P, 2, TOK], F32))
        xc = ctx.enter_context(sbuf(nc, "xc", [P, TOK], F32))
        (block, w_in, lat_sq, lat_sum, lat_scaled, lat_root, lat_done, up_mult, up_out, v_out, x_sq, x_sum,
         x_scaled, x_root, x_normed, x_rot, x_done, dve_own) = ctx.enter_context(stage(
            nc, "w_in", "lat_sq", "lat_sum", "lat_scaled", "lat_root", "lat_done", "up_mult", "up_out", "v_out",
            "x_sq", "x_sum", "x_scaled", "x_root", "x_normed", "x_rot", "x_done", "dve_own"))
        lats = [(t.cq[:, 0, :], V_MQ, q0), (t.cq[:, 1, :], V_MQ + 1, q0), (t.ckv[:, :], V_MKV, 0)]
        tiles = ([(t.qm[0:MLA_QK, h, :], MLA_QK, V_QKQ, q0, 0, C_ROT_M) for h in range(MLA_H)]
                 + [(t.km[0:MLA_QK, h, :], MLA_QK, V_QKK, 0, 0, C_ROT_M) for h in range(MLA_H)]
                 + [(t.gq[:, a, :], P, V_GQ, q0, 2, C_ROT_G) for a in range(2)]
                 + [(t.gk[:, :], P, V_GK, 0, 2, C_ROT_G)])

        @block.sync
        def _(sp):
            sp.dma_start(wuq[:, :, :], d["mla_w_uq"][l].rearrange("(k p) n -> p k n", p=P)).then_inc(w_in, 16)
            sp.dma_start(wukv[:, :], d["mla_w_ukv"][l]).then_inc(w_in, 16)
            sp.dma_start(rope[:, :, :], d["k_rope"].rearrange("(c p) n -> p c n", p=P)).then_inc(w_in, 16)

        @block.scalar
        def _(act):
            for i, (x, _, t0) in enumerate(lats):
                nc.scalar.activation(sq[:, i, t0:], x[:, t0:], ACT.Square).then_inc(lat_sq, 1)
            for i, t0 in ((0, q0), (1, 0)):
                act.wait_ge(lat_scaled, i + 1)
                nc.scalar.activation(rs[:, i, t0:], rs[:, i, t0:], ACT.Sqrt).then_inc(lat_root, 1)
            for h in range(MLA_H):
                nc.scalar.copy(t.km[64:96, h, :], t.kpe[64:96, :])
            for h in range(MLA_H):
                act.wait_ge(up_mult, 2 * h + 1)
                nc.scalar.copy(t.qm[0:MLA_QK, h, q0:], m.ps[0:MLA_QK, 2 + 2 * (h % 2), q0 - q0:TOK - q0])
                act.wait_ge(up_mult, 2 * h + 2)
                nc.scalar.copy(t.km[0:MLA_NOPE, h, :], m.ps[0:MLA_NOPE, 3 + 2 * (h % 2), :]).then_inc(up_out, 1)
            act.wait_ge(up_out, MLA_H)
            act.wait_ge(lat_sum, 3)
            for i, (x, rows, _, t0, _, _) in enumerate(tiles):
                if i >= 3:
                    act.wait_ge(x_sum, i - 2)
                nc.scalar.activation(sq[0:rows, i % 3, t0:], x[:, t0:], ACT.Square).then_inc(x_sq, 1)
                act.wait_ge(x_scaled, i + 1)
                nc.scalar.activation(rs[0:rows, i % 3, t0:], rs[0:rows, i % 3, t0:], ACT.Sqrt).then_inc(x_root, 1)

        @block.tensor
        def _(pe):
            pe.wait_ge(w_in, 48)
            pe.wait_ge(lat_sq, 2)
            for i in range(2):
                nc.tensor.matmul(m.ps[:, 0, 0:TOK - q0], m.sq[:, C_ONES, :], sq[:, i, q0:], start=(i == 0),
                                 stop=(i == 1)).then_inc(lat_sum, 1)
            pe.wait_ge(lat_sq, 3)
            nc.tensor.matmul(m.ps[:, 1, :], m.sq[:, C_ONES, :], sq[:, 2, :], start=True, stop=True).then_inc(lat_sum, 1)
            pe.wait_ge(lat_done, 3)
            W = MLA_NOPE + MLA_V
            for h in range(MLA_H):
                if h >= 2:
                    pe.wait_ge(up_out, h - 1)
                for k in range(2):
                    ins = nc.tensor.matmul(m.ps[0:MLA_QK, 2 + 2 * (h % 2), 0:TOK - q0],
                                           wuq[:, k, h * MLA_QK:(h + 1) * MLA_QK], lat[:, k, q0:], start=(k == 0),
                                           stop=(k == 1))
                ins.then_inc(up_mult, 1)
                nc.tensor.matmul(m.ps[0:MLA_NOPE, 3 + 2 * (h % 2), :], wukv[:, h * W:h * W + MLA_NOPE],
                                 lat[:, 2, :], start=True, stop=True).then_inc(up_mult, 1)
            vcols = wukv[:, :].rearrange("p (h c) -> p h c", h=MLA_H)[:, :, MLA_NOPE:]
            for b in range(NB):
                if b >= 2:
                    pe.wait_ge(v_out, b - 1)
                nc.tensor.matmul(m.ps[:, 6 + b % 2, 0:MLA_H * MLA_V], lat[:, 2, b * P:(b + 1) * P], vcols,
                                 start=True, stop=True).then_inc(up_mult, 1)

            def rotate(i):
                x, rows, _, t0, _, rot = tiles[i]
                pe.wait_ge(x_normed, i + 1)
                nc.tensor.matmul(m.ps[0:rows, 2 + i % 2, 0:TOK - t0], m.sq[0:rows, rot, 0:rows], xn[0:rows, i % 2, t0:],
                                 start=True, stop=True).then_inc(x_rot, 1)

            for i, (x, rows, _, t0, _, rot) in enumerate(tiles):
                pe.wait_ge(x_sq, i + 1)
                if i >= 2:
                    pe.wait_ge(x_scaled, i - 1)
                ones = m.sq[0:rows, C_BONES if rows == P else C_ONES, 0:rows]
                nc.tensor.matmul(m.ps[0:rows, i % 2, 0:TOK - t0], ones, sq[0:rows, i % 3, t0:], start=True,
                                 stop=True).then_inc(x_sum, 1)
                if i >= 1:
                    rotate(i - 1)
            rotate(len(tiles) - 1)

        @block.vector
        def _(dve):
            own = Chain(dve, dve_own)
            for i, (n, t0, width) in enumerate(((2, q0, MLA_Q), (3, 0, MLA_KV))):
                dve.wait_ge(lat_sum, n)
                nc.vector.tensor_scalar(rs[:, i, t0:], m.ps[:, i, 0:TOK - t0], 1.0 / width, EPS, ALU.mult,
                                        ALU.add).then_inc(lat_scaled, 1)
            for i, t0 in ((0, q0), (1, 0)):
                dve.wait_ge(lat_root, i + 1)
                own.link(nc.vector.reciprocal(rs[:, i, t0:], rs[:, i, t0:]))
            for i, (x, v, t0) in enumerate(lats):
                nc.vector.scalar_tensor_tensor(out=lat[:, i, t0:], in0=x[:, t0:], scalar=m.vec[:, v:v + 1],
                                               in1=rs[:, i // 2, t0:], op0=ALU.mult, op1=ALU.mult
                                               ).then_inc(lat_done, 1)
            for b in range(NB):
                dve.wait_ge(up_mult, 2 * MLA_H + b + 1)
                nc.vector.tensor_copy(t.vm[:, b, :], m.ps[:, 6 + b % 2, 0:MLA_H * MLA_V]).then_inc(v_out, 1)
            dve.wait_ge(lat_done, 3)

            def turn(i):
                x, rows, _, t0, table, _ = tiles[i]
                dve.wait_ge(x_rot, i + 1)
                own.link(nc.vector.tensor_tensor(xc[0:rows, t0:], m.ps[0:rows, 2 + i % 2, 0:TOK - t0],
                                                 rope[0:rows, table + 1, t0:], ALU.mult))
                own.link(nc.vector.tensor_tensor(x[:, t0:], xn[0:rows, i % 2, t0:], rope[0:rows, table, t0:], ALU.mult))
                own.link(nc.vector.tensor_tensor(x[:, t0:], x[:, t0:], xc[0:rows, t0:], ALU.add))

            for i, (x, rows, v, t0, table, _) in enumerate(tiles):
                n = MLA_QK if rows == MLA_QK else HD
                dve.wait_ge(x_sum, i + 1)
                nc.vector.tensor_scalar(rs[0:rows, i % 3, t0:], m.ps[0:rows, i % 2, 0:TOK - t0], 1.0 / n, EPS,
                                        ALU.mult, ALU.add).then_inc(x_scaled, 1)
                if i >= 1:
                    turn(i - 1)
                dve.wait_ge(x_root, i + 1)
                own.link(nc.vector.reciprocal(rs[0:rows, i % 3, t0:], rs[0:rows, i % 3, t0:]))
                nc.vector.scalar_tensor_tensor(out=xn[0:rows, i % 2, t0:], in0=x[:, t0:], scalar=m.vec[0:rows, v:v + 1],
                                               in1=rs[0:rows, i % 3, t0:], op0=ALU.mult, op1=ALU.mult
                                               ).then_inc(x_normed, 1)
            turn(len(tiles) - 1)




def attention(nc, m, t, blocks):
    SC = {0: MLA_QK ** -0.5, 1: HD ** -0.5}
    units = []
    for h in range(4):
        half = 64 * (h % 2)
        for b in blocks:
            qs = slice(b * P, (b + 1) * P)
            units.append((0, t.qm[0:MLA_QK, h, qs], lambda n, h=h: t.km[0:MLA_QK, h, 0:n],
                          lambda kb, h=h: t.vm[:, kb, h * HD:(h + 1) * HD], t.yT[half:half + 64, 0, h // 2, qs], b, half))
    for h in range(4):
        half, kv = 64 * (h % 2), h // 2
        for b in blocks:
            qs = slice(b * P, (b + 1) * P)
            units.append((1, t.gq[64 * kv:64 * kv + 64, h % 2, qs],
                          lambda n, kv=kv: t.gk[64 * kv:64 * kv + 64, 0:n],
                          lambda kb, kv=kv: t.gv[:, kb, kv * HD:(kv + 1) * HD],
                          t.yT[half:half + 64, 1, h // 2, qs], b, half))
    N = len(units)
    nkeys = lambda b: CTX if b < CTX // P else TOK
    with ExitStack() as ctx:
        pr = ctx.enter_context(sbuf(nc, "probs", [P, 2, TOK], F32))
        pt = ctx.enter_context(sbuf(nc, "probsT", [P, 2, TOK], F32))
        st = ctx.enter_context(sbuf(nc, "stat", [P, 3, N], F32))
        (block, scored, maxed, exped, normed, turned, turn_out, summed, y_out, dve_own) = ctx.enter_context(stage(
            nc, "scored", "maxed", "exped", "normed", "turned", "turn_out", "summed", "y_out", "dve_own"))

        @block.tensor
        def _(pe):
            def score(u):
                _, q, k, _, _, b, _ = units[u]
                if u >= 2:
                    pe.wait_ge(exped, u - 1)
                nc.tensor.matmul(m.ps[:, u % 2, 0:nkeys(b)], q, k(nkeys(b)), start=True, stop=True).then_inc(scored, 1)

            def turn(u):
                b = units[u][5]
                pe.wait_ge(normed, u + 1)
                if u >= 2:
                    pe.wait_ge(turn_out, u - 1)
                for kb in range(nkeys(b) // P):
                    ins = nc.tensor.transpose(m.ps[:, 2 + u % 2, kb * P:(kb + 1) * P], pr[:, u % 2, kb * P:(kb + 1) * P],
                                              m.sq[:, C_ID, :])
                ins.then_inc(turned, 1)

            def values(u):
                _, _, _, v, _, b, half = units[u]
                pe.wait_ge(turn_out, u + 1)
                if u >= 2:
                    pe.wait_ge(y_out, u - 1)
                n = nkeys(b) // P
                for kb in range(n):
                    ins = nc.tensor.matmul(m.ps[half:half + 64, 4 + u % 2, 0:P], v(kb), pt[:, u % 2, kb * P:(kb + 1) * P],
                                           start=(kb == 0), stop=(kb == n - 1))
                ins.then_inc(summed, 1)

            score(0)
            for u in range(N):
                if u + 1 < N:
                    score(u + 1)
                turn(u)
                if u >= 1:
                    values(u - 1)
            values(N - 1)

        @block.scalar
        def _(act):
            def y_copy(u):
                act.wait_ge(summed, u + 1)
                nc.scalar.copy(units[u][4], m.ps[units[u][6]:units[u][6] + 64, 4 + u % 2, 0:P]).then_inc(y_out, 1)

            def t_copy(u):
                n = nkeys(units[u][5])
                act.wait_ge(turned, u + 1)
                if u >= 2:
                    act.wait_ge(summed, u - 1)
                nc.scalar.copy(pt[:, u % 2, 0:n], m.ps[:, 2 + u % 2, 0:n]).then_inc(turn_out, 1)

            for u, (br, _, _, _, _, b, _) in enumerate(units):
                n = nkeys(b)
                act.wait_ge(maxed, u + 1)
                if u >= 2:
                    act.wait_ge(turned, u - 1)
                nc.scalar.activation(pr[:, u % 2, 0:n], m.ps[:, u % 2, 0:n], ACT.Exp, bias=st[:, 0, u:u + 1],
                                     scale=SC[br], accum_out=st[:, 1, u:u + 1]).then_inc(exped, 1)
                if u >= 1:
                    t_copy(u - 1)
                if u >= 2:
                    y_copy(u - 2)
            t_copy(N - 1)
            y_copy(N - 2)
            y_copy(N - 1)

        @block.vector
        def _(dve):
            own = Chain(dve, dve_own)

            def top(u):
                br, b = units[u][0], units[u][5]
                dve.wait_ge(scored, u + 1)
                own.link(nc.vector.reduce_max(st[:, 2, u:u + 1], m.ps[:, u % 2, 0:nkeys(b)], axis=AX.X))
                nc.vector.tensor_scalar(st[:, 0, u:u + 1], st[:, 2, u:u + 1], -SC[br], None, ALU.mult).then_inc(maxed, 1)

            top(0)
            for u, unit in enumerate(units):
                if u + 1 < N:
                    top(u + 1)
                n = nkeys(unit[5])
                dve.wait_ge(exped, u + 1)
                own.link(nc.vector.reciprocal(st[:, 1, u:u + 1], st[:, 1, u:u + 1]))
                nc.vector.tensor_scalar(pr[:, u % 2, 0:n], pr[:, u % 2, 0:n], st[:, 1, u:u + 1], None,
                                        ALU.mult).then_inc(normed, 1)



ORDER = {0: (0, 1, 2, 3), 1: (1, 0, 3, 2)}


def mlstm(nc, m, t, q_at):
    units = [(dr, h, p) for dr in range(2) for h in range(ML_H) for p in q_at]
    N = len(units)
    SCALE = HD ** -0.5
    with ExitStack() as ctx:
        lf = ctx.enter_context(sbuf(nc, "logf", [P, NB, 2 * ML_H], F32))
        af = ctx.enter_context(sbuf(nc, "absf", [P, NB, 2 * ML_H], F32))
        ft = ctx.enter_context(sbuf(nc, "ftot", [P, 2, NB, ML_H], F32))
        same = ctx.enter_context(sbuf(nc, "same", [P, 2, NB, P], F32))
        fb = ctx.enter_context(sbuf(nc, "fbcast", [P, 2, NB, P], F32))
        w = ctx.enter_context(sbuf(nc, "w", [P, 2, TOK], F32))
        a = ctx.enter_context(sbuf(nc, "a", [P, 2, TOK], F32))
        at = ctx.enter_context(sbuf(nc, "aT", [P, 2, TOK], F32))
        st = ctx.enter_context(sbuf(nc, "stat", [P, 6, N], F32))
        hh = ctx.enter_context(sbuf(nc, "h", [P, NB, ML_W], F32))
        h2 = ctx.enter_context(sbuf(nc, "h2", [P, NB, ML_W], F32))
        og = ctx.enter_context(sbuf(nc, "og", [P, NB, ML_W], F32))
        nr = ctx.enter_context(sbuf(nc, "nr", [P, NB, ML_H], F32))
        (block, f_abs, f_exp, f_exp1, f_ln, f_done, f_tot, tot_out, built, decayed, scored, maxed, exped, den_exp,
         weighed, turned, turn_out, summed, h_done, o_exp, n_scaled, n_root, y_done, y_turned, y_out, dve_own
         ) = ctx.enter_context(stage(
             nc, "f_abs", "f_exp", "f_exp1", "f_ln", "f_done", "f_tot", "tot_out", "built", "decayed", "scored",
             "maxed", "exped", "den_exp", "weighed", "turned", "turn_out", "summed", "h_done", "o_exp", "n_scaled",
             "n_root", "y_done", "y_turned", "y_out", "dve_own"))
        qb = sorted({ORDER[0][p] for p in q_at})
        b0, b1 = qb[0], qb[-1] + 1
        tri = (C_TRI_F, C_TRI_B)
        strict = (C_STR_F, C_STR_B)
        neg = (C_NEG_F, C_NEG_B)
        heads = [(dr, h) for dr in range(2) for h in range(ML_H)]

        @block.scalar
        def _(act):
            act.wait_ge(f_abs, 1)
            nc.scalar.activation(af[:, :, :], af[:, :, :], ACT.Exp, scale=-1.0).then_inc(f_exp, 1)
            act.wait_ge(f_exp1, 1)
            nc.scalar.activation(af[:, :, :], af[:, :, :], ACT.Ln).then_inc(f_ln, 1)
            nc.scalar.activation(og[:, b0:b1, :], t.mvo[:, b0:b1, ML_W:], ACT.Exp, scale=-1.0).then_inc(o_exp, 1)

            def t_copy(u):
                n = (units[u][2] + 1) * P
                act.wait_ge(turned, u + 1)
                if u >= 2:
                    act.wait_ge(summed, u - 1)
                nc.scalar.copy(at[:, u % 2, 0:n], m.ps[:, 4 + u % 2, 0:n]).then_inc(turn_out, 1)

            for u, (dr, h, p) in enumerate(units):
                n = (p + 1) * P
                act.wait_ge(maxed, u + 1)
                if u >= 2:
                    act.wait_ge(weighed, u - 1)
                nc.scalar.activation(w[:, u % 2, 0:n], m.ps[:, u % 2, 0:n], ACT.Exp, bias=st[:, 1, u:u + 1]
                                     ).then_inc(exped, 1)
                nc.scalar.activation(st[:, 2, u:u + 1], st[:, 1, u:u + 1], ACT.Exp).then_inc(den_exp, 1)
                if u >= 1:
                    t_copy(u - 1)
            t_copy(N - 1)
            act.wait_ge(n_scaled, 1)
            nc.scalar.activation(nr[:, b0:b1, :], nr[:, b0:b1, :], ACT.Sqrt).then_inc(n_root, 1)

        @block.tensor
        def _(pe):
            pe.wait_ge(f_done, 1)
            for dr in range(2):
                for p in range(NB):
                    blk = ORDER[dr]
                    for j in range(p + 1):
                        ins = nc.tensor.matmul(m.ps[:, 6, (dr * NB + p) * ML_H:(dr * NB + p + 1) * ML_H],
                                               m.sq[:, tri[dr] if j == p else C_ONES, :],
                                               lf[:, blk[j], dr * ML_H:(dr + 1) * ML_H], start=(j == 0), stop=(j == p))
            ins.then_inc(f_tot, 1)

            def decay(u):
                dr, h, p = units[u]
                blk, hd = ORDER[dr], heads.index((dr, h)) % 2
                pe.wait_ge(built, heads.index((dr, h)) + 1)
                if u >= 2:
                    pe.wait_ge(exped, u - 1)
                ones = m.sq[:, C_ONES, :]
                for j in range(p + 1):
                    out = m.ps[:, u % 2, j * P:(j + 1) * P]
                    if j == p:
                        nc.tensor.matmul(out, m.sq[:, tri[dr], :], same[:, hd, blk[p], :], start=True, stop=False)
                        ins = nc.tensor.matmul(out, m.sq[:, C_ID, :], m.sq[:, neg[dr], :], start=False, stop=True)
                        continue
                    nc.tensor.matmul(out, ones, same[:, hd, blk[j], :], start=True, stop=False)
                    for i in range(j + 1, p):
                        nc.tensor.matmul(out, ones, fb[:, hd, blk[i], :], start=False, stop=False)
                    nc.tensor.matmul(out, m.sq[:, tri[dr], :], fb[:, hd, blk[p], :], start=False, stop=True)
                ins.then_inc(decayed, 1)

            def score(u):
                dr, h, p = units[u]
                blk, half = ORDER[dr], 64 * (h % 2)
                if u >= 2:
                    pe.wait_ge(weighed, u - 1)
                for j in range(p + 1):
                    ins = nc.tensor.matmul(m.ps[:, 2 + u % 2, j * P:(j + 1) * P],
                                           t.mq[half:half + 64, h // 2, blk[p] * P:(blk[p] + 1) * P],
                                           t.mk[half:half + 64, h // 2, blk[j] * P:(blk[j] + 1) * P],
                                           start=True, stop=True)
                ins.then_inc(scored, 1)

            def turn(u):
                pe.wait_ge(weighed, u + 1)
                if u >= 2:
                    pe.wait_ge(turn_out, u - 1)
                for j in range(units[u][2] + 1):
                    ins = nc.tensor.transpose(m.ps[:, 4 + u % 2, j * P:(j + 1) * P], a[:, u % 2, j * P:(j + 1) * P],
                                              m.sq[:, C_ID, :])
                ins.then_inc(turned, 1)

            def values(u):
                dr, h, p = units[u]
                pe.wait_ge(turn_out, u + 1)
                if u == 0:
                    pe.wait_ge(tot_out, 1)
                if u >= 2:
                    pe.wait_ge(h_done, u - 1)
                for j in range(p + 1):
                    ins = nc.tensor.matmul(m.ps[:, 6 + u % 2, 0:HD], at[:, u % 2, j * P:(j + 1) * P],
                                           t.mvo[:, ORDER[dr][j], h * HD:(h + 1) * HD], start=(j == 0), stop=(j == p))
                ins.then_inc(summed, 1)

            decay(0)
            score(0)
            for u in range(N):
                if u + 1 < N:
                    decay(u + 1)
                    score(u + 1)
                turn(u)
                if u >= 1:
                    values(u - 1)
            values(N - 1)
            pe.wait_ge(y_done, 1)
            for i, b in enumerate(range(b0, b1)):
                if i >= 2:
                    pe.wait_ge(y_out, i - 1)
                for g in range(2):
                    ins = nc.tensor.transpose(m.ps[:, i % 2, g * P:(g + 1) * P], hh[:, b, g * P:(g + 1) * P],
                                              m.sq[:, C_ID, :])
                ins.then_inc(y_turned, 1)

        @block.vector
        def _(dve):
            own = Chain(dve, dve_own)
            nc.vector.scalar_tensor_tensor(out=af[:, :, :], in0=t.mg[:, :, 2 * ML_H:], scalar=-1.0,
                                           in1=t.mg[:, :, 2 * ML_H:], op0=ALU.mult, op1=ALU.max).then_inc(f_abs, 1)
            own.link(nc.vector.tensor_scalar(lf[:, :, :], t.mg[:, :, 2 * ML_H:], 0.0, None, ALU.min))
            dve.wait_ge(f_exp, 1)
            nc.vector.tensor_scalar(af[:, :, :], af[:, :, :], 1.0, None, ALU.add).then_inc(f_exp1, 1)
            dve.wait_ge(f_ln, 1)
            nc.vector.tensor_tensor(lf[:, :, :], lf[:, :, :], af[:, :, :], ALU.subtract).then_inc(f_done, 1)
            dve.wait_ge(f_done, 1)
            dve.wait_ge(f_tot, 1)
            nc.vector.tensor_copy(ft[:, :, :, :].rearrange("p a b c -> p (a b c)"),
                                  m.ps[:, 6, 0:2 * NB * ML_H]).then_inc(tot_out, 1)
            dve.wait_ge(tot_out, 1)

            def build(i):
                dr, h = heads[i]
                if i >= 2:
                    dve.wait_ge(decayed, (i - 1) * len(q_at))
                for b in range(NB):
                    own.step(nc.vector.tensor_scalar(same[:, i % 2, b, :], m.sq[:, C_ID, :],
                                                     t.mg[:, b, dr * ML_H + h:dr * ML_H + h + 1], None, ALU.mult))
                    own.step(nc.vector.tensor_scalar(fb[:, i % 2, b, :], m.sq[:, C_ONES, :],
                                                     lf[:, b, dr * ML_H + h:dr * ML_H + h + 1], None, ALU.mult))
                own.meet()
                for b in range(NB):
                    ins = nc.vector.scalar_tensor_tensor(
                        out=same[:, i % 2, b, :], in0=m.sq[:, strict[dr], :],
                        scalar=lf[:, b, dr * ML_H + h:dr * ML_H + h + 1], in1=same[:, i % 2, b, :],
                        op0=ALU.mult, op1=ALU.add)
                ins.then_inc(built, 1)

            def top(u):
                dr, h, p = units[u]
                dve.wait_ge(decayed, u + 1)
                own.link(nc.vector.reduce_max(st[:, 0, u:u + 1], m.ps[:, u % 2, 0:(p + 1) * P], axis=AX.X))
                nc.vector.tensor_scalar(st[:, 1, u:u + 1], st[:, 0, u:u + 1], ft[:, dr, p, h:h + 1], -1.0, ALU.max,
                                        ALU.mult).then_inc(maxed, 1)

            def output(u):
                dr, h, p = units[u]
                b = ORDER[dr][p]
                dve.wait_ge(den_exp, u + 1)
                own.link(nc.vector.scalar_tensor_tensor(out=st[:, 4, u:u + 1], in0=st[:, 3, u:u + 1], scalar=-1.0,
                                                        in1=st[:, 3, u:u + 1], op0=ALU.mult, op1=ALU.max))
                own.link(nc.vector.tensor_tensor(st[:, 4, u:u + 1], st[:, 4, u:u + 1], st[:, 2, u:u + 1], ALU.max))
                own.link(nc.vector.reciprocal(st[:, 5, u:u + 1], st[:, 4, u:u + 1]))
                dve.wait_ge(summed, u + 1)
                out, got = hh[:, b, h * HD:(h + 1) * HD], m.ps[:, 6 + u % 2, 0:HD]
                if dr == 0:
                    ins = nc.vector.tensor_scalar(out, got, st[:, 5, u:u + 1], None, ALU.mult)
                else:
                    ins = nc.vector.scalar_tensor_tensor(out=out, in0=got, scalar=st[:, 5, u:u + 1], in1=out,
                                                         op0=ALU.mult, op1=ALU.add)
                ins.then_inc(h_done, 1)

            build(0)
            build(1)
            top(0)
            for u, (dr, h, p) in enumerate(units):
                if u + 1 < N:
                    top(u + 1)
                i = u // len(q_at)
                if u % len(q_at) == len(q_at) - 1 and i + 2 < len(heads):
                    build(i + 2)
                n = (p + 1) * P
                dve.wait_ge(exped, u + 1)
                dve.wait_ge(scored, u + 1)
                if u >= 2:
                    dve.wait_ge(turned, u - 1)
                nc.vector.tensor_tensor_reduce(a[:, u % 2, 0:n], w[:, u % 2, 0:n], m.ps[:, 2 + u % 2, 0:n], SCALE, 0.0,
                                               ALU.mult, ALU.add, st[:, 3, u:u + 1]).then_inc(weighed, 1)
                dve.wait_ge(weighed, u + 1)
                if u >= 1:
                    output(u - 1)
            output(N - 1)
            dve.wait_ge(h_done, N)
            own.link(nc.vector.tensor_tensor(h2[:, b0:b1, :], hh[:, b0:b1, :], hh[:, b0:b1, :], ALU.mult))
            own.link(nc.vector.tensor_reduce(nr[:, b0:b1, :], h2[:, b0:b1, :].rearrange("p b (h e) -> p b h e", h=ML_H),
                                             axis=AX.X, op=ALU.add))
            nc.vector.tensor_scalar(nr[:, b0:b1, :], nr[:, b0:b1, :], 1.0 / HD, EPS, ALU.mult, ALU.add
                                    ).then_inc(n_scaled, 1)
            dve.wait_ge(o_exp, 1)
            own.link(nc.vector.tensor_scalar(og[:, b0:b1, :], og[:, b0:b1, :], 1.0, None, ALU.add))
            own.link(nc.vector.reciprocal(og[:, b0:b1, :], og[:, b0:b1, :]))
            own.link(nc.vector.tensor_tensor(hh[:, b0:b1, :], hh[:, b0:b1, :], og[:, b0:b1, :], ALU.mult))
            dve.wait_ge(n_root, 1)
            own.link(nc.vector.reciprocal(nr[:, b0:b1, :], nr[:, b0:b1, :]))
            for b in range(b0, b1):
                ins = nc.vector.tensor_tensor(
                    hh[:, b, :].rearrange("p (h e) -> p h e", h=ML_H), hh[:, b, :].rearrange("p (h e) -> p h e", h=ML_H),
                    nr[:, b, :].unsqueeze(2).to_broadcast([P, ML_H, HD]), ALU.mult)
                own.step(ins)
            own.meet()
            dve.sem_inc(y_done, 1)
            for i, b in enumerate(range(b0, b1)):
                dve.wait_ge(y_turned, i + 1)
                for g in range(2):
                    ins = nc.vector.tensor_scalar(t.yT[:, 2, g, b * P:(b + 1) * P], m.ps[:, i % 2, g * P:(g + 1) * P],
                                                  m.vec[:, V_MLN + g:V_MLN + g + 1], None, ALU.mult)
                ins.then_inc(y_out, 1)



SEQ = 256
KF = SEQ // P
TWO_PI_HI = 6.28125
TWO_PI_LO = 6.283185307179586 - 6.28125
ROUND = 1.5 * 2.0 ** 23
PI = 3.1415925


def hyena(nc, m, d, t, l, streams):
    S = len(streams)
    s0, C2 = streams[0], 2 * HY_W
    with ExitStack() as ctx:
        sb = lambda name, shape: ctx.enter_context(sbuf(nc, name, shape, F32))
        dft = sb("dft", [P, 4, KF, SEQ])
        dec = sb("decay", [P, KF, HY_W])
        feat = sb("feat", [33, SEQ])
        w1, w2, w3 = sb("w1", [33, 64]), sb("w2", [64, 64]), sb("w3", [64, 2 * C2])
        hid, arg, rnd = sb("hid", [64, SEQ]), sb("arg", [64, SEQ]), sb("rnd", [64, SEQ])
        filt = sb("filt", [P, KF, 2, 2, HY_W])
        fsq = sb("fsq", [P, KF, 2 * C2])
        frs = sb("frs", [P, C2])
        comb = sb("comb", [P, 2, KF, C2])
        spec = sb("spec", [P, 2, KF, C2])
        cv = sb("cv", [P, 6, TOK])
        z = sb("z", [P, KF, 2, HY_W])
        zf = sb("zf", [P, 2, KF, S * HY_W])
        yf = sb("yf", [P, 2, KF, S * HY_W])
        tmp = sb("tmp", [P, KF, S * HY_W])
        zt = sb("zt", [P, 2, TOK])
        (block, k_in, h_mult, arg_done, sine_done, f_mult, f_out, f_sq, f_sum, f_scaled, f_root, comb_done, s_mult,
         s_out, conv_done, z_turned, z_out, z_mult, zf_out, yf_done, y_mult, y_out, dve_own) = ctx.enter_context(stage(
             nc, "k_in", "h_mult", "arg_done", "sine_done", "f_mult", "f_out", "f_sq", "f_sum", "f_scaled", "f_root",
             "comb_done", "s_mult", "s_out", "conv_done", "z_turned", "z_out", "z_mult", "zf_out", "yf_done",
             "y_mult", "y_out", "dve_own"))

        @block.sync
        def _(sp):
            sp.dma_start(feat[:, :], d["k_feat"]).then_inc(k_in, 16)
            sp.dma_start(w1[:, :], d["hy_w1"][l]).then_inc(k_in, 16)
            sp.dma_start(w2[:, :], d["hy_w2"][l]).then_inc(k_in, 16)
            sp.dma_start(w3[:, :], d["hy_w3"][l]).then_inc(k_in, 16)
            sp.dma_start(dec[:, :, :], d["k_decay"].rearrange("(a p) n -> p a n", p=P)).then_inc(k_in, 16)
            sp.dma_start(dft[:, :, :, :], d["k_dft"].rearrange("c (a p) n -> p c a n", p=P)).then_inc(k_in, 16)

        @block.tensor
        def _(pe):
            pe.wait_ge(k_in, 96)
            nc.tensor.matmul(m.ps[0:64, 0, 0:SEQ], w1[:, :], feat[:, :], start=True, stop=True).then_inc(h_mult, 1)
            pe.wait_ge(sine_done, 1)
            nc.tensor.matmul(m.ps[0:64, 1, 0:SEQ], w2[:, :], hid[:, :], start=True, stop=True).then_inc(h_mult, 1)
            pe.wait_ge(sine_done, 2)
            for a in range(KF):
                for o in range(2):
                    nc.tensor.matmul(m.ps[:, 2 + 2 * a + o, :], hid[:, a * P:(a + 1) * P], w3[:, o * C2:(o + 1) * C2],
                                     start=True, stop=True).then_inc(f_mult, 1)
            pe.wait_ge(f_sq, 1)
            for o in range(2):
                for i in range(2 * KF):
                    a, r = i % KF, i // KF
                    ins = nc.tensor.matmul(m.ps[:, 0, o * HY_W:(o + 1) * HY_W], m.sq[:, C_ONES, :],
                                           fsq[:, a, o * C2 + r * HY_W:o * C2 + (r + 1) * HY_W], start=(i == 0),
                                           stop=(i == 2 * KF - 1))
            ins.then_inc(f_sum, 1)
            pe.wait_ge(comb_done, 1)
            for r in range(2):
                for kt in range(KF):
                    for a in range(KF):
                        ins = nc.tensor.matmul(m.ps[:, 4 + 2 * r + kt, :], dft[:, r, a, kt * P:(kt + 1) * P],
                                               comb[:, r, a, :], start=(a == 0), stop=(a == KF - 1))
                    ins.then_inc(s_mult, 1)
            pe.wait_ge(conv_done, 1)
            for order in range(2):
                src = cv if order == 0 else zt
                pe.wait_ge(s_out, 4)
                if order == 1:
                    pe.wait_ge(y_out, 2 * S)
                for a in range(KF):
                    for i, s in enumerate(streams):
                        for c in range(2):
                            ins = nc.tensor.transpose(m.ps[:, 2 + a, i * HY_W + c * P:i * HY_W + (c + 1) * P],
                                                      src[:, c, s * SEQ + a * P:s * SEQ + (a + 1) * P], m.sq[:, C_ID, :])
                    ins.then_inc(z_turned, 1)
                pe.wait_ge(z_out, 2 * (order + 1))
                for r in range(2):
                    for kt in range(KF):
                        for a in range(KF):
                            ins = nc.tensor.matmul(m.ps[:, 4 + 2 * r + kt, 0:S * HY_W], dft[:, r, a, kt * P:(kt + 1) * P],
                                                   z[:, a, 0:S, :].rearrange("p s c -> p (s c)"), start=(a == 0),
                                                   stop=(a == KF - 1))
                        ins.then_inc(z_mult, 1)
                pe.wait_ge(yf_done, order + 1)
                for i in range(S):
                    for c in range(2):
                        n = 0
                        for r in range(2):
                            for kt in range(KF):
                                ins = nc.tensor.matmul(m.ps[:, 2 * i + c, 0:SEQ],
                                                       yf[:, r, kt, i * HY_W + c * P:i * HY_W + (c + 1) * P],
                                                       dft[:, 2 + r, kt, :], start=(n == 0), stop=(n == 2 * KF - 1))
                                n += 1
                        ins.then_inc(y_mult, 1)

        @block.scalar
        def _(act):
            for i in range(2):
                act.wait_ge(arg_done, i + 1)
                nc.scalar.activation(hid[:, :], arg[:, :], ACT.Sin).then_inc(sine_done, 1)
            act.wait_ge(f_scaled, 1)
            nc.scalar.activation(frs[:, :], frs[:, :], ACT.Sqrt).then_inc(f_root, 1)
            for i in range(4):
                act.wait_ge(s_mult, i + 1)
                nc.scalar.copy(spec[:, i // 2, i % 2, :], m.ps[:, 4 + i, :]).then_inc(s_out, 1)
            for order in range(2):
                for a in range(KF):
                    act.wait_ge(z_turned, 2 * order + a + 1)
                    nc.scalar.copy(z[:, a, 0:S, :].rearrange("p s c -> p (s c)"), m.ps[:, 2 + a, 0:S * HY_W]
                                   ).then_inc(z_out, 1)
                if order == 1:
                    act.wait_ge(yf_done, 1)
                for i in range(4):
                    act.wait_ge(z_mult, 4 * order + i + 1)
                    nc.scalar.copy(zf[:, i // 2, i % 2, :], m.ps[:, 4 + i, 0:S * HY_W]).then_inc(zf_out, 1)

        @block.vector
        def _(dve):
            own = Chain(dve, dve_own)
            for i, vb in enumerate((V_B1, V_B2)):
                dve.wait_ge(h_mult, i + 1)
                if i == 1:
                    dve.wait_ge(sine_done, 1)
                own.link(nc.vector.tensor_scalar(arg[:, :], m.ps[0:64, i, 0:SEQ], m.vec[0:64, vb:vb + 1],
                                                 m.vec[0:64, V_FREQ + i:V_FREQ + i + 1], ALU.add, ALU.mult))
                own.link(nc.vector.tensor_scalar(rnd[:, :], arg[:, :], 1.0 / (TWO_PI_HI + TWO_PI_LO), ROUND, ALU.mult,
                                                 ALU.add))
                own.link(nc.vector.tensor_scalar(rnd[:, :], rnd[:, :], -ROUND, None, ALU.add))
                for part in (TWO_PI_HI, TWO_PI_LO):
                    own.link(nc.vector.scalar_tensor_tensor(out=arg[:, :], in0=rnd[:, :], scalar=-part, in1=arg[:, :],
                                                            op0=ALU.mult, op1=ALU.add))
                nc.vector.tensor_scalar(arg[:, :], arg[:, :], PI, -PI, ALU.min, ALU.max).then_inc(arg_done, 1)
            for a in range(KF):
                for o in range(2):
                    dve.wait_ge(f_mult, 2 * a + o + 1)
                    own.step(nc.vector.tensor_tensor(
                        filt[:, a, o, :, :], m.ps[:, 2 + 2 * a + o, :].rearrange("p (r c) -> p r c", r=2),
                        dec[:, a:a + 1, :].to_broadcast([P, 2, HY_W]), ALU.mult))
            own.meet()
            nc.vector.tensor_tensor(fsq[:, :, :], filt[:, :, :, :, :].rearrange("p a o r c -> p a (o r c)"),
                                    filt[:, :, :, :, :].rearrange("p a o r c -> p a (o r c)"), ALU.mult).then_inc(f_sq, 1)
            dve.wait_ge(f_sum, 1)
            nc.vector.tensor_scalar(frs[:, :], m.ps[:, 0, :], EPS, None, ALU.add).then_inc(f_scaled, 1)
            dve.wait_ge(f_root, 1)
            own.link(nc.vector.reciprocal(frs[:, :], frs[:, :]))
            for a in range(KF):
                for r in range(2):
                    own.step(nc.vector.tensor_tensor(filt[:, a, :, r, :], filt[:, a, :, r, :],
                                                     frs[:, :].rearrange("p (o c) -> p o c", o=2), ALU.mult))
            own.meet()
            own.link(nc.vector.memset(filt[0:1, 0, :, 1, :], 0.0))
            for a in range(KF):
                view = lambda x: x.rearrange("p (o c) -> p o c", o=2)
                own.step(nc.vector.tensor_tensor(view(comb[:, 0, a, :]), filt[:, a, :, 0, :], filt[:, a, :, 1, :], ALU.add))
                own.step(nc.vector.tensor_tensor(view(comb[:, 1, a, :]), filt[:, a, :, 0, :], filt[:, a, :, 1, :],
                                                 ALU.subtract))
            own.meet()
            dve.sem_inc(comb_done, 1)
            for g in range(6):
                tap = [m.vec[:, V_CONV + 6 * j + g:V_CONV + 6 * j + g + 1] for j in range(3)]
                u = lambda lo, hi: t.hy[:, g, s0 * SEQ:].rearrange("p (s n) -> p s n", n=SEQ)[:, :, lo:hi]
                o = lambda lo, hi: cv[:, g, s0 * SEQ:].rearrange("p (s n) -> p s n", n=SEQ)[:, :, lo:hi]
                own.link(nc.vector.tensor_scalar(o(0, SEQ), u(0, SEQ), tap[1], None, ALU.mult))
                own.link(nc.vector.scalar_tensor_tensor(out=o(1, SEQ), in0=u(0, SEQ - 1), scalar=tap[0],
                                                        in1=o(1, SEQ), op0=ALU.mult, op1=ALU.add))
                own.link(nc.vector.scalar_tensor_tensor(out=o(0, SEQ - 1), in0=u(1, SEQ), scalar=tap[2],
                                                        in1=o(0, SEQ - 1), op0=ALU.mult, op1=ALU.add))
            dve.sem_inc(conv_done, 1)
            for order in range(2):
                src = cv if order == 0 else zt
                dve.wait_ge(zf_out, 4 * (order + 1))
                bc = lambda r: spec[:, r, :, order * HY_W:(order + 1) * HY_W].unsqueeze(2).to_broadcast(
                    [P, KF, S, HY_W])
                vw = lambda x: x.rearrange("p k (s c) -> p k s c", s=S)
                if order == 1:
                    dve.wait_ge(y_mult, 2 * S)
                for r in range(2):
                    for kt in range(KF):
                        kk = slice(kt, kt + 1)
                        own.step(nc.vector.tensor_tensor(vw(yf[:, r, kk, :]), vw(zf[:, 0, kk, :]), bc(r)[:, kk], ALU.mult))
                        own.step(nc.vector.tensor_tensor(vw(tmp[:, kk, :]), vw(zf[:, 1, kk, :]), bc(1 - r)[:, kk],
                                                         ALU.mult))
                    own.meet()
                    own.link(nc.vector.tensor_tensor(yf[:, r, :, :], yf[:, r, :, :], tmp[:, :, :],
                                                     ALU.add if r else ALU.subtract))
                dve.sem_inc(yf_done, 1)
                for i, s in enumerate(streams):
                    for c in range(2):
                        dve.wait_ge(y_mult, 2 * S * order + 2 * i + c + 1)
                        tk = slice(s * SEQ, (s + 1) * SEQ)
                        vb = m.vec[:, V_HYB + 2 * order + c:V_HYB + 2 * order + c + 1]
                        own.link(nc.vector.scalar_tensor_tensor(out=zt[:, c, tk], in0=src[:, c, tk], scalar=vb,
                                                                in1=m.ps[:, 2 * i + c, 0:SEQ], op0=ALU.mult,
                                                                op1=ALU.add))
                        out = zt[:, c, tk] if order == 0 else t.yT[:, 3, c, tk]
                        nc.vector.tensor_tensor(out, zt[:, c, tk], cv[:, 2 + 2 * order + c, tk], ALU.mult
                                                ).then_inc(y_out, 1)
                if order == 0:
                    dve.wait_ge(y_out, 2 * S)




def merge(nc, m, d, hT, t, l, t0):
    T = TOK - t0
    halves = [(kind, lo, hi) for kind, lo, hi in ((1, 0, CTX), (0, CTX, TOK)) if lo >= t0]
    steps = [(k, i) for k in range(KD) for i in range(N_BRANCH)]
    with ExitStack() as ctx:
        wb = ctx.enter_context(sbuf(nc, "w_branch", [P, N_BRANCH * 2, D], F32))
        wg = ctx.enter_context(sbuf(nc, "w_gate", [P, 2, KD, N_BRANCH, P], F32))
        wo = ctx.enter_context(sbuf(nc, "w_out", [P, KD, D], F32))
        acc = ctx.enter_context(sbuf(nc, "merged", [P, KD, TOK], F32))
        sg = ctx.enter_context(sbuf(nc, "sig", [P, 2, TOK], F32))
        pr = ctx.enter_context(sbuf(nc, "prod", [P, 2, TOK], F32))
        (block, wb_in, wo_in, gate_mult, y_mult, sig_done, prod_done, acc_done, o_mult, o_out, wg_in0, wg_in1
         ) = ctx.enter_context(stage(nc, "wb_in", "wo_in", "gate_mult", "y_mult", "sig_done", "prod_done", "acc_done",
                                     "o_mult", "o_out", "wg_in0", "wg_in1"))
        wg_ins = (wg_in0, wg_in1)

        @block.sync
        def _(sp):
            gates = d["w_in"][l].rearrange("(k p) n -> p k n", p=P)[:, :, O_GATE:].rearrange(
                "p k (i n) -> p k i n", i=N_BRANCH)
            for k in range(KD):
                if k >= 2:
                    sp.wait_ge(gate_mult, N_BRANCH * (k - 1))
                for i in range(N_BRANCH):
                    sp.dma_start(wg[:, k % 2, :, i, :], gates[:, :, i, k * P:(k + 1) * P]).then_inc(wg_ins[k % 2], 16)
                if k == 0:
                    sp.dma_start(wb[:, :, :], d["w_branch"][l].rearrange("i (a p) n -> p (i a) n", p=P)).then_inc(wb_in, 16)
                if k == 2:
                    sp.dma_start(wo[:, :, :], d["w_out"][l].rearrange("(k p) n -> p k n", p=P)).then_inc(wo_in, 16)

        @block.tensor
        def _(pe):
            for n, (k, i) in enumerate(steps):
                if i == 0:
                    pe.wait_ge(wg_ins[k % 2], 16 * N_BRANCH * (k // 2 + 1))
                if n >= 2:
                    pe.wait_ge(sig_done, n - 1)
                for kk in range(KD):
                    ins = nc.tensor.matmul(m.ps[:, n % 2, 0:T], wg[:, k % 2, kk, i, :], hT[:, kk, t0:],
                                           start=(kk == 0), stop=(kk == KD - 1))
                ins.then_inc(gate_mult, 1)
                if n == 0:
                    pe.wait_ge(wb_in, 16)
                if n >= 2:
                    pe.wait_ge(prod_done, n - 1)
                for a in range(2):
                    ins = nc.tensor.matmul(m.ps[:, 2 + n % 2, 0:T], wb[:, 2 * i + a, k * P:(k + 1) * P],
                                           t.yT[:, i, a, t0:], start=(a == 0), stop=(a == 1))
                ins.then_inc(y_mult, 1)
            pe.wait_ge(wo_in, 16)
            pe.wait_ge(acc_done, len(steps))
            for k in range(KD):
                if k >= 4:
                    pe.wait_ge(o_out, k - 3)
                for kk in range(KD):
                    ins = nc.tensor.matmul(m.ps[:, 4 + k % 4, 0:T], wo[:, kk, k * P:(k + 1) * P], acc[:, kk, t0:],
                                           start=(kk == 0), stop=(kk == KD - 1))
                ins.then_inc(o_mult, 1)

        @block.scalar
        def _(act):
            for n in range(len(steps)):
                act.wait_ge(gate_mult, n + 1)
                if n >= 2:
                    act.wait_ge(prod_done, n - 1)
                nc.scalar.activation(sg[:, n % 2, t0:], m.ps[:, n % 2, 0:T], ACT.Sigmoid).then_inc(sig_done, 1)

        @block.vector
        def _(dve):
            for n, (k, i) in enumerate(steps):
                dve.wait_ge(y_mult, n + 1)
                dve.wait_ge(sig_done, n + 1)
                if n >= 2:
                    dve.wait_ge(acc_done, n - 1)
                if i == 0:
                    nc.vector.tensor_tensor(acc[:, k, t0:], sg[:, n % 2, t0:], m.ps[:, 2 + n % 2, 0:T], ALU.mult
                                            ).then_inc(prod_done, 1)
                    dve.wait_ge(prod_done, n + 1)
                    dve.sem_inc(acc_done, 1)
                    continue
                nc.vector.tensor_tensor(pr[:, n % 2, t0:], sg[:, n % 2, t0:], m.ps[:, 2 + n % 2, 0:T], ALU.mult
                                        ).then_inc(prod_done, 1)
                dve.wait_ge(prod_done, n + 1)
                dve.wait_ge(acc_done, n)
                nc.vector.tensor_tensor(acc[:, k, t0:], acc[:, k, t0:], pr[:, n % 2, t0:], ALU.add).then_inc(acc_done, 1)
            for k in range(KD):
                dve.wait_ge(o_mult, k + 1)
                for kind, lo, hi in halves:
                    ins = nc.vector.scalar_tensor_tensor(
                        out=m.resid[:, k, lo:hi], in0=m.ps[:, 4 + k % 4, lo - t0:hi - t0],
                        scalar=m.mod[:, 2 * KD + k, kind:kind + 1], in1=m.resid[:, k, lo:hi], op0=ALU.mult, op1=ALU.add)
                ins.then_inc(o_out, 1)




def peer_select(nc, m, d, hT, sel, l, t0):
    T = TOK - t0
    CH = 512
    NCH = PH * 2 * P // CH
    tb0 = t0 // P
    blocks = list(range(tb0, NB))
    with ExitStack() as ctx:
        sb = lambda name, shape, dt=F32: ctx.enter_context(sbuf(nc, name, shape, dt))
        wq = sb("wq", [P, 2, KD, CH])
        qT = sb("qT", [P, HC, TOK])
        sk = sb("subkeys", [P, HC, P])
        skT = sb("subkeysT", [P, HC, P])
        sc = sb("scores", [P, 2, HC, P])
        s2 = sb("scores2", [P, HC, P])
        sv = sb("sv", [P, HC, TOPK])
        si = sb("si", [P, HC, TOPK], U32)
        sif = sb("sif", [P, HC, TOPK])
        cand = sb("cand", [P, PH, TOPK * TOPK])
        cand2 = sb("cand2", [P, PH, TOPK * TOPK])
        best = sb("best", [P, PH, TOPK])
        pos = sb("pos", [P, PH, TOPK], U32)
        part = sb("part", [P, 2, PH, TOPK], U32)
        partf = sb("partf", [P, 2, PH, TOPK])
        eq = sb("eq", [P, PH * TOPK, TOPK])
        pick = sb("pick", [P, 2, 3, P])
        dn = sb("dn", [P, PH])
        (block, sk_in, sk_turned, sk_out, q_mult, q_out, s_mult, s_out, s_used, diffed, g_exp, picked, p_turned,
         p_out, dve_own, wq_in0, wq_in1) = ctx.enter_context(stage(
             nc, "sk_in", "sk_turned", "sk_out", "q_mult", "q_out", "s_mult", "s_out", "s_used", "diffed", "g_exp",
             "picked", "p_turned", "p_out", "dve_own", "wq_in0", "wq_in1"))
        wq_ins = (wq_in0, wq_in1)
        LOW = -3.0e38

        @block.sync
        def _(sp):
            for c in range(NCH):
                if c >= 2:
                    sp.wait_ge(q_mult, 4 * (c - 1))
                sp.dma_start(wq[:, c % 2, :, :], d["peer_wq"][l].rearrange("(k p) n -> p k n", p=P)[
                    :, :, c * CH:(c + 1) * CH]).then_inc(wq_ins[c % 2], 16)
                if c == 0:
                    sp.dma_start(sk[:, :, :], d["peer_subkeys"][l].rearrange("h c n d -> n (h c) d")).then_inc(sk_in, 16)

        @block.tensor
        def _(pe):
            for g in range(HC):
                if g % 4 == 0:
                    pe.wait_ge(wq_ins[g // 4 % 2], 16 * (g // 8 + 1))
                if g >= 2:
                    pe.wait_ge(q_out, g - 1)
                for k in range(KD):
                    ins = nc.tensor.matmul(m.ps[:, g % 2, 0:T], wq[:, g // 4 % 2, k, (g % 4) * P:(g % 4 + 1) * P],
                                           hT[:, k, t0:], start=(k == 0), stop=(k == KD - 1))
                ins.then_inc(q_mult, 1)
            pe.wait_ge(sk_in, 16)
            for q in range(4):
                if q >= 2:
                    pe.wait_ge(sk_out, q - 1)
                for i in range(4):
                    ins = nc.tensor.transpose(m.ps[:, 2 + q % 2, i * P:(i + 1) * P], sk[:, 4 * q + i, :], m.sq[:, C_ID, :])
                ins.then_inc(sk_turned, 1)
            pe.wait_ge(sk_out, 4)
            pe.wait_ge(q_out, HC)

            def turn(n):
                pe.wait_ge(picked, n + 1)
                if n >= 1:
                    pe.wait_ge(p_out, n)
                for i in range(3):
                    ins = nc.tensor.transpose(m.ps[:, 0, i * P:(i + 1) * P], pick[:, n % 2, i, :], m.sq[:, C_ID, :])
                ins.then_inc(p_turned, 1)

            for n, b in enumerate(blocks):
                for q in range(4):
                    if n >= 1:
                        pe.wait_ge(s_out, 4 * (n - 1) + q + 1)
                    for i in range(4):
                        hc = 4 * q + i
                        ins = nc.tensor.matmul(m.ps[:, 4 + q, i * P:(i + 1) * P], qT[:, hc, b * P:(b + 1) * P],
                                               skT[:, hc, :], start=True, stop=True)
                    ins.then_inc(s_mult, 1)
                if n >= 1:
                    turn(n - 1)
            turn(len(blocks) - 1)

        @block.scalar
        def _(act):
            for g in range(HC):
                act.wait_ge(q_mult, g + 1)
                nc.scalar.copy(qT[:, g, t0:], m.ps[:, g % 2, 0:T]).then_inc(q_out, 1)
            for q in range(4):
                act.wait_ge(sk_turned, q + 1)
                nc.scalar.copy(skT[:, 4 * q:4 * q + 4, :].rearrange("p a b -> p (a b)"), m.ps[:, 2 + q % 2, :]
                               ).then_inc(sk_out, 1)

            def weights(n):
                act.wait_ge(diffed, n + 1)
                nc.scalar.activation(pick[:, n % 2, 2, :], pick[:, n % 2, 2, :], ACT.Exp).then_inc(g_exp, 1)
                act.wait_ge(p_turned, n + 1)
                b = blocks[n]
                nc.scalar.copy(sel[:, :, b * P:(b + 1) * P], m.ps[:, 0, 0:3 * P].rearrange("p (a b) -> p a b", a=3)
                               ).then_inc(p_out, 1)

            for n, b in enumerate(blocks):
                if n >= 2:
                    act.wait_ge(s_used, n - 1)
                for q in range(4):
                    act.wait_ge(s_mult, 4 * n + q + 1)
                    nc.scalar.copy(sc[:, n % 2, 4 * q:4 * q + 4, :].rearrange("p a b -> p (a b)"), m.ps[:, 4 + q, :]
                                   ).then_inc(s_out, 1)
                if n >= 1:
                    weights(n - 1)
            weights(len(blocks) - 1)

        @block.vector
        def _(dve):
            own = Chain(dve, dve_own)

            def top16(rows, val, idx, src, src2):
                for r in range(rows):
                    own.step(nc.vector.max(val(r, 0), src(r)))
                own.meet()
                for r in range(rows):
                    own.step(nc.vector.max_index(idx(r, 0), val(r, 0), src(r)))
                    own.step(nc.vector.match_replace(src2(r), val(r, 0), src(r), LOW))
                own.meet()
                for r in range(rows):
                    own.step(nc.vector.max(val(r, 1), src2(r)))
                own.meet()
                for r in range(rows):
                    own.step(nc.vector.max_index(idx(r, 1), val(r, 1), src2(r)))
                own.meet()

            for n, b in enumerate(blocks):
                dve.wait_ge(s_out, 4 * (n + 1))
                top16(HC, lambda r, j: sv[:, r, 8 * j:8 * j + 8], lambda r, j: si[:, r, 8 * j:8 * j + 8],
                      lambda r: sc[:, n % 2, r, :], lambda r: s2[:, r, :])
                dve.sem_inc(s_used, 1)
                own.link(nc.vector.tensor_copy(sif[:, :, :], si[:, :, :]))
                svp = sv[:, :, :].rearrange("p (h c) k -> p h c k", c=2)
                own.link(nc.vector.tensor_tensor(
                    cand[:, :, :].rearrange("p h (a b) -> p h a b", a=TOPK),
                    svp[:, :, 0, :].unsqueeze(3).to_broadcast([P, PH, TOPK, TOPK]),
                    svp[:, :, 1, :].unsqueeze(2).to_broadcast([P, PH, TOPK, TOPK]), ALU.add))
                top16(PH, lambda r, j: best[:, r, 8 * j:8 * j + 8], lambda r, j: pos[:, r, 8 * j:8 * j + 8],
                      lambda r: cand[:, r, :], lambda r: cand2[:, r, :])
                if n >= 2:
                    dve.wait_ge(p_turned, n - 1)
                nc.vector.tensor_tensor(pick[:, n % 2, 2, :].rearrange("p (h k) -> p h k", h=PH), best[:, :, :],
                                        best[:, :, 0:1].to_broadcast([P, PH, TOPK]), ALU.subtract).then_inc(diffed, 1)
                own.step(nc.vector.tensor_scalar(part[:, 0, :, :], pos[:, :, :], 4, None, ALU.logical_shift_right))
                own.step(nc.vector.tensor_scalar(part[:, 1, :, :], pos[:, :, :], 15, None, ALU.bitwise_and))
                own.meet()
                own.link(nc.vector.tensor_copy(partf[:, :, :, :], part[:, :, :, :]))
                sip = sif[:, :, :].rearrange("p (h c) k -> p h c k", c=2)
                for c in range(2):
                    own.link(nc.vector.tensor_tensor(
                        eq[:, :, :], partf[:, c, :, :].rearrange("p h k -> p (h k)").unsqueeze(2).to_broadcast(
                            [P, PH * TOPK, TOPK]),
                        m.sq[:, C_IOTA:C_IOTA + 1, 0:TOPK].to_broadcast([P, PH * TOPK, TOPK]), ALU.is_equal))
                    for h in range(PH):
                        e = eq[:, h * TOPK:(h + 1) * TOPK, :]
                        own.step(nc.vector.tensor_tensor(e, e, sip[:, h, c:c + 1, :].to_broadcast([P, TOPK, TOPK]),
                                                         ALU.mult))
                    own.meet()
                    own.link(nc.vector.tensor_reduce(pick[:, n % 2, c, :], eq[:, :, :], axis=AX.X, op=ALU.add))
                dve.wait_ge(g_exp, n + 1)
                own.link(nc.vector.tensor_reduce(dn[:, :], pick[:, n % 2, 2, :].rearrange("p (h k) -> p h k", h=PH),
                                                 axis=AX.X, op=ALU.add))
                own.link(nc.vector.reciprocal(dn[:, :], dn[:, :]))
                nc.vector.tensor_tensor(pick[:, n % 2, 2, :].rearrange("p (h k) -> p h k", h=PH),
                                        pick[:, n % 2, 2, :].rearrange("p (h k) -> p h k", h=PH),
                                        dn[:, :].unsqueeze(2).to_broadcast([P, PH, TOPK]), ALU.mult).then_inc(picked, 1)


def peer_weights(nc, m, sel, wd, t0):
    GRP = 4
    STEP = 16
    TURNS = P // STEP
    G = STEP // GRP
    blocks = list(range(t0 // P, NB))
    with ExitStack() as ctx:
        ia = ctx.enter_context(sbuf(nc, "hot_i", [P, STEP, P], F32))
        ib = ctx.enter_context(sbuf(nc, "hot_j", [P, STEP, P], F32))
        wsb = ctx.enter_context(sbuf(nc, "w_block", [P, 2, P, P], F32))
        keys = ctx.enter_context(sbuf(nc, "keys", [P, STEP], F32))
        (block, slots_seen, keys_in, hot_i, hot_j, w_free, w_mult, w_banks, w_out, w_stored0, w_stored1) = ctx.enter_context(
            stage(nc, "slots_seen", "keys_in", "hot_i", "hot_j", "w_free", "w_mult", "w_banks", "w_out", "w_stored0", "w_stored1"))
        w_stored = (w_stored0, w_stored1)

        @block.vector
        def _(dve):
            dve.sem_inc(w_free, G)
            for n, b in enumerate(blocks):
                with dve.Fori(0, TURNS) as i:
                    for s in range(STEP):
                        if s % GRP == 0:
                            dve.wait_ge(w_free, i * G + (n * TURNS * G + s // GRP + 1))
                        tok = i * STEP + (b * P + s)
                        nc.vector.tensor_scalar(ia[:, s, :], m.sq[:, C_IOTA, :], sel[:, 0, bass.ds(tok, 1)],
                                                sel[:, 2, bass.ds(tok, 1)], ALU.is_equal, ALU.mult).then_inc(hot_i, 1)

        @block.gpsimd
        def _(pool):
            for n, b in enumerate(blocks):
                with pool.Fori(0, TURNS) as i:
                    nc.gpsimd.tensor_copy(keys[:, :], sel[:, 1, bass.ds(i * STEP + b * P, STEP)]).then_inc(keys_in, 1)
                    pool.wait_ge(keys_in, i + (n * TURNS + 1))
                    for s in range(STEP):
                        if s % GRP == 0:
                            pool.wait_ge(w_free, i * G + (n * TURNS * G + s // GRP + 1))
                            pool.sem_inc(slots_seen, 1)
                        nc.gpsimd.tensor_scalar(ib[:, s, :], m.sq[:, C_IOTA, :], keys[:, s:s + 1], None,
                                                ALU.is_equal).then_inc(hot_j, 1)
                    pool.wait_ge(hot_j, i * STEP + (n * P + STEP))

        @block.tensor
        def _(pe):
            for n, b in enumerate(blocks):
                with pe.Fori(0, TURNS) as i:
                    for g in range(G):
                        pe.wait_ge(hot_i, i * STEP + (n * P + (g + 1) * GRP))
                        pe.wait_ge(hot_j, i * STEP + (n * P + (g + 1) * GRP))
                        pe.wait_ge(w_banks, i * G + (n * TURNS * G + g + 1))
                        for s in range(GRP):
                            ins = nc.tensor.matmul(m.ps[:, g, s * P:(s + 1) * P], ia[:, g * GRP + s, :],
                                                   ib[:, g * GRP + s, :], start=True, stop=True)
                        ins.then_inc(w_mult, 1)
                        pe.wait_ge(w_mult, i * G + (n * TURNS * G + g + 1))
                        pe.sem_inc(w_free, 1)

        @block.scalar
        def _(act):
            act.sem_inc(w_banks, G)
            for n, b in enumerate(blocks):
                if n >= 2:
                    act.wait_ge(w_stored[n % 2], 16 * (n // 2))
                with act.Fori(0, TURNS) as i:
                    for g in range(G):
                        act.wait_ge(w_mult, i * G + (n * TURNS * G + g + 1))
                        nc.scalar.copy(wsb[:, n % 2, :, bass.ds(i * STEP + g * GRP, GRP)],
                                       m.ps[:, g, :].rearrange("p (s j) -> p j s", s=GRP)).then_inc(w_out, 1)
                        act.wait_ge(w_out, i * G + (n * TURNS * G + g + 1))
                        act.sem_inc(w_banks, 1)

        @block.sync
        def _(sp):
            for n, b in enumerate(blocks):
                sp.wait_ge(w_out, (n + 1) * TURNS * G)
                sp.dma_start(wd.rearrange("j i t -> i j t")[:, :, b * P:(b + 1) * P], wsb[:, n % 2, :, :]
                             ).then_inc(w_stored[n % 2], 16)
            for n in range(max(0, len(blocks) - 2), len(blocks)):
                sp.wait_ge(w_stored[n % 2], 16 * (n // 2 + 1))


def peer_experts(nc, m, d, hT, wd, l, t0):
    T = TOK - t0
    GRP = 4
    NG = NK // GRP
    halves = [(kind, lo, hi) for kind, lo, hi in ((1, 0, CTX), (0, CTX, TOK)) if lo >= t0]
    ug = d["peer_u"][l].rearrange("(i g q) n -> g i q n", g=NG, q=GRP)
    vg = d["peer_v"][l].rearrange("(i g q) n -> g i q n", g=NG, q=GRP)
    wg = wd.rearrange("(g q) i t -> g i q t", q=GRP)
    with ExitStack() as ctx:
        sb = lambda name, shape: ctx.enter_context(sbuf(nc, name, shape, F32))
        us = [sb(f"u{i}", [P, GRP, D]) for i in range(2)]
        vs = [sb(f"v{i}", [P, GRP, D]) for i in range(2)]
        ws = [sb(f"w{i}", [P, GRP, T]) for i in range(2)]
        ut = sb("uT", [P, 2, KD, P])
        ga = sb("gelu", [P, 2, T])
        wa = sb("wa", [P, 2, GRP, T])
        acc = sb("experts_out", [P, KD, T])
        (block, u_in0, u_in1, vw_in0, vw_in1, u_turned, ut_act, ut_dve, a_mult, gelu_done, wa_done, o_mult, o_out,
         dve_own) = ctx.enter_context(stage(
             nc, "u_in0", "u_in1", "vw_in0", "vw_in1", "u_turned", "ut_act", "ut_dve", "a_mult", "gelu_done",
             "wa_done", "o_mult", "o_out", "dve_own"))
        u_ins, vw_ins = (u_in0, u_in1), (vw_in0, vw_in1)

        @block.sync
        def _(sp):
            def pair(i, first):
                for r in range(2):
                    g = 2 * i + r
                    if not first:
                        sp.wait_ge(u_turned, i * (2 * GRP) + (r - 1) * GRP)
                    sp.dma_start(us[r][:, :, :], ug[g]).then_inc(u_ins[r], 16)
                    if not first:
                        sp.wait_ge(o_mult, i * (2 * KD) + (r - 1) * KD)
                    sp.dma_start(vs[r][:, :, :], vg[g]).then_inc(vw_ins[r], 16)
                    sp.dma_start(ws[r][:, :, :], wg[g][:, :, t0:]).then_inc(vw_ins[r], 16)

            pair(0, True)
            with sp.Fori(1, NG // 2) as i:
                pair(i, False)

        @block.tensor
        def _(pe):
            def tile(pair, r, q, first):
                n = pair * (2 * GRP) + (r * GRP + q)
                if q == 0:
                    pe.wait_ge(u_ins[r], pair * 16 + 16)
                if not (first and r == 0 and q < 2):
                    pe.wait_ge(ut_act, n - 1)
                    pe.wait_ge(ut_dve, n - 1)
                for k in range(KD):
                    ins = nc.tensor.transpose(m.ps[:, 2 * (q % 2) + k // 4, (k % 4) * P:(k % 4 + 1) * P],
                                              us[r][:, q, k * P:(k + 1) * P], m.sq[:, C_ID, :])
                ins.then_inc(u_turned, 1)

            def activations(pair, r, q, first):
                n = pair * (2 * GRP) + (r * GRP + q)
                pe.wait_ge(ut_act, n + 1)
                pe.wait_ge(ut_dve, n + 1)
                if not (first and r == 0 and q < 2):
                    pe.wait_ge(gelu_done, n - 1)
                for k in range(KD):
                    ins = nc.tensor.matmul(m.ps[:, 4 + q % 2, 0:T], ut[:, q % 2, k, :], hT[:, k, t0:], start=(k == 0),
                                           stop=(k == KD - 1))
                ins.then_inc(a_mult, 1)

            def outputs(pair, r, q, first):
                g = pair * 2 + r
                if q == 0:
                    pe.wait_ge(wa_done, g * GRP)
                    pe.wait_ge(vw_ins[1 - r], pair * 32 + 32 * r)
                for j in range(2):
                    k = 2 * q + j
                    if not (first and r == 1 and q == 0):
                        pe.wait_ge(o_out, g * KD + (k - KD - 1))
                    for e in range(GRP):
                        ins = nc.tensor.matmul(m.ps[:, 6 + j, 0:T], vs[1 - r][:, e, k * P:(k + 1) * P],
                                               wa[:, 1 - r, e, :], start=(e == 0), stop=(e == GRP - 1))
                    ins.then_inc(o_mult, 1)

            def group(pair, r, first):
                for q in range(GRP):
                    if q + 1 < GRP:
                        tile(pair, r, q + 1, first)
                    elif r == 0:
                        tile(pair, 1, 0, first)
                    activations(pair, r, q, first)
                    if not (first and r == 0):
                        outputs(pair, r, q, first)

            tile(0, 0, 0, True)
            group(0, 0, True)
            group(0, 1, True)
            with pe.Fori(1, NG // 2) as i:
                tile(i, 0, 0, False)
                group(i, 0, False)
                group(i, 1, False)
            for q in range(GRP):
                outputs(NG // 2, 0, q, False)

        @block.scalar
        def _(act):
            def group(pair, r, first):
                for q in range(GRP):
                    n = pair * (2 * GRP) + (r * GRP + q)
                    act.wait_ge(u_turned, n + 1)
                    if not (first and r == 0 and q < 2):
                        act.wait_ge(a_mult, n - 1)
                    nc.scalar.copy(ut[:, q % 2, 0:4, :].rearrange("p a b -> p (a b)"), m.ps[:, 2 * (q % 2), :]
                                   ).then_inc(ut_act, 1)
                    act.wait_ge(a_mult, n + 1)
                    if not (first and r == 0 and q < 2):
                        act.wait_ge(wa_done, n - 1)
                    nc.scalar.activation(ga[:, q % 2, :], m.ps[:, 4 + q % 2, 0:T], ACT.Gelu_apprx_tanh
                                         ).then_inc(gelu_done, 1)

            group(0, 0, True)
            group(0, 1, True)
            with act.Fori(1, NG // 2) as i:
                group(i, 0, False)
                group(i, 1, False)

        @block.vector
        def _(dve):
            def add_out(pair, r, q):
                for j in range(2):
                    k = 2 * q + j
                    dve.wait_ge(o_mult, pair * (2 * KD) + (r * KD + k - KD + 1))
                    nc.vector.tensor_tensor(acc[:, k, :], acc[:, k, :], m.ps[:, 6 + j, 0:T], ALU.add).then_inc(o_out, 1)

            def group(pair, r, first):
                for q in range(GRP):
                    n = pair * (2 * GRP) + (r * GRP + q)
                    dve.wait_ge(u_turned, n + 1)
                    if not (first and r == 0 and q < 2):
                        dve.wait_ge(a_mult, n - 1)
                    nc.vector.tensor_copy(ut[:, q % 2, 4:8, :].rearrange("p a b -> p (a b)"),
                                          m.ps[:, 2 * (q % 2) + 1, :]).then_inc(ut_dve, 1)
                    if not (first and r == 0):
                        add_out(pair, r, q)
                    if q == 0:
                        dve.wait_ge(vw_ins[r], pair * 32 + 32)
                        if not first:
                            dve.wait_ge(o_mult, pair * (2 * KD) + (r - 1) * KD)
                    dve.wait_ge(gelu_done, n + 1)
                    nc.vector.tensor_tensor(wa[:, r, q, :], ga[:, q % 2, :], ws[r][:, q, :], ALU.mult
                                            ).then_inc(wa_done, 1)

            own = Chain(dve, dve_own)
            own.link(nc.vector.memset(acc[:, :, :], 0.0))
            group(0, 0, True)
            group(0, 1, True)
            with dve.Fori(1, NG // 2) as i:
                group(i, 0, False)
                group(i, 1, False)
            for q in range(GRP):
                add_out(NG // 2, 0, q)
            dve.wait_ge(o_out, NG * KD)
            for k in range(KD):
                for kind, lo, hi in halves:
                    nc.vector.scalar_tensor_tensor(
                        out=m.resid[:, k, lo:hi], in0=acc[:, k, lo - t0:hi - t0],
                        scalar=m.mod[:, 5 * KD + k, kind:kind + 1], in1=m.resid[:, k, lo:hi], op0=ALU.mult, op1=ALU.add)


def store(nc, m, out):
    with ExitStack() as ctx:
        tok = ctx.enter_context(sbuf(nc, "tok", [P, 2, D], F32))
        block, turned, copied, stored = ctx.enter_context(stage(nc, "turned", "copied", "stored"))

        @block.tensor
        def _(pe):
            for b in range(2):
                for k in range(KD):
                    ins = nc.tensor.transpose(m.ps[:, 2 * b + k // 4, (k % 4) * P:(k % 4 + 1) * P],
                                              m.resid[:, k, CTX + b * P:CTX + (b + 1) * P], m.sq[:, C_ID, :])
                    if k % 4 == 3:
                        ins.then_inc(turned, 1)

        @block.scalar
        def _(act):
            for i in range(4):
                act.wait_ge(turned, i + 1)
                nc.scalar.copy(tok[:, i // 2, (i % 2) * 512:(i % 2) * 512 + 512], m.ps[:, i, :]).then_inc(copied, 1)

        @block.sync
        def _(sp):
            sp.wait_ge(copied, 4)
            sp.dma_start(out[0].rearrange("(b p) n -> p b n", p=P), tok[:, :, :]).then_inc(stored, 16)
            sp.wait_ge(stored, 16)


def build(nc, d, out, upto=None, tap=None):
    NUMBER[:] = [0, 0]
    wd = nc.dram_tensor("peer_w", (NK, NK, TOK), F32, kind="Internal").ap()
    m = Mem()
    t = Mem()
    with ExitStack() as ctx:
        sb = lambda name, shape: ctx.enter_context(sbuf(nc, name, shape, F32))
        m.ps = ctx.enter_context(nc.psum_tensor("ps", [P, BANKS, BANK], F32))
        m.sq = sb("squares", [P, C_N, P])
        m.resid = sb("resid", [P, KD, TOK])
        m.cond = sb("cond", [P, KD, 2])
        m.vec = sb("vec", [P, V_ROWS])
        m.mod = sb("mod", [P, 6 * KD, 2])
        setup(nc, m, d)
        for l in range(LAYERS):
            last = l == LAYERS - 1
            own0 = CTX if last else 0
            modulation(nc, m, d, l)
            with sbuf(nc, "hT", [P, KD, TOK], F32) as hT:
                mod_norm(nc, m, hT, 0, 0)
                with ExitStack() as inner:
                    tb = lambda name, shape: inner.enter_context(sbuf(nc, name, shape, F32))
                    t.yT = tb("yT", [P, N_BRANCH, 2, TOK])
                    with ExitStack() as branch:
                        tb = lambda name, shape: branch.enter_context(sbuf(nc, name, shape, F32))
                        t.ckv, t.kpe, t.cq = tb("ckv", [P, TOK]), tb("kpe", [P, TOK]), tb("cq", [P, 2, TOK])
                        t.gq, t.gk, t.gv = tb("gq", [P, 2, TOK]), tb("gk", [P, TOK]), tb("gv", [P, NB, P])
                        t.mq, t.mk = tb("mq", [P, 2, TOK]), tb("mk", [P, 2, TOK])
                        t.mvo, t.mg = tb("mvo", [P, NB, 2 * ML_W]), tb("mg", [P, NB, 4 * ML_H])
                        t.hy = tb("hy", [P, 6, TOK])
                        input_projection(nc, m, d, hT, t, l, own0)
                        with sbuf(nc, "qm", [P, MLA_H, TOK], F32) as t.qm, \
                                sbuf(nc, "km", [P, MLA_H, TOK], F32) as t.km, \
                                sbuf(nc, "vm", [P, NB, MLA_H * MLA_V], F32) as t.vm:
                            attention_heads(nc, m, d, t, l, own0)
                            attention(nc, m, t, range(own0 // P, NB))
                        mlstm(nc, m, t, range(own0 // P, NB))
                        hyena(nc, m, d, t, l, (1,) if last else (0, 1))
                    if tap:
                        tap(f"hT{l}", hT)
                        tap(f"yT{l}", t.yT)
                    merge(nc, m, d, hT, t, l, own0)
                mod_norm(nc, m, hT, 3 * KD, own0)
                if tap:
                    tap(f"xm{l}", m.resid)
                    tap(f"h2T{l}", hT)
                with sbuf(nc, "sel", [P, 3, TOK], F32) as sel:
                    peer_select(nc, m, d, hT, sel, l, own0)
                    if tap:
                        tap(f"sel{l}", sel)
                    peer_weights(nc, m, sel, wd, own0)
                peer_experts(nc, m, d, hT, wd, l, own0)
            if tap:
                tap(f"x{l}", m.resid)
            if upto == l:
                break
        store(nc, m, out)



_INS = ["x", "c", "ctx", "c_ctx", "ada_w", "ada_b", "norm1", "norm2", "w_in", "mla_q_norm", "mla_kv_norm",
        "mla_w_uq", "mla_w_ukv", "mla_qk_norm_q", "mla_qk_norm_k", "gqa_qk_norm_q", "gqa_qk_norm_k", "ml_gate_b",
        "ml_norm", "hy_conv", "hy_w1", "hy_b1", "hy_freq", "hy_w2", "hy_b2", "hy_w3", "hy_bias", "w_branch", "w_out",
        "peer_wq", "peer_subkeys", "peer_u", "peer_v"]


def _constants():
    import math

    import numpy as np

    f = np.float32
    r, c = np.arange(P)[:, None], np.arange(P)[None, :]
    rot = {}
    for name, base, half, n in (("m", MLA_NOPE, 8, 2), ("g", 0, 16, 4)):
        a = np.zeros((P, P), f)
        for s in range(n):
            for j in range(half):
                lo = base + s * 2 * half + j
                a[lo + half, lo] = -1
                a[lo, lo + half] = 1
        rot[name] = a
    square = np.concatenate([
        r == c, np.ones((P, P)), r // HD == c // HD, r <= c, r >= c, r > c, r < c,
        np.where(c > r, -1e30, 0), np.where(c < r, -1e30, 0), rot["m"], rot["g"], np.broadcast_to(c, (P, P))]).astype(f)
    grid_w = 64
    pos = (np.arange(LAT) // grid_w, np.arange(LAT) % grid_w)
    rope = np.zeros((4, P, TOK), f)
    rope[0::2] = 1
    for i, (base, half, reps) in enumerate(((MLA_NOPE, 8, 1), (0, 16, 2))):
        inv = (f(10000.0) ** (-np.arange(0, 2 * half, 2, dtype=f) / f(2 * half))).astype(f)
        for rep in range(reps):
            for ax in range(2):
                ang = (pos[ax].astype(f)[:, None] * inv).T
                for side in range(2):
                    at = base + rep * HD + ax * 2 * half + side * half
                    rope[2 * i, at:at + half, CTX:] = np.cos(ang)
                    rope[2 * i + 1, at:at + half, CTX:] = np.sin(ang)
    n = np.arange(SEQ)
    ang = 2 * np.pi * np.outer(n, n + 0.5) / (2 * SEQ)
    dft = np.stack([np.cos(ang), -np.sin(ang), np.cos(ang).T / SEQ, -np.sin(ang).T / SEQ]).astype(f)
    tt = np.arange(SEQ, dtype=f) / f(SEQ)
    a2 = f(2.0 * math.pi) * tt[:, None] * np.arange(1, 17, dtype=f)
    feat = np.concatenate([tt[:, None], np.sin(a2), np.cos(a2)], axis=1).T.astype(f)
    lt = math.log(1e-2)
    alpha = np.linspace(-lt / 1.5, -lt / 0.3, HY_W, dtype=f)
    decay = np.exp(-tt[:, None] * alpha).astype(f)
    return {"k_square": square, "k_rope": rope.reshape(4 * P, TOK), "k_dft": dft, "k_feat": feat, "k_decay": decay}


def kernel(**inputs):
    import numpy as _np
    import concourse.bacc as _bacc
    from concourse.bass_utils import run_bass_kernel_spmd as _run

    nc = _bacc.Bacc("TRN2", target_bir_lowering=False, num_devices=1)
    arrays, d = {}, {}
    for name, a in [(n, inputs[n]) for n in _INS] + list(_constants().items()):
        a = _np.ascontiguousarray(a)
        arrays[f"in_{name}"] = a
        d[name] = nc.dram_tensor(f"in_{name}", a.shape, mybir.dt.from_np(a.dtype), kind="ExternalInput").ap()
    out = nc.dram_tensor("out", (1, LAT, D), F32, kind="ExternalOutput").ap()
    build(nc, d, out)
    r = _run(nc, [arrays], core_ids=[0])
    return r.results[0]["out"]
```

```python
from contextlib import ExitStack, contextmanager

import concourse.bass as bass
from concourse import mybir

F32 = mybir.dt.float32
F32R = mybir.dt.float32r
U32 = mybir.dt.uint32
ALU = mybir.AluOpType
ACT = mybir.ActivationFunctionType
AX = mybir.AxisListType

P = 128
D = 1024
KD = D // P
CTX = 256
LAT = 256
TOK = CTX + LAT
NB = TOK // P
LAYERS = 2
EPS = 1e-6
BANK = 512
BANKS = 8

MLA_Q, MLA_KV, MLA_PE, MLA_NOPE, MLA_V, MLA_H = 256, 128, 32, 64, 64, 4
MLA_QK = MLA_NOPE + MLA_PE
GQA_Q, GQA_KV, HD = 4, 2, 64
ML_H = 4
ML_W = ML_H * HD
HY_W = 256
O_GQA = MLA_Q + MLA_KV + MLA_PE
O_ML = O_GQA + (GQA_Q + 2 * GQA_KV) * HD
O_HY = O_ML + 4 * ML_W + 4 * ML_H
O_GATE = O_HY + 3 * HY_W
N_BRANCH = 4

PH, NK, TOPK = 8, 128, 16
HC = 2 * PH

V_ADAB, V_N1, V_N2, V_CONV, V_HYB = 0, 48, 56, 64, 82
V_MQ, V_MKV, V_MLN, V_QKQ, V_QKK, V_GQ, V_GK = 86, 88, 89, 91, 92, 93, 94
V_B1, V_B2, V_FREQ, V_ROWS = 95, 96, 97, 99

(C_ID, C_ONES, C_BONES, C_TRI_F, C_TRI_B, C_STR_F, C_STR_B, C_NEG_F, C_NEG_B, C_ROT_M, C_ROT_G, C_IOTA,
 C_N) = range(13)


NUMBER = [0, 0]


@contextmanager
def stage(nc, *names):
    NUMBER[0] += 1
    sems = [nc.alloc_semaphore(f"{n}_{NUMBER[0]}") for n in names]
    with nc.Block() as block:
        yield (block, *sems)
    nc.clear_and_free_semaphores(sems)
    nc.all_engine_barrier()


def sbuf(nc, name, shape, dtype):
    NUMBER[1] += 1
    return nc.sbuf_tensor(f"{name}_{NUMBER[1]}", shape, dtype)


class Chain:

    def __init__(self, eng, sem):
        self.eng, self.sem, self.n = eng, sem, 0

    def step(self, ins):
        self.n += 1
        ins.then_inc(self.sem, 1)

    def meet(self):
        self.eng.wait_ge(self.sem, self.n)

    def link(self, ins):
        self.step(ins)
        self.meet()


def split_matmul(nc, out, left, right, first, last):
    nc.tensor.matmul(out, left(0), right(0), start=first, stop=False)
    nc.tensor.matmul(out, left(0), right(1), start=False, stop=False)
    return nc.tensor.matmul(out, left(1), right(0), start=False, stop=last)


class Mem:
    pass




def setup(nc, m, d):
    with ExitStack() as ctx:
        tok = ctx.enter_context(sbuf(nc, "tok", [P, NB, D], F32))
        crow = ctx.enter_context(sbuf(nc, "crow", [2 * KD, P], F32))
        craw = ctx.enter_context(sbuf(nc, "craw", [P, 2 * KD], F32))
        cexp = ctx.enter_context(sbuf(nc, "cexp", [P, 2 * KD], F32))
        (block, consts_in, tok_in, c_in, tok_turned, c_turned, resid_by_act, c_exp, c_copied, dve_own, act_own) = (
            ctx.enter_context(stage(nc, "consts_in", "tok_in", "c_in", "tok_turned", "c_turned", "resid_by_act",
                                    "c_exp", "c_copied", "dve_own", "act_own")))

        @block.sync
        def _(sp):
            sp.dma_start(m.sq[:, :, :], d["k_square"].rearrange("(c p) n -> p c n", p=P)).then_inc(consts_in, 16)
            sp.dma_start(tok[:, 0:2, :], d["ctx"][0].rearrange("(b p) n -> p b n", p=P)).then_inc(tok_in, 16)
            sp.dma_start(tok[:, 2:4, :], d["x"][0].rearrange("(b p) n -> p b n", p=P)).then_inc(tok_in, 16)
            sp.dma_start(crow[0:KD, :], d["c"].rearrange("o (k p) -> (o k) p", p=P)).then_inc(c_in, 16)
            sp.dma_start(crow[KD:, :], d["c_ctx"].rearrange("(k p) -> k p", p=P)).then_inc(c_in, 16)

        @block.tensor
        def _(pe):
            pe.wait_ge(consts_in, 16)
            pe.wait_ge(c_in, 32)
            nc.tensor.transpose(m.ps[:, 7, 0:2 * KD], crow[:, :], m.sq[0:2 * KD, C_ID, 0:2 * KD]).then_inc(c_turned, 1)
            pe.wait_ge(tok_in, 32)
            for k in range(KD):
                if k >= 4:
                    pe.wait_ge(resid_by_act, k - 3)
                for b in range(NB):
                    ins = nc.tensor.transpose(m.ps[:, k % 4, b * P:(b + 1) * P], tok[:, b, k * P:(k + 1) * P],
                                              m.sq[:, C_ID, :])
                ins.then_inc(tok_turned, 1)

        @block.scalar
        def _(act):
            act.wait_ge(c_turned, 1)
            act.wait_ge(c_copied, 1)
            nc.scalar.activation(cexp[:, :], craw[:, :], ACT.Exp, scale=-1.0).then_inc(c_exp, 1)
            for k in range(KD):
                act.wait_ge(tok_turned, k + 1)
                nc.scalar.copy(m.resid[:, k, :], m.ps[:, k % 4, :]).then_inc(resid_by_act, 1)

        @block.vector
        def _(dve):
            own = Chain(dve, dve_own)
            dve.wait_ge(c_turned, 1)
            nc.vector.tensor_copy(craw[:, :], m.ps[:, 7, 0:2 * KD]).then_inc(c_copied, 1)
            dve.wait_ge(c_copied, 1)
            dve.wait_ge(c_exp, 1)
            own.link(nc.vector.tensor_scalar(cexp[:, :], cexp[:, :], 1.0, None, ALU.add))
            own.link(nc.vector.reciprocal(cexp[:, :], cexp[:, :]))
            own.link(nc.vector.tensor_tensor(m.cond[:, :, :].rearrange("p k r -> p r k"),
                                             craw[:, :].rearrange("p (r k) -> p r k", r=2),
                                             cexp[:, :].rearrange("p (r k) -> p r k", r=2), ALU.mult))




def modulation(nc, m, d, l):
    CH = 512
    NCH = 6 * D // CH
    RING = 3
    with ExitStack() as ctx:
        vrow = ctx.enter_context(sbuf(nc, "vrow", [P, P], F32))
        wada = ctx.enter_context(sbuf(nc, "wada", [P, RING, KD, CH], F32))
        mrow = ctx.enter_context(sbuf(nc, "mrow", [2, 6 * D], F32))
        (block, zeroed, vecs_in, chunk_mult, row_out, vecs_turned, mods_turned, dve_own, *w_ins) = (
            ctx.enter_context(stage(nc, "zeroed", "vecs_in", "chunk_mult", "row_out", "vecs_turned",
                                    "mods_turned", "dve_own", *[f"w_in{r}" for r in range(RING)])))

        vecs = [
            (V_ADAB, 48, P, d["ada_b"][l].rearrange("(k p) -> k p", p=P), 0),
            (V_N1, 8, P, d["norm1"][l].rearrange("(k p) -> k p", p=P), 0),
            (V_N2, 8, P, d["norm2"][l].rearrange("(k p) -> k p", p=P), 0),
            (V_CONV, 18, P, d["hy_conv"][l].rearrange("j (k p) -> (j k) p", p=P), 0),
            (V_HYB, 4, P, d["hy_bias"][l].rearrange("j (k p) -> (j k) p", p=P), 0),
            (V_MQ, 2, P, d["mla_q_norm"][l].rearrange("(k p) -> k p", p=P), 0),
            (V_MKV, 1, P, d["mla_kv_norm"][l].rearrange("(k p) -> k p", p=P), 0),
            (V_MLN, 2, P, d["ml_norm"][l].rearrange("(a b) e -> a (b e)", b=2), 0),
            (V_QKQ, 1, MLA_QK, d["mla_qk_norm_q"][l:l + 1, :], 0),
            (V_QKK, 1, MLA_QK, d["mla_qk_norm_k"][l:l + 1, :], 0),
            (V_GQ, 1, HD, d["gqa_qk_norm_q"][l:l + 1, :], 0),
            (V_GQ, 1, HD, d["gqa_qk_norm_q"][l:l + 1, :], HD),
            (V_GK, 1, HD, d["gqa_qk_norm_k"][l:l + 1, :], 0),
            (V_GK, 1, HD, d["gqa_qk_norm_k"][l:l + 1, :], HD),
            (V_B1, 1, HD, d["hy_b1"][l:l + 1, :], 0),
            (V_B2, 1, HD, d["hy_b2"][l:l + 1, :], 0),
            (V_FREQ, 2, HD, d["hy_freq"][l], 0),
        ]

        @block.sync
        def _(sp):
            for c in range(NCH):
                if c >= RING:
                    sp.wait_ge(chunk_mult, c - RING + 1)
                sp.dma_start(wada[:, c % RING, :, :],
                             d["ada_w"][l].rearrange("(k p) n -> p k n", p=P)[:, :, c * CH:(c + 1) * CH]
                             ).then_inc(w_ins[c % RING], 16)

        @block.scalar
        def _(act):
            act.wait_ge(zeroed, 1)
            for at, n, w, src, c0 in vecs:
                act.dma_start(vrow[at:at + n, c0:c0 + w], src).then_inc(vecs_in, 16)
            for c in range(NCH):
                act.wait_ge(chunk_mult, c + 1)
                nc.scalar.copy(mrow[:, c * CH:(c + 1) * CH], m.ps[0:2, c % 2, :]).then_inc(row_out, 1)

        @block.tensor
        def _(pe):
            pe.wait_ge(vecs_in, 16 * len(vecs))
            nc.tensor.transpose(m.ps[:, 6, 0:P], vrow[:, :], m.sq[:, C_ID, :]).then_inc(vecs_turned, 1)

            def turn(c):
                pe.wait_ge(row_out, c + 1)
                for q in range(CH // P):
                    j = c * (CH // P) + q
                    ins = nc.tensor.transpose(m.ps[:, 7, 2 * j:2 * j + 2], mrow[:, j * P:(j + 1) * P],
                                              m.sq[0:2, C_ID, 0:2])
                ins.then_inc(mods_turned, 1)

            for c in range(NCH):
                pe.wait_ge(w_ins[c % RING], 16 * (c // RING + 1))
                if c >= 2:
                    pe.wait_ge(row_out, c - 1)
                for k in range(KD):
                    ins = nc.tensor.matmul(m.ps[0:2, c % 2, :], m.cond[:, k, :], wada[:, c % RING, k, :],
                                           start=(k == 0), stop=(k == KD - 1))
                ins.then_inc(chunk_mult, 1)
                if c >= 1:
                    turn(c - 1)
            turn(NCH - 1)

        @block.vector
        def _(dve):
            own = Chain(dve, dve_own)
            nc.vector.memset(vrow[:, :], 0.0).then_inc(zeroed, 1)
            dve.wait_ge(vecs_turned, 1)
            own.link(nc.vector.tensor_copy(m.vec[:, :], m.ps[:, 6, 0:V_ROWS]))
            dve.wait_ge(mods_turned, NCH)
            own.link(nc.vector.tensor_tensor(
                m.mod[:, :, :], m.ps[:, 7, 0:12 * KD].rearrange("p (j r) -> p j r", r=2),
                m.vec[:, V_ADAB:V_ADAB + 6 * KD].unsqueeze(2).to_broadcast([P, 6 * KD, 2]), ALU.add))
            for v, at in ((V_N1, KD), (V_N2, 4 * KD)):
                own.link(nc.vector.tensor_scalar(m.mod[:, at:at + KD, :], m.mod[:, at:at + KD, :], 1.0, None, ALU.add))
                own.link(nc.vector.tensor_tensor(m.mod[:, at:at + KD, :], m.mod[:, at:at + KD, :],
                                                 m.vec[:, v:v + KD].unsqueeze(2).to_broadcast([P, KD, 2]), ALU.mult))


def mod_norm(nc, m, hs, at, t0):
    T = TOK - t0
    halves = [(kind, lo, hi) for kind, lo, hi in ((1, 0, CTX), (0, CTX, TOK)) if lo >= t0]
    with ExitStack() as ctx:
        sq = ctx.enter_context(sbuf(nc, "sq", [P, 3, TOK], F32))
        rs = ctx.enter_context(sbuf(nc, "rs", [P, TOK], F32))
        xn = ctx.enter_context(sbuf(nc, "xn", [P, TOK], F32))
        h = ctx.enter_context(sbuf(nc, "h", [P, 2, TOK], F32))
        (block, squared, summed, scaled, rooted, normed, rounded, rested, dve_own) = ctx.enter_context(
            stage(nc, "squared", "summed", "scaled", "rooted", "normed", "rounded", "rested", "dve_own"))

        @block.scalar
        def _(act):
            for k in range(KD):
                if k >= 3:
                    act.wait_ge(summed, k - 2)
                nc.scalar.activation(sq[:, k % 3, t0:], m.resid[:, k, t0:], ACT.Square).then_inc(squared, 1)
            act.wait_ge(scaled, 1)
            nc.scalar.activation(rs[:, t0:], rs[:, t0:], ACT.Sqrt).then_inc(rooted, 1)
            for k in range(KD):
                act.wait_ge(normed, k + 1)
                nc.scalar.copy(hs[:, 0, k, t0:], h[:, k % 2, t0:]).then_inc(rounded, 1)

        @block.tensor
        def _(pe):
            for k in range(KD):
                pe.wait_ge(squared, k + 1)
                nc.tensor.matmul(m.ps[:, 0, 0:T], m.sq[:, C_ONES, :], sq[:, k % 3, t0:], start=(k == 0),
                                 stop=(k == KD - 1)).then_inc(summed, 1)

        @block.vector
        def _(dve):
            own = Chain(dve, dve_own)

            def rest(k):
                dve.wait_ge(rounded, k + 1)
                nc.vector.tensor_tensor(hs[:, 1, k, t0:], h[:, k % 2, t0:], hs[:, 0, k, t0:].bitcast(F32),
                                        ALU.subtract).then_inc(rested, 1)

            dve.wait_ge(summed, KD)
            nc.vector.tensor_scalar(rs[:, t0:], m.ps[:, 0, 0:T], 1.0 / D, EPS, ALU.mult, ALU.add).then_inc(scaled, 1)
            dve.wait_ge(rooted, 1)
            own.link(nc.vector.reciprocal(rs[:, t0:], rs[:, t0:]))
            for k in range(KD):
                if k >= 1:
                    dve.wait_ge(normed, k)
                own.link(nc.vector.tensor_tensor(xn[:, t0:], m.resid[:, k, t0:], rs[:, t0:], ALU.mult))
                if k >= 2:
                    dve.wait_ge(rested, k - 1)
                for kind, lo, hi in halves:
                    ins = nc.vector.tensor_scalar(h[:, k % 2, lo:hi], xn[:, lo:hi],
                                                  m.mod[:, at + KD + k, kind:kind + 1],
                                                  m.mod[:, at + k, kind:kind + 1], ALU.mult, ALU.add)
                ins.then_inc(normed, 1)
                if k >= 1:
                    rest(k - 1)
            rest(KD - 1)




def input_projection(nc, m, d, hs, t, l, q0):
    wide = lambda dst: [(dst, slice(0, P))]
    chunks = [
        (0, 256, [(P * g, wide(t.cq[:, g, :]), q0) for g in range(2)], []),
        (256, 256, [
            (256, wide(t.ckv[:, :]), 0),
            (384, [(t.kpe[64:96, :], slice(0, MLA_PE))], 0)], []),
        (O_GQA, 256, [
            (O_GQA, [(t.gq[0:64, 0, :], slice(0, 64)), (t.gq[0:64, 1, :], slice(64, P))], q0),
            (O_GQA + P, [(t.gq[64:128, 0, :], slice(0, 64)), (t.gq[64:128, 1, :], slice(64, P))], q0)], []),
        (O_GQA + 256, 256, [(O_GQA + 256, wide(t.gk[:, :]), 0)], [(O_GQA + 384, P, t.gv[:, :, :], False)]),
        (O_ML, 256, [(O_ML + P * g, wide(t.mq[:, g, :]), q0) for g in range(2)], []),
        (O_ML + 256, 256, [(O_ML + 256 + P * g, wide(t.mk[:, g, :]), 0) for g in range(2)], []),
        (O_ML + 512, 256, [], [(O_ML + 512, ML_W, t.mvo[:, :, 0:ML_W], False)]),
        (O_ML + 768, 272, [], [
            (O_ML + 768, ML_W, t.mvo[:, :, ML_W:], False),
            (O_ML + 1024, 16, t.mg[:, :, :], True)]),
    ] + [(O_HY + 256 * c, 256, [(O_HY + P * g, wide(t.hy[:, g, :]), q0) for g in (2 * c, 2 * c + 1)], [])
         for c in range(3)]
    CW = 272
    groups = []
    for c, (_, _, fm, tm) in enumerate(chunks):
        groups += [(c, "fm", g, None) for g in fm]
        groups += [(c, "tm", g, b) for b in range(NB) for g in tm]
    last_of = {c: max(i for i, g in enumerate(groups) if g[0] == c) + 1 for c in range(len(chunks))}
    with ExitStack() as ctx:
        raw = ctx.enter_context(sbuf(nc, "w_raw", [P, 2, KD, CW], F32))
        w = [ctx.enter_context(sbuf(nc, f"w_split{r}", [P, 2, KD, CW], F32R)) for r in range(2)]
        gbias = ctx.enter_context(sbuf(nc, "gbias", [1, 16], F32))
        (block, bias_in, group_mult, act_out, dve_out, w_rounded, w_rested, w_in0, w_in1) = ctx.enter_context(
            stage(nc, "bias_in", "group_mult", "act_out", "dve_out", "w_rounded", "w_rested", "w_in0", "w_in1"))
        w_ins = (w_in0, w_in1)

        @block.sync
        def _(sp):
            sp.dma_start(gbias[:, :], d["ml_gate_b"][l:l + 1].rearrange("o a h -> o (a h)")).then_inc(bias_in, 16)
            for c, (c0, n, _, _) in enumerate(chunks):
                if c >= 2:
                    sp.wait_ge(w_rested, c - 1)
                sp.dma_start(raw[:, c % 2, :, 0:n], d["w_in"][l].rearrange("(k p) n -> p k n", p=P)[:, :, c0:c0 + n]
                             ).then_inc(w_ins[c % 2], 16)

        @block.gpsimd
        def _(pool):
            for c, (_, n, _, _) in enumerate(chunks):
                pool.wait_ge(w_rounded, c + 1)
                nc.gpsimd.tensor_tensor(w[c % 2][:, 1, :, 0:n], raw[:, c % 2, :, 0:n],
                                        w[c % 2][:, 0, :, 0:n].bitcast(F32), ALU.subtract).then_inc(w_rested, 1)

        @block.tensor
        def _(pe):
            pe.wait_ge(bias_in, 16)
            seen = 0
            for i, (c, kind, grp, b) in enumerate(groups):
                while seen <= c:
                    pe.wait_ge(w_rested, seen + 1)
                    seen += 1
                if i >= BANKS:
                    pe.wait_ge(dve_out if i % 2 else act_out, (i - BANKS) // 2 + 1)
                at = grp[0] - chunks[c][0]
                if kind == "fm":
                    t0 = grp[2]
                    out = m.ps[:, i % BANKS, 0:TOK - t0]
                    for k in range(KD):
                        ins = split_matmul(nc, out, lambda r: w[c % 2][:, r, k, at:at + P],
                                           lambda r: hs[:, r, k, t0:], k == 0, k == KD - 1)
                else:
                    _, n, _, biased = grp
                    out = m.ps[:, i % BANKS, 0:n]
                    for k in range(KD):
                        ins = split_matmul(nc, out, lambda r: hs[:, r, k, b * P:(b + 1) * P],
                                           lambda r: w[c % 2][:, r, k, at:at + n], k == 0,
                                           k == KD - 1 and not biased)
                    if biased:
                        ins = nc.tensor.matmul(out, m.sq[0:1, C_ONES, :], gbias[:, :], start=False, stop=True)
                ins.then_inc(group_mult, 1)

        def out_of(i):
            _, kind, grp, b = groups[i]
            if kind == "tm":
                return [(grp[2][:, b, :], m.ps[:, i % BANKS, 0:grp[1]])]
            _, dsts, t0 = grp
            return [(x[:, t0:], m.ps[rows, i % BANKS, 0:TOK - t0]) for x, rows in dsts]

        @block.scalar
        def _(act):
            def round_chunk(c):
                act.wait_ge(w_ins[c % 2], 16 * (c // 2 + 1))
                if c >= 2:
                    act.wait_ge(group_mult, last_of[c - 2])
                nc.scalar.copy(w[c % 2][:, 0, :, 0:chunks[c][1]], raw[:, c % 2, :, 0:chunks[c][1]]).then_inc(w_rounded, 1)

            round_chunk(0)
            round_chunk(1)
            nxt = 2
            for i in range(0, len(groups), 2):
                act.wait_ge(group_mult, i + 1)
                for dst, src in out_of(i):
                    ins = nc.scalar.copy(dst, src)
                ins.then_inc(act_out, 1)
                while nxt < len(chunks) and last_of[nxt - 2] <= i + 2:
                    round_chunk(nxt)
                    nxt += 1

        @block.vector
        def _(dve):
            for i in range(1, len(groups), 2):
                dve.wait_ge(group_mult, i + 1)
                for dst, src in out_of(i):
                    ins = nc.vector.tensor_copy(dst, src)
                ins.then_inc(dve_out, 1)




def attention_heads(nc, m, d, t, l, q0):
    with ExitStack() as ctx:
        wuq = ctx.enter_context(sbuf(nc, "wuq", [P, 2, MLA_H * MLA_QK], F32))
        wukv = ctx.enter_context(sbuf(nc, "wukv", [P, MLA_H * (MLA_NOPE + MLA_V)], F32))
        rope = ctx.enter_context(sbuf(nc, "rope", [P, 4, TOK], F32))
        lat = ctx.enter_context(sbuf(nc, "lat", [P, 3, TOK], F32))
        sq = ctx.enter_context(sbuf(nc, "sq", [P, 3, TOK], F32))
        rs = ctx.enter_context(sbuf(nc, "rs", [P, 3, TOK], F32))
        xn = ctx.enter_context(sbuf(nc, "xn", [P, 2, TOK], F32))
        xc = ctx.enter_context(sbuf(nc, "xc", [P, TOK], F32))
        (block, w_in, lat_sq, lat_sum, lat_scaled, lat_root, lat_done, up_mult, up_out, v_out, x_sq, x_sum,
         x_scaled, x_root, x_normed, x_rot, x_done, dve_own) = ctx.enter_context(stage(
            nc, "w_in", "lat_sq", "lat_sum", "lat_scaled", "lat_root", "lat_done", "up_mult", "up_out", "v_out",
            "x_sq", "x_sum", "x_scaled", "x_root", "x_normed", "x_rot", "x_done", "dve_own"))
        lats = [(t.cq[:, 0, :], V_MQ, q0), (t.cq[:, 1, :], V_MQ + 1, q0), (t.ckv[:, :], V_MKV, 0)]
        tiles = ([(t.qm[0:MLA_QK, h, :], MLA_QK, V_QKQ, q0, 0, C_ROT_M) for h in range(MLA_H)]
                 + [(t.km[0:MLA_QK, h, :], MLA_QK, V_QKK, 0, 0, C_ROT_M) for h in range(MLA_H)]
                 + [(t.gq[:, a, :], P, V_GQ, q0, 2, C_ROT_G) for a in range(2)]
                 + [(t.gk[:, :], P, V_GK, 0, 2, C_ROT_G)])

        @block.sync
        def _(sp):
            sp.dma_start(wuq[:, :, :], d["mla_w_uq"][l].rearrange("(k p) n -> p k n", p=P)).then_inc(w_in, 16)
            sp.dma_start(wukv[:, :], d["mla_w_ukv"][l]).then_inc(w_in, 16)
            sp.dma_start(rope[:, :, :], d["k_rope"].rearrange("(c p) n -> p c n", p=P)).then_inc(w_in, 16)

        @block.scalar
        def _(act):
            for i, (x, _, t0) in enumerate(lats):
                nc.scalar.activation(sq[:, i, t0:], x[:, t0:], ACT.Square).then_inc(lat_sq, 1)
            for i, t0 in ((0, q0), (1, 0)):
                act.wait_ge(lat_scaled, i + 1)
                nc.scalar.activation(rs[:, i, t0:], rs[:, i, t0:], ACT.Sqrt).then_inc(lat_root, 1)
            for h in range(MLA_H):
                nc.scalar.copy(t.km[64:96, h, :], t.kpe[64:96, :])
            for h in range(MLA_H):
                act.wait_ge(up_mult, 2 * h + 1)
                nc.scalar.copy(t.qm[0:MLA_QK, h, q0:], m.ps[0:MLA_QK, 2 + 2 * (h % 2), q0 - q0:TOK - q0])
                act.wait_ge(up_mult, 2 * h + 2)
                nc.scalar.copy(t.km[0:MLA_NOPE, h, :], m.ps[0:MLA_NOPE, 3 + 2 * (h % 2), :]).then_inc(up_out, 1)
            act.wait_ge(up_out, MLA_H)
            act.wait_ge(lat_sum, 3)
            for i, (x, rows, _, t0, _, _) in enumerate(tiles):
                if i >= 3:
                    act.wait_ge(x_sum, i - 2)
                nc.scalar.activation(sq[0:rows, i % 3, t0:], x[:, t0:], ACT.Square).then_inc(x_sq, 1)
                act.wait_ge(x_scaled, i + 1)
                nc.scalar.activation(rs[0:rows, i % 3, t0:], rs[0:rows, i % 3, t0:], ACT.Sqrt).then_inc(x_root, 1)

        @block.tensor
        def _(pe):
            pe.wait_ge(w_in, 48)
            pe.wait_ge(lat_sq, 2)
            for i in range(2):
                nc.tensor.matmul(m.ps[:, 0, 0:TOK - q0], m.sq[:, C_ONES, :], sq[:, i, q0:], start=(i == 0),
                                 stop=(i == 1)).then_inc(lat_sum, 1)
            pe.wait_ge(lat_sq, 3)
            nc.tensor.matmul(m.ps[:, 1, :], m.sq[:, C_ONES, :], sq[:, 2, :], start=True, stop=True).then_inc(lat_sum, 1)
            pe.wait_ge(lat_done, 3)
            W = MLA_NOPE + MLA_V
            for h in range(MLA_H):
                if h >= 2:
                    pe.wait_ge(up_out, h - 1)
                for k in range(2):
                    ins = nc.tensor.matmul(m.ps[0:MLA_QK, 2 + 2 * (h % 2), 0:TOK - q0],
                                           wuq[:, k, h * MLA_QK:(h + 1) * MLA_QK], lat[:, k, q0:], start=(k == 0),
                                           stop=(k == 1))
                ins.then_inc(up_mult, 1)
                nc.tensor.matmul(m.ps[0:MLA_NOPE, 3 + 2 * (h % 2), :], wukv[:, h * W:h * W + MLA_NOPE],
                                 lat[:, 2, :], start=True, stop=True).then_inc(up_mult, 1)
            vcols = wukv[:, :].rearrange("p (h c) -> p h c", h=MLA_H)[:, :, MLA_NOPE:]
            for b in range(NB):
                if b >= 2:
                    pe.wait_ge(v_out, b - 1)
                nc.tensor.matmul(m.ps[:, 6 + b % 2, 0:MLA_H * MLA_V], lat[:, 2, b * P:(b + 1) * P], vcols,
                                 start=True, stop=True).then_inc(up_mult, 1)

            def rotate(i):
                x, rows, _, t0, _, rot = tiles[i]
                pe.wait_ge(x_normed, i + 1)
                nc.tensor.matmul(m.ps[0:rows, 2 + i % 2, 0:TOK - t0], m.sq[0:rows, rot, 0:rows], xn[0:rows, i % 2, t0:],
                                 start=True, stop=True).then_inc(x_rot, 1)

            for i, (x, rows, _, t0, _, rot) in enumerate(tiles):
                pe.wait_ge(x_sq, i + 1)
                if i >= 2:
                    pe.wait_ge(x_scaled, i - 1)
                ones = m.sq[0:rows, C_BONES if rows == P else C_ONES, 0:rows]
                nc.tensor.matmul(m.ps[0:rows, i % 2, 0:TOK - t0], ones, sq[0:rows, i % 3, t0:], start=True,
                                 stop=True).then_inc(x_sum, 1)
                if i >= 1:
                    rotate(i - 1)
            rotate(len(tiles) - 1)

        @block.vector
        def _(dve):
            own = Chain(dve, dve_own)
            for i, (n, t0, width) in enumerate(((2, q0, MLA_Q), (3, 0, MLA_KV))):
                dve.wait_ge(lat_sum, n)
                nc.vector.tensor_scalar(rs[:, i, t0:], m.ps[:, i, 0:TOK - t0], 1.0 / width, EPS, ALU.mult,
                                        ALU.add).then_inc(lat_scaled, 1)
            for i, t0 in ((0, q0), (1, 0)):
                dve.wait_ge(lat_root, i + 1)
                own.link(nc.vector.reciprocal(rs[:, i, t0:], rs[:, i, t0:]))
            for i, (x, v, t0) in enumerate(lats):
                nc.vector.scalar_tensor_tensor(out=lat[:, i, t0:], in0=x[:, t0:], scalar=m.vec[:, v:v + 1],
                                               in1=rs[:, i // 2, t0:], op0=ALU.mult, op1=ALU.mult
                                               ).then_inc(lat_done, 1)
            for b in range(NB):
                dve.wait_ge(up_mult, 2 * MLA_H + b + 1)
                nc.vector.tensor_copy(t.vm[:, b, :], m.ps[:, 6 + b % 2, 0:MLA_H * MLA_V]).then_inc(v_out, 1)
            dve.wait_ge(lat_done, 3)

            def turn(i):
                x, rows, _, t0, table, _ = tiles[i]
                dve.wait_ge(x_rot, i + 1)
                own.link(nc.vector.tensor_tensor(xc[0:rows, t0:], m.ps[0:rows, 2 + i % 2, 0:TOK - t0],
                                                 rope[0:rows, table + 1, t0:], ALU.mult))
                own.link(nc.vector.tensor_tensor(x[:, t0:], xn[0:rows, i % 2, t0:], rope[0:rows, table, t0:], ALU.mult))
                own.link(nc.vector.tensor_tensor(x[:, t0:], x[:, t0:], xc[0:rows, t0:], ALU.add))

            for i, (x, rows, v, t0, table, _) in enumerate(tiles):
                n = MLA_QK if rows == MLA_QK else HD
                dve.wait_ge(x_sum, i + 1)
                nc.vector.tensor_scalar(rs[0:rows, i % 3, t0:], m.ps[0:rows, i % 2, 0:TOK - t0], 1.0 / n, EPS,
                                        ALU.mult, ALU.add).then_inc(x_scaled, 1)
                if i >= 1:
                    turn(i - 1)
                dve.wait_ge(x_root, i + 1)
                own.link(nc.vector.reciprocal(rs[0:rows, i % 3, t0:], rs[0:rows, i % 3, t0:]))
                nc.vector.scalar_tensor_tensor(out=xn[0:rows, i % 2, t0:], in0=x[:, t0:], scalar=m.vec[0:rows, v:v + 1],
                                               in1=rs[0:rows, i % 3, t0:], op0=ALU.mult, op1=ALU.mult
                                               ).then_inc(x_normed, 1)
            turn(len(tiles) - 1)




def attention(nc, m, t, blocks):
    SC = {0: MLA_QK ** -0.5, 1: HD ** -0.5}
    units = []
    for h in range(4):
        half = 64 * (h % 2)
        for b in blocks:
            qs = slice(b * P, (b + 1) * P)
            units.append((0, t.qm[0:MLA_QK, h, qs], lambda n, h=h: t.km[0:MLA_QK, h, 0:n],
                          lambda kb, h=h: t.vm[:, kb, h * HD:(h + 1) * HD], t.yT[half:half + 64, 0, h // 2, qs], b, half))
    for h in range(4):
        half, kv = 64 * (h % 2), h // 2
        for b in blocks:
            qs = slice(b * P, (b + 1) * P)
            units.append((1, t.gq[64 * kv:64 * kv + 64, h % 2, qs],
                          lambda n, kv=kv: t.gk[64 * kv:64 * kv + 64, 0:n],
                          lambda kb, kv=kv: t.gv[:, kb, kv * HD:(kv + 1) * HD],
                          t.yT[half:half + 64, 1, h // 2, qs], b, half))
    N = len(units)
    nkeys = lambda b: CTX if b < CTX // P else TOK
    with ExitStack() as ctx:
        pr = ctx.enter_context(sbuf(nc, "probs", [P, 2, TOK], F32))
        pt = ctx.enter_context(sbuf(nc, "probsT", [P, 2, TOK], F32))
        st = ctx.enter_context(sbuf(nc, "stat", [P, 3, N], F32))
        (block, scored, maxed, exped, normed, turned, turn_out, summed, y_out, dve_own) = ctx.enter_context(stage(
            nc, "scored", "maxed", "exped", "normed", "turned", "turn_out", "summed", "y_out", "dve_own"))

        @block.tensor
        def _(pe):
            def score(u):
                _, q, k, _, _, b, _ = units[u]
                if u >= 2:
                    pe.wait_ge(exped, u - 1)
                nc.tensor.matmul(m.ps[:, u % 2, 0:nkeys(b)], q, k(nkeys(b)), start=True, stop=True).then_inc(scored, 1)

            def turn(u):
                b = units[u][5]
                pe.wait_ge(normed, u + 1)
                if u >= 2:
                    pe.wait_ge(turn_out, u - 1)
                for kb in range(nkeys(b) // P):
                    ins = nc.tensor.transpose(m.ps[:, 2 + u % 2, kb * P:(kb + 1) * P], pr[:, u % 2, kb * P:(kb + 1) * P],
                                              m.sq[:, C_ID, :])
                ins.then_inc(turned, 1)

            def values(u):
                _, _, _, v, _, b, half = units[u]
                pe.wait_ge(turn_out, u + 1)
                if u >= 2:
                    pe.wait_ge(y_out, u - 1)
                n = nkeys(b) // P
                for kb in range(n):
                    ins = nc.tensor.matmul(m.ps[half:half + 64, 4 + u % 2, 0:P], v(kb), pt[:, u % 2, kb * P:(kb + 1) * P],
                                           start=(kb == 0), stop=(kb == n - 1))
                ins.then_inc(summed, 1)

            score(0)
            for u in range(N):
                if u + 1 < N:
                    score(u + 1)
                turn(u)
                if u >= 1:
                    values(u - 1)
            values(N - 1)

        @block.scalar
        def _(act):
            def y_copy(u):
                act.wait_ge(summed, u + 1)
                nc.scalar.copy(units[u][4], m.ps[units[u][6]:units[u][6] + 64, 4 + u % 2, 0:P]).then_inc(y_out, 1)

            def t_copy(u):
                n = nkeys(units[u][5])
                act.wait_ge(turned, u + 1)
                if u >= 2:
                    act.wait_ge(summed, u - 1)
                nc.scalar.copy(pt[:, u % 2, 0:n], m.ps[:, 2 + u % 2, 0:n]).then_inc(turn_out, 1)

            for u, (br, _, _, _, _, b, _) in enumerate(units):
                n = nkeys(b)
                act.wait_ge(maxed, u + 1)
                if u >= 2:
                    act.wait_ge(turned, u - 1)
                nc.scalar.activation(pr[:, u % 2, 0:n], m.ps[:, u % 2, 0:n], ACT.Exp, bias=st[:, 0, u:u + 1],
                                     scale=SC[br], accum_out=st[:, 1, u:u + 1]).then_inc(exped, 1)
                if u >= 1:
                    t_copy(u - 1)
                if u >= 2:
                    y_copy(u - 2)
            t_copy(N - 1)
            y_copy(N - 2)
            y_copy(N - 1)

        @block.vector
        def _(dve):
            own = Chain(dve, dve_own)

            def top(u):
                br, b = units[u][0], units[u][5]
                dve.wait_ge(scored, u + 1)
                own.link(nc.vector.reduce_max(st[:, 2, u:u + 1], m.ps[:, u % 2, 0:nkeys(b)], axis=AX.X))
                nc.vector.tensor_scalar(st[:, 0, u:u + 1], st[:, 2, u:u + 1], -SC[br], None, ALU.mult).then_inc(maxed, 1)

            top(0)
            for u, unit in enumerate(units):
                if u + 1 < N:
                    top(u + 1)
                n = nkeys(unit[5])
                dve.wait_ge(exped, u + 1)
                own.link(nc.vector.reciprocal(st[:, 1, u:u + 1], st[:, 1, u:u + 1]))
                nc.vector.tensor_scalar(pr[:, u % 2, 0:n], pr[:, u % 2, 0:n], st[:, 1, u:u + 1], None,
                                        ALU.mult).then_inc(normed, 1)



ORDER = {0: (0, 1, 2, 3), 1: (1, 0, 3, 2)}


def mlstm(nc, m, t, q_at):
    units = [(dr, h, p) for dr in range(2) for h in range(ML_H) for p in q_at]
    N = len(units)
    SCALE = HD ** -0.5
    with ExitStack() as ctx:
        lf = ctx.enter_context(sbuf(nc, "logf", [P, NB, 2 * ML_H], F32))
        af = ctx.enter_context(sbuf(nc, "absf", [P, NB, 2 * ML_H], F32))
        ft = ctx.enter_context(sbuf(nc, "ftot", [P, 2, NB, ML_H], F32))
        same = ctx.enter_context(sbuf(nc, "same", [P, 2, NB, P], F32))
        fb = ctx.enter_context(sbuf(nc, "fbcast", [P, 2, NB, P], F32))
        w = ctx.enter_context(sbuf(nc, "w", [P, 2, TOK], F32))
        a = ctx.enter_context(sbuf(nc, "a", [P, 2, TOK], F32))
        at = ctx.enter_context(sbuf(nc, "aT", [P, 2, TOK], F32))
        st = ctx.enter_context(sbuf(nc, "stat", [P, 6, N], F32))
        hh = ctx.enter_context(sbuf(nc, "h", [P, NB, ML_W], F32))
        h2 = ctx.enter_context(sbuf(nc, "h2", [P, NB, ML_W], F32))
        og = ctx.enter_context(sbuf(nc, "og", [P, NB, ML_W], F32))
        nr = ctx.enter_context(sbuf(nc, "nr", [P, NB, ML_H], F32))
        (block, f_abs, f_exp, f_exp1, f_ln, f_done, f_tot, tot_out, built, decayed, scored, maxed, exped, den_exp,
         weighed, turned, turn_out, summed, h_done, o_exp, n_scaled, n_root, y_done, y_turned, y_out, dve_own
         ) = ctx.enter_context(stage(
             nc, "f_abs", "f_exp", "f_exp1", "f_ln", "f_done", "f_tot", "tot_out", "built", "decayed", "scored",
             "maxed", "exped", "den_exp", "weighed", "turned", "turn_out", "summed", "h_done", "o_exp", "n_scaled",
             "n_root", "y_done", "y_turned", "y_out", "dve_own"))
        qb = sorted({ORDER[0][p] for p in q_at})
        b0, b1 = qb[0], qb[-1] + 1
        tri = (C_TRI_F, C_TRI_B)
        strict = (C_STR_F, C_STR_B)
        neg = (C_NEG_F, C_NEG_B)
        heads = [(dr, h) for dr in range(2) for h in range(ML_H)]

        @block.scalar
        def _(act):
            act.wait_ge(f_abs, 1)
            nc.scalar.activation(af[:, :, :], af[:, :, :], ACT.Exp, scale=-1.0).then_inc(f_exp, 1)
            act.wait_ge(f_exp1, 1)
            nc.scalar.activation(af[:, :, :], af[:, :, :], ACT.Ln).then_inc(f_ln, 1)
            nc.scalar.activation(og[:, b0:b1, :], t.mvo[:, b0:b1, ML_W:], ACT.Exp, scale=-1.0).then_inc(o_exp, 1)

            def t_copy(u):
                n = (units[u][2] + 1) * P
                act.wait_ge(turned, u + 1)
                if u >= 2:
                    act.wait_ge(summed, u - 1)
                nc.scalar.copy(at[:, u % 2, 0:n], m.ps[:, 4 + u % 2, 0:n]).then_inc(turn_out, 1)

            for u, (dr, h, p) in enumerate(units):
                n = (p + 1) * P
                act.wait_ge(maxed, u + 1)
                if u >= 2:
                    act.wait_ge(weighed, u - 1)
                nc.scalar.activation(w[:, u % 2, 0:n], m.ps[:, u % 2, 0:n], ACT.Exp, bias=st[:, 1, u:u + 1]
                                     ).then_inc(exped, 1)
                nc.scalar.activation(st[:, 2, u:u + 1], st[:, 1, u:u + 1], ACT.Exp).then_inc(den_exp, 1)
                if u >= 1:
                    t_copy(u - 1)
            t_copy(N - 1)
            act.wait_ge(n_scaled, 1)
            nc.scalar.activation(nr[:, b0:b1, :], nr[:, b0:b1, :], ACT.Sqrt).then_inc(n_root, 1)

        @block.tensor
        def _(pe):
            pe.wait_ge(f_done, 1)
            for dr in range(2):
                for p in range(NB):
                    blk = ORDER[dr]
                    for j in range(p + 1):
                        ins = nc.tensor.matmul(m.ps[:, 6, (dr * NB + p) * ML_H:(dr * NB + p + 1) * ML_H],
                                               m.sq[:, tri[dr] if j == p else C_ONES, :],
                                               lf[:, blk[j], dr * ML_H:(dr + 1) * ML_H], start=(j == 0), stop=(j == p))
            ins.then_inc(f_tot, 1)

            def decay(u):
                dr, h, p = units[u]
                blk, hd = ORDER[dr], heads.index((dr, h)) % 2
                pe.wait_ge(built, heads.index((dr, h)) + 1)
                if u >= 2:
                    pe.wait_ge(exped, u - 1)
                ones = m.sq[:, C_ONES, :]
                for j in range(p + 1):
                    out = m.ps[:, u % 2, j * P:(j + 1) * P]
                    if j == p:
                        nc.tensor.matmul(out, m.sq[:, tri[dr], :], same[:, hd, blk[p], :], start=True, stop=False)
                        ins = nc.tensor.matmul(out, m.sq[:, C_ID, :], m.sq[:, neg[dr], :], start=False, stop=True)
                        continue
                    nc.tensor.matmul(out, ones, same[:, hd, blk[j], :], start=True, stop=False)
                    for i in range(j + 1, p):
                        nc.tensor.matmul(out, ones, fb[:, hd, blk[i], :], start=False, stop=False)
                    nc.tensor.matmul(out, m.sq[:, tri[dr], :], fb[:, hd, blk[p], :], start=False, stop=True)
                ins.then_inc(decayed, 1)

            def score(u):
                dr, h, p = units[u]
                blk, half = ORDER[dr], 64 * (h % 2)
                if u >= 2:
                    pe.wait_ge(weighed, u - 1)
                for j in range(p + 1):
                    ins = nc.tensor.matmul(m.ps[:, 2 + u % 2, j * P:(j + 1) * P],
                                           t.mq[half:half + 64, h // 2, blk[p] * P:(blk[p] + 1) * P],
                                           t.mk[half:half + 64, h // 2, blk[j] * P:(blk[j] + 1) * P],
                                           start=True, stop=True)
                ins.then_inc(scored, 1)

            def turn(u):
                pe.wait_ge(weighed, u + 1)
                if u >= 2:
                    pe.wait_ge(turn_out, u - 1)
                for j in range(units[u][2] + 1):
                    ins = nc.tensor.transpose(m.ps[:, 4 + u % 2, j * P:(j + 1) * P], a[:, u % 2, j * P:(j + 1) * P],
                                              m.sq[:, C_ID, :])
                ins.then_inc(turned, 1)

            def values(u):
                dr, h, p = units[u]
                pe.wait_ge(turn_out, u + 1)
                if u == 0:
                    pe.wait_ge(tot_out, 1)
                if u >= 2:
                    pe.wait_ge(h_done, u - 1)
                for j in range(p + 1):
                    ins = nc.tensor.matmul(m.ps[:, 6 + u % 2, 0:HD], at[:, u % 2, j * P:(j + 1) * P],
                                           t.mvo[:, ORDER[dr][j], h * HD:(h + 1) * HD], start=(j == 0), stop=(j == p))
                ins.then_inc(summed, 1)

            decay(0)
            score(0)
            for u in range(N):
                if u + 1 < N:
                    decay(u + 1)
                    score(u + 1)
                turn(u)
                if u >= 1:
                    values(u - 1)
            values(N - 1)
            pe.wait_ge(y_done, 1)
            for i, b in enumerate(range(b0, b1)):
                if i >= 2:
                    pe.wait_ge(y_out, i - 1)
                for g in range(2):
                    ins = nc.tensor.transpose(m.ps[:, i % 2, g * P:(g + 1) * P], hh[:, b, g * P:(g + 1) * P],
                                              m.sq[:, C_ID, :])
                ins.then_inc(y_turned, 1)

        @block.vector
        def _(dve):
            own = Chain(dve, dve_own)
            nc.vector.scalar_tensor_tensor(out=af[:, :, :], in0=t.mg[:, :, 2 * ML_H:], scalar=-1.0,
                                           in1=t.mg[:, :, 2 * ML_H:], op0=ALU.mult, op1=ALU.max).then_inc(f_abs, 1)
            own.link(nc.vector.tensor_scalar(lf[:, :, :], t.mg[:, :, 2 * ML_H:], 0.0, None, ALU.min))
            dve.wait_ge(f_exp, 1)
            nc.vector.tensor_scalar(af[:, :, :], af[:, :, :], 1.0, None, ALU.add).then_inc(f_exp1, 1)
            dve.wait_ge(f_ln, 1)
            nc.vector.tensor_tensor(lf[:, :, :], lf[:, :, :], af[:, :, :], ALU.subtract).then_inc(f_done, 1)
            dve.wait_ge(f_done, 1)
            dve.wait_ge(f_tot, 1)
            nc.vector.tensor_copy(ft[:, :, :, :].rearrange("p a b c -> p (a b c)"),
                                  m.ps[:, 6, 0:2 * NB * ML_H]).then_inc(tot_out, 1)
            dve.wait_ge(tot_out, 1)

            def build(i):
                dr, h = heads[i]
                if i >= 2:
                    dve.wait_ge(decayed, (i - 1) * len(q_at))
                for b in range(NB):
                    own.step(nc.vector.tensor_scalar(same[:, i % 2, b, :], m.sq[:, C_ID, :],
                                                     t.mg[:, b, dr * ML_H + h:dr * ML_H + h + 1], None, ALU.mult))
                    own.step(nc.vector.tensor_scalar(fb[:, i % 2, b, :], m.sq[:, C_ONES, :],
                                                     lf[:, b, dr * ML_H + h:dr * ML_H + h + 1], None, ALU.mult))
                own.meet()
                for b in range(NB):
                    ins = nc.vector.scalar_tensor_tensor(
                        out=same[:, i % 2, b, :], in0=m.sq[:, strict[dr], :],
                        scalar=lf[:, b, dr * ML_H + h:dr * ML_H + h + 1], in1=same[:, i % 2, b, :],
                        op0=ALU.mult, op1=ALU.add)
                ins.then_inc(built, 1)

            def top(u):
                dr, h, p = units[u]
                dve.wait_ge(decayed, u + 1)
                own.link(nc.vector.reduce_max(st[:, 0, u:u + 1], m.ps[:, u % 2, 0:(p + 1) * P], axis=AX.X))
                nc.vector.tensor_scalar(st[:, 1, u:u + 1], st[:, 0, u:u + 1], ft[:, dr, p, h:h + 1], -1.0, ALU.max,
                                        ALU.mult).then_inc(maxed, 1)

            def output(u):
                dr, h, p = units[u]
                b = ORDER[dr][p]
                dve.wait_ge(den_exp, u + 1)
                own.link(nc.vector.scalar_tensor_tensor(out=st[:, 4, u:u + 1], in0=st[:, 3, u:u + 1], scalar=-1.0,
                                                        in1=st[:, 3, u:u + 1], op0=ALU.mult, op1=ALU.max))
                own.link(nc.vector.tensor_tensor(st[:, 4, u:u + 1], st[:, 4, u:u + 1], st[:, 2, u:u + 1], ALU.max))
                own.link(nc.vector.reciprocal(st[:, 5, u:u + 1], st[:, 4, u:u + 1]))
                dve.wait_ge(summed, u + 1)
                out, got = hh[:, b, h * HD:(h + 1) * HD], m.ps[:, 6 + u % 2, 0:HD]
                if dr == 0:
                    ins = nc.vector.tensor_scalar(out, got, st[:, 5, u:u + 1], None, ALU.mult)
                else:
                    ins = nc.vector.scalar_tensor_tensor(out=out, in0=got, scalar=st[:, 5, u:u + 1], in1=out,
                                                         op0=ALU.mult, op1=ALU.add)
                ins.then_inc(h_done, 1)

            build(0)
            build(1)
            top(0)
            for u, (dr, h, p) in enumerate(units):
                if u + 1 < N:
                    top(u + 1)
                i = u // len(q_at)
                if u % len(q_at) == len(q_at) - 1 and i + 2 < len(heads):
                    build(i + 2)
                n = (p + 1) * P
                dve.wait_ge(exped, u + 1)
                dve.wait_ge(scored, u + 1)
                if u >= 2:
                    dve.wait_ge(turned, u - 1)
                nc.vector.tensor_tensor_reduce(a[:, u % 2, 0:n], w[:, u % 2, 0:n], m.ps[:, 2 + u % 2, 0:n], SCALE, 0.0,
                                               ALU.mult, ALU.add, st[:, 3, u:u + 1]).then_inc(weighed, 1)
                dve.wait_ge(weighed, u + 1)
                if u >= 1:
                    output(u - 1)
            output(N - 1)
            dve.wait_ge(h_done, N)
            own.link(nc.vector.tensor_tensor(h2[:, b0:b1, :], hh[:, b0:b1, :], hh[:, b0:b1, :], ALU.mult))
            own.link(nc.vector.tensor_reduce(nr[:, b0:b1, :], h2[:, b0:b1, :].rearrange("p b (h e) -> p b h e", h=ML_H),
                                             axis=AX.X, op=ALU.add))
            nc.vector.tensor_scalar(nr[:, b0:b1, :], nr[:, b0:b1, :], 1.0 / HD, EPS, ALU.mult, ALU.add
                                    ).then_inc(n_scaled, 1)
            dve.wait_ge(o_exp, 1)
            own.link(nc.vector.tensor_scalar(og[:, b0:b1, :], og[:, b0:b1, :], 1.0, None, ALU.add))
            own.link(nc.vector.reciprocal(og[:, b0:b1, :], og[:, b0:b1, :]))
            own.link(nc.vector.tensor_tensor(hh[:, b0:b1, :], hh[:, b0:b1, :], og[:, b0:b1, :], ALU.mult))
            dve.wait_ge(n_root, 1)
            own.link(nc.vector.reciprocal(nr[:, b0:b1, :], nr[:, b0:b1, :]))
            for b in range(b0, b1):
                ins = nc.vector.tensor_tensor(
                    hh[:, b, :].rearrange("p (h e) -> p h e", h=ML_H), hh[:, b, :].rearrange("p (h e) -> p h e", h=ML_H),
                    nr[:, b, :].unsqueeze(2).to_broadcast([P, ML_H, HD]), ALU.mult)
                own.step(ins)
            own.meet()
            dve.sem_inc(y_done, 1)
            for i, b in enumerate(range(b0, b1)):
                dve.wait_ge(y_turned, i + 1)
                for g in range(2):
                    ins = nc.vector.tensor_scalar(t.yT[:, 2, g, b * P:(b + 1) * P], m.ps[:, i % 2, g * P:(g + 1) * P],
                                                  m.vec[:, V_MLN + g:V_MLN + g + 1], None, ALU.mult)
                ins.then_inc(y_out, 1)



SEQ = 256
KF = SEQ // P
TWO_PI_HI = 6.28125
TWO_PI_LO = 6.283185307179586 - 6.28125
ROUND = 1.5 * 2.0 ** 23
PI = 3.1415925


def hyena(nc, m, d, t, l, streams):
    S = len(streams)
    s0, C2 = streams[0], 2 * HY_W
    with ExitStack() as ctx:
        sb = lambda name, shape: ctx.enter_context(sbuf(nc, name, shape, F32))
        dft = sb("dft", [P, 4, KF, SEQ])
        dec = sb("decay", [P, KF, HY_W])
        feat = sb("feat", [33, SEQ])
        w1, w2, w3 = sb("w1", [33, 64]), sb("w2", [64, 64]), sb("w3", [64, 2 * C2])
        hid, arg, rnd = sb("hid", [64, SEQ]), sb("arg", [64, SEQ]), sb("rnd", [64, SEQ])
        filt = sb("filt", [P, KF, 2, 2, HY_W])
        fsq = sb("fsq", [P, KF, 2 * C2])
        frs = sb("frs", [P, C2])
        comb = sb("comb", [P, 2, KF, C2])
        spec = sb("spec", [P, 2, KF, C2])
        cv = sb("cv", [P, 6, TOK])
        z = sb("z", [P, KF, 2, HY_W])
        zf = sb("zf", [P, 2, KF, S * HY_W])
        yf = sb("yf", [P, 2, KF, S * HY_W])
        tmp = sb("tmp", [P, KF, S * HY_W])
        zt = sb("zt", [P, 2, TOK])
        (block, k_in, h_mult, arg_done, sine_done, f_mult, f_out, f_sq, f_sum, f_scaled, f_root, comb_done, s_mult,
         s_out, conv_done, z_turned, z_out, z_mult, zf_out, yf_done, y_mult, y_out, dve_own) = ctx.enter_context(stage(
             nc, "k_in", "h_mult", "arg_done", "sine_done", "f_mult", "f_out", "f_sq", "f_sum", "f_scaled", "f_root",
             "comb_done", "s_mult", "s_out", "conv_done", "z_turned", "z_out", "z_mult", "zf_out", "yf_done",
             "y_mult", "y_out", "dve_own"))

        @block.sync
        def _(sp):
            sp.dma_start(feat[:, :], d["k_feat"]).then_inc(k_in, 16)
            sp.dma_start(w1[:, :], d["hy_w1"][l]).then_inc(k_in, 16)
            sp.dma_start(w2[:, :], d["hy_w2"][l]).then_inc(k_in, 16)
            sp.dma_start(w3[:, :], d["hy_w3"][l]).then_inc(k_in, 16)
            sp.dma_start(dec[:, :, :], d["k_decay"].rearrange("(a p) n -> p a n", p=P)).then_inc(k_in, 16)
            sp.dma_start(dft[:, :, :, :], d["k_dft"].rearrange("c (a p) n -> p c a n", p=P)).then_inc(k_in, 16)

        @block.tensor
        def _(pe):
            pe.wait_ge(k_in, 96)
            nc.tensor.matmul(m.ps[0:64, 0, 0:SEQ], w1[:, :], feat[:, :], start=True, stop=True).then_inc(h_mult, 1)
            pe.wait_ge(sine_done, 1)
            nc.tensor.matmul(m.ps[0:64, 1, 0:SEQ], w2[:, :], hid[:, :], start=True, stop=True).then_inc(h_mult, 1)
            pe.wait_ge(sine_done, 2)
            for a in range(KF):
                for o in range(2):
                    nc.tensor.matmul(m.ps[:, 2 + 2 * a + o, :], hid[:, a * P:(a + 1) * P], w3[:, o * C2:(o + 1) * C2],
                                     start=True, stop=True).then_inc(f_mult, 1)
            pe.wait_ge(f_sq, 1)
            for o in range(2):
                for i in range(2 * KF):
                    a, r = i % KF, i // KF
                    ins = nc.tensor.matmul(m.ps[:, 0, o * HY_W:(o + 1) * HY_W], m.sq[:, C_ONES, :],
                                           fsq[:, a, o * C2 + r * HY_W:o * C2 + (r + 1) * HY_W], start=(i == 0),
                                           stop=(i == 2 * KF - 1))
            ins.then_inc(f_sum, 1)
            pe.wait_ge(comb_done, 1)
            for r in range(2):
                for kt in range(KF):
                    for a in range(KF):
                        ins = nc.tensor.matmul(m.ps[:, 4 + 2 * r + kt, :], dft[:, r, a, kt * P:(kt + 1) * P],
                                               comb[:, r, a, :], start=(a == 0), stop=(a == KF - 1))
                    ins.then_inc(s_mult, 1)
            pe.wait_ge(conv_done, 1)
            for order in range(2):
                src = cv if order == 0 else zt
                pe.wait_ge(s_out, 4)
                if order == 1:
                    pe.wait_ge(y_out, 2 * S)
                for a in range(KF):
                    for i, s in enumerate(streams):
                        for c in range(2):
                            ins = nc.tensor.transpose(m.ps[:, 2 + a, i * HY_W + c * P:i * HY_W + (c + 1) * P],
                                                      src[:, c, s * SEQ + a * P:s * SEQ + (a + 1) * P], m.sq[:, C_ID, :])
                    ins.then_inc(z_turned, 1)
                pe.wait_ge(z_out, 2 * (order + 1))
                for r in range(2):
                    for kt in range(KF):
                        for a in range(KF):
                            ins = nc.tensor.matmul(m.ps[:, 4 + 2 * r + kt, 0:S * HY_W], dft[:, r, a, kt * P:(kt + 1) * P],
                                                   z[:, a, 0:S, :].rearrange("p s c -> p (s c)"), start=(a == 0),
                                                   stop=(a == KF - 1))
                        ins.then_inc(z_mult, 1)
                pe.wait_ge(yf_done, order + 1)
                for i in range(S):
                    for c in range(2):
                        n = 0
                        for r in range(2):
                            for kt in range(KF):
                                ins = nc.tensor.matmul(m.ps[:, 2 * i + c, 0:SEQ],
                                                       yf[:, r, kt, i * HY_W + c * P:i * HY_W + (c + 1) * P],
                                                       dft[:, 2 + r, kt, :], start=(n == 0), stop=(n == 2 * KF - 1))
                                n += 1
                        ins.then_inc(y_mult, 1)

        @block.scalar
        def _(act):
            for i in range(2):
                act.wait_ge(arg_done, i + 1)
                nc.scalar.activation(hid[:, :], arg[:, :], ACT.Sin).then_inc(sine_done, 1)
            act.wait_ge(f_scaled, 1)
            nc.scalar.activation(frs[:, :], frs[:, :], ACT.Sqrt).then_inc(f_root, 1)
            for i in range(4):
                act.wait_ge(s_mult, i + 1)
                nc.scalar.copy(spec[:, i // 2, i % 2, :], m.ps[:, 4 + i, :]).then_inc(s_out, 1)
            for order in range(2):
                for a in range(KF):
                    act.wait_ge(z_turned, 2 * order + a + 1)
                    nc.scalar.copy(z[:, a, 0:S, :].rearrange("p s c -> p (s c)"), m.ps[:, 2 + a, 0:S * HY_W]
                                   ).then_inc(z_out, 1)
                if order == 1:
                    act.wait_ge(yf_done, 1)
                for i in range(4):
                    act.wait_ge(z_mult, 4 * order + i + 1)
                    nc.scalar.copy(zf[:, i // 2, i % 2, :], m.ps[:, 4 + i, 0:S * HY_W]).then_inc(zf_out, 1)

        @block.vector
        def _(dve):
            own = Chain(dve, dve_own)
            for i, vb in enumerate((V_B1, V_B2)):
                dve.wait_ge(h_mult, i + 1)
                if i == 1:
                    dve.wait_ge(sine_done, 1)
                own.link(nc.vector.tensor_scalar(arg[:, :], m.ps[0:64, i, 0:SEQ], m.vec[0:64, vb:vb + 1],
                                                 m.vec[0:64, V_FREQ + i:V_FREQ + i + 1], ALU.add, ALU.mult))
                own.link(nc.vector.tensor_scalar(rnd[:, :], arg[:, :], 1.0 / (TWO_PI_HI + TWO_PI_LO), ROUND, ALU.mult,
                                                 ALU.add))
                own.link(nc.vector.tensor_scalar(rnd[:, :], rnd[:, :], -ROUND, None, ALU.add))
                for part in (TWO_PI_HI, TWO_PI_LO):
                    own.link(nc.vector.scalar_tensor_tensor(out=arg[:, :], in0=rnd[:, :], scalar=-part, in1=arg[:, :],
                                                            op0=ALU.mult, op1=ALU.add))
                nc.vector.tensor_scalar(arg[:, :], arg[:, :], PI, -PI, ALU.min, ALU.max).then_inc(arg_done, 1)
            for a in range(KF):
                for o in range(2):
                    dve.wait_ge(f_mult, 2 * a + o + 1)
                    own.step(nc.vector.tensor_tensor(
                        filt[:, a, o, :, :], m.ps[:, 2 + 2 * a + o, :].rearrange("p (r c) -> p r c", r=2),
                        dec[:, a:a + 1, :].to_broadcast([P, 2, HY_W]), ALU.mult))
            own.meet()
            nc.vector.tensor_tensor(fsq[:, :, :], filt[:, :, :, :, :].rearrange("p a o r c -> p a (o r c)"),
                                    filt[:, :, :, :, :].rearrange("p a o r c -> p a (o r c)"), ALU.mult).then_inc(f_sq, 1)
            dve.wait_ge(f_sum, 1)
            nc.vector.tensor_scalar(frs[:, :], m.ps[:, 0, :], EPS, None, ALU.add).then_inc(f_scaled, 1)
            dve.wait_ge(f_root, 1)
            own.link(nc.vector.reciprocal(frs[:, :], frs[:, :]))
            for a in range(KF):
                for r in range(2):
                    own.step(nc.vector.tensor_tensor(filt[:, a, :, r, :], filt[:, a, :, r, :],
                                                     frs[:, :].rearrange("p (o c) -> p o c", o=2), ALU.mult))
            own.meet()
            own.link(nc.vector.memset(filt[0:1, 0, :, 1, :], 0.0))
            for a in range(KF):
                view = lambda x: x.rearrange("p (o c) -> p o c", o=2)
                own.step(nc.vector.tensor_tensor(view(comb[:, 0, a, :]), filt[:, a, :, 0, :], filt[:, a, :, 1, :], ALU.add))
                own.step(nc.vector.tensor_tensor(view(comb[:, 1, a, :]), filt[:, a, :, 0, :], filt[:, a, :, 1, :],
                                                 ALU.subtract))
            own.meet()
            dve.sem_inc(comb_done, 1)
            for g in range(6):
                tap = [m.vec[:, V_CONV + 6 * j + g:V_CONV + 6 * j + g + 1] for j in range(3)]
                u = lambda lo, hi: t.hy[:, g, s0 * SEQ:].rearrange("p (s n) -> p s n", n=SEQ)[:, :, lo:hi]
                o = lambda lo, hi: cv[:, g, s0 * SEQ:].rearrange("p (s n) -> p s n", n=SEQ)[:, :, lo:hi]
                own.link(nc.vector.tensor_scalar(o(0, SEQ), u(0, SEQ), tap[1], None, ALU.mult))
                own.link(nc.vector.scalar_tensor_tensor(out=o(1, SEQ), in0=u(0, SEQ - 1), scalar=tap[0],
                                                        in1=o(1, SEQ), op0=ALU.mult, op1=ALU.add))
                own.link(nc.vector.scalar_tensor_tensor(out=o(0, SEQ - 1), in0=u(1, SEQ), scalar=tap[2],
                                                        in1=o(0, SEQ - 1), op0=ALU.mult, op1=ALU.add))
            dve.sem_inc(conv_done, 1)
            for order in range(2):
                src = cv if order == 0 else zt
                dve.wait_ge(zf_out, 4 * (order + 1))
                bc = lambda r: spec[:, r, :, order * HY_W:(order + 1) * HY_W].unsqueeze(2).to_broadcast(
                    [P, KF, S, HY_W])
                vw = lambda x: x.rearrange("p k (s c) -> p k s c", s=S)
                if order == 1:
                    dve.wait_ge(y_mult, 2 * S)
                for r in range(2):
                    for kt in range(KF):
                        kk = slice(kt, kt + 1)
                        own.step(nc.vector.tensor_tensor(vw(yf[:, r, kk, :]), vw(zf[:, 0, kk, :]), bc(r)[:, kk], ALU.mult))
                        own.step(nc.vector.tensor_tensor(vw(tmp[:, kk, :]), vw(zf[:, 1, kk, :]), bc(1 - r)[:, kk],
                                                         ALU.mult))
                    own.meet()
                    own.link(nc.vector.tensor_tensor(yf[:, r, :, :], yf[:, r, :, :], tmp[:, :, :],
                                                     ALU.add if r else ALU.subtract))
                dve.sem_inc(yf_done, 1)
                for i, s in enumerate(streams):
                    for c in range(2):
                        dve.wait_ge(y_mult, 2 * S * order + 2 * i + c + 1)
                        tk = slice(s * SEQ, (s + 1) * SEQ)
                        vb = m.vec[:, V_HYB + 2 * order + c:V_HYB + 2 * order + c + 1]
                        own.link(nc.vector.scalar_tensor_tensor(out=zt[:, c, tk], in0=src[:, c, tk], scalar=vb,
                                                                in1=m.ps[:, 2 * i + c, 0:SEQ], op0=ALU.mult,
                                                                op1=ALU.add))
                        out = zt[:, c, tk] if order == 0 else t.yT[:, 3, c, tk]
                        nc.vector.tensor_tensor(out, zt[:, c, tk], cv[:, 2 + 2 * order + c, tk], ALU.mult
                                                ).then_inc(y_out, 1)
                if order == 0:
                    dve.wait_ge(y_out, 2 * S)




def merge(nc, m, d, hs, t, l, t0):
    T = TOK - t0
    halves = [(kind, lo, hi) for kind, lo, hi in ((1, 0, CTX), (0, CTX, TOK)) if lo >= t0]
    steps = [(k, i) for k in range(KD) for i in range(N_BRANCH)]
    PAIRS = len(steps) // 2
    with ExitStack() as ctx:
        raw = ctx.enter_context(sbuf(nc, "wg_raw", [P, 2, KD, 2, P], F32))
        wg = [ctx.enter_context(sbuf(nc, f"wg_split{r}", [P, 2, KD, 2, P], F32R)) for r in range(2)]
        wb = ctx.enter_context(sbuf(nc, "w_branch", [P, 2, N_BRANCH * 2, P], F32))
        wo = ctx.enter_context(sbuf(nc, "w_out", [P, 2, KD, P], F32))
        acc = ctx.enter_context(sbuf(nc, "merged", [P, KD, TOK], F32))
        sg = ctx.enter_context(sbuf(nc, "sig", [P, 2, TOK], F32))
        pr = ctx.enter_context(sbuf(nc, "prod", [P, 2, TOK], F32))
        (block, gate_mult, y_mult, sig_done, prod_done, acc_done, o_mult, o_out, rounded, rested, wg_in0, wg_in1,
         wb_in0, wb_in1, wo_in0, wo_in1) = ctx.enter_context(stage(
             nc, "gate_mult", "y_mult", "sig_done", "prod_done", "acc_done", "o_mult", "o_out", "rounded", "rested",
             "wg_in0", "wg_in1", "wb_in0", "wb_in1", "wo_in0", "wo_in1"))
        wg_ins, wb_ins, wo_ins = (wg_in0, wg_in1), (wb_in0, wb_in1), (wo_in0, wo_in1)

        @block.sync
        def _(sp):
            gates = d["w_in"][l].rearrange("(k p) n -> p k n", p=P)[:, :, O_GATE:].rearrange(
                "p k (i n) -> p k i n", i=N_BRANCH)
            for c in range(PAIRS):
                k, i = steps[2 * c]
                if c >= 2:
                    sp.wait_ge(rested, c - 1)
                for j in range(2):
                    sp.dma_start(raw[:, c % 2, :, j, :], gates[:, :, i + j, k * P:(k + 1) * P]).then_inc(wg_ins[c % 2], 16)
                if c % 2 == 0:
                    if k >= 2:
                        sp.wait_ge(y_mult, N_BRANCH * (k - 1))
                    sp.dma_start(wb[:, k % 2, :, :], d["w_branch"][l].rearrange("i (a p) n -> p (i a) n", p=P)[
                        :, :, k * P:(k + 1) * P]).then_inc(wb_ins[k % 2], 16)
            for k in range(KD):
                if k >= 2:
                    sp.wait_ge(o_mult, k - 1)
                sp.dma_start(wo[:, k % 2, :, :], d["w_out"][l].rearrange("(k p) n -> p k n", p=P)[
                    :, :, k * P:(k + 1) * P]).then_inc(wo_ins[k % 2], 16)

        @block.gpsimd
        def _(pool):
            for c in range(PAIRS):
                pool.wait_ge(rounded, c + 1)
                flat = lambda x: x.rearrange("p k i n -> p (k i n)")
                nc.gpsimd.tensor_tensor(flat(wg[c % 2][:, 1]), flat(raw[:, c % 2]), flat(wg[c % 2][:, 0]).bitcast(F32),
                                        ALU.subtract).then_inc(rested, 1)

        @block.tensor
        def _(pe):
            for n, (k, i) in enumerate(steps):
                if n % 2 == 0:
                    pe.wait_ge(rested, n // 2 + 1)
                if n >= 2:
                    pe.wait_ge(sig_done, n - 1)
                w = wg[n // 2 % 2]
                for kk in range(KD):
                    ins = split_matmul(nc, m.ps[:, n % 2, 0:T], lambda r: w[:, r, kk, i % 2, :],
                                       lambda r: hs[:, r, kk, t0:], kk == 0, kk == KD - 1)
                ins.then_inc(gate_mult, 1)
                if i == 0:
                    pe.wait_ge(wb_ins[k % 2], 16 * (k // 2 + 1))
                if n >= 2:
                    pe.wait_ge(prod_done, n - 1)
                for a in range(2):
                    ins = nc.tensor.matmul(m.ps[:, 2 + n % 2, 0:T], wb[:, k % 2, 2 * i + a, :],
                                           t.yT[:, i, a, t0:], start=(a == 0), stop=(a == 1))
                ins.then_inc(y_mult, 1)
            pe.wait_ge(acc_done, len(steps))
            for k in range(KD):
                pe.wait_ge(wo_ins[k % 2], 16 * (k // 2 + 1))
                if k >= 4:
                    pe.wait_ge(o_out, k - 3)
                for kk in range(KD):
                    ins = nc.tensor.matmul(m.ps[:, 4 + k % 4, 0:T], wo[:, k % 2, kk, :], acc[:, kk, t0:],
                                           start=(kk == 0), stop=(kk == KD - 1))
                ins.then_inc(o_mult, 1)

        @block.scalar
        def _(act):
            def round_pair(c):
                act.wait_ge(wg_ins[c % 2], 32 * (c // 2 + 1))
                if c >= 2:
                    act.wait_ge(gate_mult, 2 * (c - 1))
                flat = lambda x: x.rearrange("p k i n -> p (k i n)")
                nc.scalar.copy(flat(wg[c % 2][:, 0]), flat(raw[:, c % 2])).then_inc(rounded, 1)

            round_pair(0)
            round_pair(1)
            for n in range(len(steps)):
                act.wait_ge(gate_mult, n + 1)
                if n >= 2:
                    act.wait_ge(prod_done, n - 1)
                nc.scalar.activation(sg[:, n % 2, t0:], m.ps[:, n % 2, 0:T], ACT.Sigmoid).then_inc(sig_done, 1)
                if n % 2 == 1 and n // 2 + 2 < PAIRS:
                    round_pair(n // 2 + 2)

        @block.vector
        def _(dve):
            for n, (k, i) in enumerate(steps):
                dve.wait_ge(y_mult, n + 1)
                dve.wait_ge(sig_done, n + 1)
                if n >= 2:
                    dve.wait_ge(acc_done, n - 1)
                if i == 0:
                    nc.vector.tensor_tensor(acc[:, k, t0:], sg[:, n % 2, t0:], m.ps[:, 2 + n % 2, 0:T], ALU.mult
                                            ).then_inc(prod_done, 1)
                    dve.wait_ge(prod_done, n + 1)
                    dve.sem_inc(acc_done, 1)
                    continue
                nc.vector.tensor_tensor(pr[:, n % 2, t0:], sg[:, n % 2, t0:], m.ps[:, 2 + n % 2, 0:T], ALU.mult
                                        ).then_inc(prod_done, 1)
                dve.wait_ge(prod_done, n + 1)
                dve.wait_ge(acc_done, n)
                nc.vector.tensor_tensor(acc[:, k, t0:], acc[:, k, t0:], pr[:, n % 2, t0:], ALU.add).then_inc(acc_done, 1)
            for k in range(KD):
                dve.wait_ge(o_mult, k + 1)
                for kind, lo, hi in halves:
                    ins = nc.vector.scalar_tensor_tensor(
                        out=m.resid[:, k, lo:hi], in0=m.ps[:, 4 + k % 4, lo - t0:hi - t0],
                        scalar=m.mod[:, 2 * KD + k, kind:kind + 1], in1=m.resid[:, k, lo:hi], op0=ALU.mult, op1=ALU.add)
                ins.then_inc(o_out, 1)




def peer_select(nc, m, d, hs, sel, l, t0):
    T = TOK - t0
    CH = 2 * P
    NCH = PH * 2 * P // CH
    tb0 = t0 // P
    blocks = list(range(tb0, NB))
    with ExitStack() as ctx:
        sb = lambda name, shape, dt=F32: ctx.enter_context(sbuf(nc, name, shape, dt))
        raw = sb("wq_raw", [P, 2, KD, CH])
        wq = [ctx.enter_context(sbuf(nc, f"wq_split{r}", [P, 2, KD, CH], F32R)) for r in range(2)]
        qT = sb("qT", [P, HC, TOK])
        sk = sb("subkeys", [P, HC, P])
        skT = sb("subkeysT", [P, HC, P])
        sc = sb("scores", [P, 2, HC, P])
        s2 = sb("scores2", [P, HC, P])
        sv = sb("sv", [P, HC, TOPK])
        si = sb("si", [P, HC, TOPK], U32)
        sif = sb("sif", [P, HC, TOPK])
        cand = sb("cand", [P, PH, TOPK * TOPK])
        cand2 = sb("cand2", [P, PH, TOPK * TOPK])
        best = sb("best", [P, PH, TOPK])
        pos = sb("pos", [P, PH, TOPK], U32)
        part = sb("part", [P, 2, PH, TOPK], U32)
        partf = sb("partf", [P, 2, PH, TOPK])
        eq = cand[:, :, :].rearrange("p h (a b) -> p (h a) b", a=TOPK)
        pick = sb("pick", [P, 2, 3, P])
        dn = sb("dn", [P, PH])
        (block, sk_in, sk_turned, sk_out, q_mult, q_out, s_mult, s_out, s_used, diffed, g_exp, picked, p_turned,
         p_out, dve_own, rounded, rested, wq_in0, wq_in1) = ctx.enter_context(stage(
             nc, "sk_in", "sk_turned", "sk_out", "q_mult", "q_out", "s_mult", "s_out", "s_used", "diffed", "g_exp",
             "picked", "p_turned", "p_out", "dve_own", "rounded", "rested", "wq_in0", "wq_in1"))
        wq_ins = (wq_in0, wq_in1)
        LOW = -3.0e38

        @block.sync
        def _(sp):
            for c in range(NCH):
                if c >= 2:
                    sp.wait_ge(rested, c - 1)
                sp.dma_start(raw[:, c % 2, :, :], d["peer_wq"][l].rearrange("(k p) n -> p k n", p=P)[
                    :, :, c * CH:(c + 1) * CH]).then_inc(wq_ins[c % 2], 16)
                if c == 0:
                    sp.dma_start(sk[:, :, :], d["peer_subkeys"][l].rearrange("h c n d -> n (h c) d")).then_inc(sk_in, 16)

        @block.gpsimd
        def _(pool):
            for c in range(NCH):
                pool.wait_ge(rounded, c + 1)
                nc.gpsimd.tensor_tensor(wq[c % 2][:, 1], raw[:, c % 2], wq[c % 2][:, 0].bitcast(F32), ALU.subtract
                                        ).then_inc(rested, 1)

        @block.tensor
        def _(pe):
            for g in range(HC):
                if g % 2 == 0:
                    pe.wait_ge(rested, g // 2 + 1)
                if g >= 2:
                    pe.wait_ge(q_out, g - 1)
                w = wq[g // 2 % 2]
                for k in range(KD):
                    ins = split_matmul(nc, m.ps[:, g % 2, 0:T], lambda r: w[:, r, k, (g % 2) * P:(g % 2 + 1) * P],
                                       lambda r: hs[:, r, k, t0:], k == 0, k == KD - 1)
                ins.then_inc(q_mult, 1)
            pe.wait_ge(sk_in, 16)
            for q in range(4):
                if q >= 2:
                    pe.wait_ge(sk_out, q - 1)
                for i in range(4):
                    ins = nc.tensor.transpose(m.ps[:, 2 + q % 2, i * P:(i + 1) * P], sk[:, 4 * q + i, :], m.sq[:, C_ID, :])
                ins.then_inc(sk_turned, 1)
            pe.wait_ge(sk_out, 4)
            pe.wait_ge(q_out, HC)

            def turn(n):
                pe.wait_ge(picked, n + 1)
                if n >= 1:
                    pe.wait_ge(p_out, n)
                for i in range(3):
                    ins = nc.tensor.transpose(m.ps[:, 0, i * P:(i + 1) * P], pick[:, n % 2, i, :], m.sq[:, C_ID, :])
                ins.then_inc(p_turned, 1)

            for n, b in enumerate(blocks):
                for q in range(4):
                    if n >= 1:
                        pe.wait_ge(s_out, 4 * (n - 1) + q + 1)
                    for i in range(4):
                        hc = 4 * q + i
                        ins = nc.tensor.matmul(m.ps[:, 4 + q, i * P:(i + 1) * P], qT[:, hc, b * P:(b + 1) * P],
                                               skT[:, hc, :], start=True, stop=True)
                    ins.then_inc(s_mult, 1)
                if n >= 1:
                    turn(n - 1)
            turn(len(blocks) - 1)

        @block.scalar
        def _(act):
            def round_chunk(c):
                act.wait_ge(wq_ins[c % 2], 16 * (c // 2 + 1))
                if c >= 2:
                    act.wait_ge(q_mult, 2 * (c - 1))
                nc.scalar.copy(wq[c % 2][:, 0], raw[:, c % 2]).then_inc(rounded, 1)

            round_chunk(0)
            round_chunk(1)
            for g in range(HC):
                act.wait_ge(q_mult, g + 1)
                nc.scalar.copy(qT[:, g, t0:], m.ps[:, g % 2, 0:T]).then_inc(q_out, 1)
                if g % 2 == 1 and g // 2 + 2 < NCH:
                    round_chunk(g // 2 + 2)
            for q in range(4):
                act.wait_ge(sk_turned, q + 1)
                nc.scalar.copy(skT[:, 4 * q:4 * q + 4, :].rearrange("p a b -> p (a b)"), m.ps[:, 2 + q % 2, :]
                               ).then_inc(sk_out, 1)

            def weights(n):
                act.wait_ge(diffed, n + 1)
                nc.scalar.activation(pick[:, n % 2, 2, :], pick[:, n % 2, 2, :], ACT.Exp).then_inc(g_exp, 1)
                act.wait_ge(p_turned, n + 1)
                b = blocks[n]
                nc.scalar.copy(sel[:, :, b * P:(b + 1) * P], m.ps[:, 0, 0:3 * P].rearrange("p (a b) -> p a b", a=3)
                               ).then_inc(p_out, 1)

            for n, b in enumerate(blocks):
                if n >= 2:
                    act.wait_ge(s_used, n - 1)
                for q in range(4):
                    act.wait_ge(s_mult, 4 * n + q + 1)
                    nc.scalar.copy(sc[:, n % 2, 4 * q:4 * q + 4, :].rearrange("p a b -> p (a b)"), m.ps[:, 4 + q, :]
                                   ).then_inc(s_out, 1)
                if n >= 1:
                    weights(n - 1)
            weights(len(blocks) - 1)

        @block.vector
        def _(dve):
            own = Chain(dve, dve_own)

            def top16(rows, val, idx, src, src2):
                for r in range(rows):
                    own.step(nc.vector.max(val(r, 0), src(r)))
                own.meet()
                for r in range(rows):
                    own.step(nc.vector.max_index(idx(r, 0), val(r, 0), src(r)))
                    own.step(nc.vector.match_replace(src2(r), val(r, 0), src(r), LOW))
                own.meet()
                for r in range(rows):
                    own.step(nc.vector.max(val(r, 1), src2(r)))
                own.meet()
                for r in range(rows):
                    own.step(nc.vector.max_index(idx(r, 1), val(r, 1), src2(r)))
                own.meet()

            for n, b in enumerate(blocks):
                dve.wait_ge(s_out, 4 * (n + 1))
                top16(HC, lambda r, j: sv[:, r, 8 * j:8 * j + 8], lambda r, j: si[:, r, 8 * j:8 * j + 8],
                      lambda r: sc[:, n % 2, r, :], lambda r: s2[:, r, :])
                dve.sem_inc(s_used, 1)
                own.link(nc.vector.tensor_copy(sif[:, :, :], si[:, :, :]))
                svp = sv[:, :, :].rearrange("p (h c) k -> p h c k", c=2)
                own.link(nc.vector.tensor_tensor(
                    cand[:, :, :].rearrange("p h (a b) -> p h a b", a=TOPK),
                    svp[:, :, 0, :].unsqueeze(3).to_broadcast([P, PH, TOPK, TOPK]),
                    svp[:, :, 1, :].unsqueeze(2).to_broadcast([P, PH, TOPK, TOPK]), ALU.add))
                top16(PH, lambda r, j: best[:, r, 8 * j:8 * j + 8], lambda r, j: pos[:, r, 8 * j:8 * j + 8],
                      lambda r: cand[:, r, :], lambda r: cand2[:, r, :])
                if n >= 2:
                    dve.wait_ge(p_turned, n - 1)
                nc.vector.tensor_tensor(pick[:, n % 2, 2, :].rearrange("p (h k) -> p h k", h=PH), best[:, :, :],
                                        best[:, :, 0:1].to_broadcast([P, PH, TOPK]), ALU.subtract).then_inc(diffed, 1)
                own.step(nc.vector.tensor_scalar(part[:, 0, :, :], pos[:, :, :], 4, None, ALU.logical_shift_right))
                own.step(nc.vector.tensor_scalar(part[:, 1, :, :], pos[:, :, :], 15, None, ALU.bitwise_and))
                own.meet()
                own.link(nc.vector.tensor_copy(partf[:, :, :, :], part[:, :, :, :]))
                sip = sif[:, :, :].rearrange("p (h c) k -> p h c k", c=2)
                for c in range(2):
                    own.link(nc.vector.tensor_tensor(
                        eq, partf[:, c, :, :].rearrange("p h k -> p (h k)").unsqueeze(2).to_broadcast(
                            [P, PH * TOPK, TOPK]),
                        m.sq[:, C_IOTA:C_IOTA + 1, 0:TOPK].to_broadcast([P, PH * TOPK, TOPK]), ALU.is_equal))
                    for h in range(PH):
                        e = eq[:, h * TOPK:(h + 1) * TOPK, :]
                        own.step(nc.vector.tensor_tensor(e, e, sip[:, h, c:c + 1, :].to_broadcast([P, TOPK, TOPK]),
                                                         ALU.mult))
                    own.meet()
                    own.link(nc.vector.tensor_reduce(pick[:, n % 2, c, :], eq, axis=AX.X, op=ALU.add))
                dve.wait_ge(g_exp, n + 1)
                own.link(nc.vector.tensor_reduce(dn[:, :], pick[:, n % 2, 2, :].rearrange("p (h k) -> p h k", h=PH),
                                                 axis=AX.X, op=ALU.add))
                own.link(nc.vector.reciprocal(dn[:, :], dn[:, :]))
                nc.vector.tensor_tensor(pick[:, n % 2, 2, :].rearrange("p (h k) -> p h k", h=PH),
                                        pick[:, n % 2, 2, :].rearrange("p (h k) -> p h k", h=PH),
                                        dn[:, :].unsqueeze(2).to_broadcast([P, PH, TOPK]), ALU.mult).then_inc(picked, 1)


def peer_weights(nc, m, sel, wd, t0):
    GRP = 4
    STEP = 16
    TURNS = P // STEP
    G = STEP // GRP
    BY_POOL = (0, 1, 4, 5, 8, 9, 10, 12, 13)
    done = lambda who, g: len([s for s in who if s < (g + 1) * GRP])
    BY_DVE = tuple(s for s in range(STEP) if s not in BY_POOL)
    blocks = list(range(t0 // P, NB))
    with ExitStack() as ctx:
        ia = ctx.enter_context(sbuf(nc, "hot_i", [P, STEP, P], F32))
        ib = ctx.enter_context(sbuf(nc, "hot_j", [P, STEP, P], F32))
        wsb = ctx.enter_context(sbuf(nc, "w_block", [P, 2, P, P], F32))
        keys = ctx.enter_context(sbuf(nc, "keys", [P, STEP], F32))
        (block, slots_seen, keys_in, hot_i, hot_j, w_free, w_mult, w_banks, w_out, w_stored0, w_stored1) = ctx.enter_context(
            stage(nc, "slots_seen", "keys_in", "hot_i", "hot_j", "w_free", "w_mult", "w_banks", "w_out", "w_stored0", "w_stored1"))
        w_stored = (w_stored0, w_stored1)

        @block.vector
        def _(dve):
            dve.sem_inc(w_free, G)
            for n, b in enumerate(blocks):
                with dve.Fori(0, TURNS) as i:
                    for s in range(STEP):
                        if s % GRP == 0:
                            dve.wait_ge(w_free, i * G + (n * TURNS * G + s // GRP + 1))
                        tok = i * STEP + (b * P + s)
                        if s in BY_DVE:
                            nc.vector.tensor_scalar(ib[:, s, :], m.sq[:, C_IOTA, :], sel[:, 1, bass.ds(tok, 1)], None,
                                                    ALU.is_equal)
                        nc.vector.tensor_scalar(ia[:, s, :], m.sq[:, C_IOTA, :], sel[:, 0, bass.ds(tok, 1)],
                                                sel[:, 2, bass.ds(tok, 1)], ALU.is_equal, ALU.mult).then_inc(hot_i, 1)

        @block.gpsimd
        def _(pool):
            for n, b in enumerate(blocks):
                with pool.Fori(0, TURNS) as i:
                    nc.gpsimd.tensor_copy(keys[:, :], sel[:, 1, bass.ds(i * STEP + b * P, STEP)]).then_inc(keys_in, 1)
                    pool.wait_ge(keys_in, i + (n * TURNS + 1))
                    for s in BY_POOL:
                        if s % GRP == 0:
                            pool.wait_ge(w_free, i * G + (n * TURNS * G + s // GRP + 1))
                            pool.sem_inc(slots_seen, 1)
                        nc.gpsimd.tensor_scalar(ib[:, s, :], m.sq[:, C_IOTA, :], keys[:, s:s + 1], None,
                                                ALU.is_equal).then_inc(hot_j, 1)
                    pool.wait_ge(hot_j, i * len(BY_POOL) + (n * TURNS + 1) * len(BY_POOL))

        @block.tensor
        def _(pe):
            for n, b in enumerate(blocks):
                with pe.Fori(0, TURNS) as i:
                    for g in range(G):
                        pe.wait_ge(hot_i, i * STEP + (n * P + (g + 1) * GRP))
                        pe.wait_ge(hot_j, i * len(BY_POOL) + (n * TURNS * len(BY_POOL) + done(BY_POOL, g)))
                        pe.wait_ge(w_banks, i * G + (n * TURNS * G + g + 1))
                        for s in range(GRP):
                            ins = nc.tensor.matmul(m.ps[:, g, s * P:(s + 1) * P], ib[:, g * GRP + s, :],
                                                   ia[:, g * GRP + s, :], start=True, stop=True)
                        ins.then_inc(w_mult, 1)
                        pe.wait_ge(w_mult, i * G + (n * TURNS * G + g + 1))
                        pe.sem_inc(w_free, 1)

        @block.scalar
        def _(act):
            act.sem_inc(w_banks, G)
            for n, b in enumerate(blocks):
                if n >= 2:
                    act.wait_ge(w_stored[n % 2], 16 * (n // 2))
                with act.Fori(0, TURNS) as i:
                    for g in range(G):
                        act.wait_ge(w_mult, i * G + (n * TURNS * G + g + 1))
                        nc.scalar.copy(wsb[:, n % 2, :, bass.ds(i * STEP + g * GRP, GRP)],
                                       m.ps[:, g, :].rearrange("p (s i) -> p i s", s=GRP)).then_inc(w_out, 1)
                        act.wait_ge(w_out, i * G + (n * TURNS * G + g + 1))
                        act.sem_inc(w_banks, 1)

        @block.sync
        def _(sp):
            for n, b in enumerate(blocks):
                sp.wait_ge(w_out, (n + 1) * TURNS * G)
                sp.dma_start(wd.rearrange("i j t -> j i t")[:, :, b * P:(b + 1) * P], wsb[:, n % 2, :, :]
                             ).then_inc(w_stored[n % 2], 16)
            for n in range(max(0, len(blocks) - 2), len(blocks)):
                sp.wait_ge(w_stored[n % 2], 16 * (n // 2 + 1))


def peer_experts(nc, m, d, hs, wd, l, t0):
    T = TOK - t0
    GRP = 2
    NG = NK // GRP
    KO = KD // GRP
    halves = [(kind, lo, hi) for kind, lo, hi in ((1, 0, CTX), (0, CTX, TOK)) if lo >= t0]
    ug = d["peer_u"][l].rearrange("(g q j) n -> g j q n", q=GRP, j=P)
    vg = d["peer_v"][l].rearrange("(g q j) n -> g j q n", q=GRP, j=P)
    wg = wd.rearrange("(g q) j t -> g j q t", q=GRP)
    with ExitStack() as ctx:
        sb = lambda name, shape, dt=F32: ctx.enter_context(sbuf(nc, name, shape, dt))
        us = [sb(f"u{i}", [P, GRP, D]) for i in range(2)]
        vs = [sb(f"v{i}", [P, GRP, D]) for i in range(2)]
        vr = [sb(f"v_split{i}", [P, 2, GRP, D], F32R) for i in range(2)]
        ws = [sb(f"w{i}", [P, GRP, T]) for i in range(2)]
        ut = sb("uT", [P, 2, 2, KD * P], F32R)
        ga = sb("gelu", [P, 2, T])
        wf = sb("weighted", [P, 2, T])
        wa = sb("w_split", [P, 2, 2, GRP, T], F32R)
        acc = sb("experts_out", [P, KD, T])
        (block, u_in0, u_in1, v_in0, v_in1, w_in0, w_in1, u_turned, u_rounded, u_rested, v_rounded, v_rested, a_mult,
         gelu_done, weighted, wa_rounded, wa_done, o_mult, o_out, dve_own) = ctx.enter_context(stage(
             nc, "u_in0", "u_in1", "v_in0", "v_in1", "w_in0", "w_in1", "u_turned", "u_rounded", "u_rested",
             "v_rounded", "v_rested", "a_mult", "gelu_done", "weighted", "wa_rounded", "wa_done", "o_mult", "o_out",
             "dve_own"))
        u_ins, v_ins, w_ins = (u_in0, u_in1), (v_in0, v_in1), (w_in0, w_in1)

        def ahead(work, pair, r, q, first, last):
            if q + 1 < GRP:
                work(pair, r, q + 1, first)
            elif r == 0:
                work(pair, 1, 0, first)
            elif not last:
                work(pair + 1, 0, 0, False)

        def pairs(engine, group):
            group(0, 0, True, False)
            group(0, 1, True, False)
            with engine.Fori(1, NG // 2 - 1) as i:
                group(i, 0, False, False)
                group(i, 1, False, False)
            group(NG // 2 - 1, 0, False, True)
            group(NG // 2 - 1, 1, False, True)

        @block.sync
        def _(sp):
            def pair(i, first):
                for r in range(2):
                    g = 2 * i + r
                    if not first:
                        sp.wait_ge(u_turned, i * (2 * GRP) + (r - 1) * GRP)
                    sp.dma_start(us[r][:, :, :], ug[g]).then_inc(u_ins[r], 16)
                    if not first:
                        sp.wait_ge(wa_done, i * (2 * GRP) + (r - 1) * GRP)
                    sp.dma_start(ws[r][:, :, :], wg[g][:, :, t0:]).then_inc(w_ins[r], 16)
                    if not first:
                        sp.wait_ge(v_rested, i * 2 + (r - 1))
                    sp.dma_start(vs[r][:, :, :], vg[g]).then_inc(v_ins[r], 16)

            pair(0, True)
            with sp.Fori(1, NG // 2) as i:
                pair(i, False)

        @block.gpsimd
        def _(pool):
            def pair(i):
                for r in range(2):
                    pool.wait_ge(v_rounded, i * 2 + (r + 1))
                    nc.gpsimd.tensor_tensor(vr[r][:, 1], vs[r][:, :, :], vr[r][:, 0].bitcast(F32), ALU.subtract
                                            ).then_inc(v_rested, 1)

            pair(0)
            with pool.Fori(1, NG // 2) as i:
                pair(i)

        @block.tensor
        def _(pe):
            def turn(pair, r, q, first):
                n = pair * (2 * GRP) + (r * GRP + q)
                if q == 0:
                    pe.wait_ge(u_ins[r], pair * 16 + 16)
                if not (first and r == 0):
                    pe.wait_ge(u_rested, n - 1)
                for k in range(KD):
                    ins = nc.tensor.transpose(m.ps[:, 2 * q + k // 4, (k % 4) * P:(k % 4 + 1) * P],
                                              us[r][:, q, k * P:(k + 1) * P], m.sq[:, C_ID, :])
                ins.then_inc(u_turned, 1)

            def activations(pair, r, q, first):
                n = pair * (2 * GRP) + (r * GRP + q)
                pe.wait_ge(u_rested, n + 1)
                if not (first and r == 0):
                    pe.wait_ge(gelu_done, n - 1)
                for k in range(KD):
                    ins = split_matmul(nc, m.ps[:, 4 + q, 0:T], lambda s: ut[:, q, s, k * P:(k + 1) * P],
                                       lambda s: hs[:, s, k, t0:], k == 0, k == KD - 1)
                ins.then_inc(a_mult, 1)

            def outputs(pair, r, q, first):
                if q == 0:
                    pe.wait_ge(wa_done, pair * (2 * GRP) + r * GRP)
                    pe.wait_ge(v_rested, pair * 2 + r)
                for k in range(KO * q, KO * q + KO):
                    if not (first and r == 1 and k < 2):
                        pe.wait_ge(o_out, pair * (2 * KD) + ((r - 1) * KD + k - 1))
                    for e in range(GRP):
                        ins = split_matmul(nc, m.ps[:, 6 + k % 2, 0:T], lambda s: vr[1 - r][:, s, e, k * P:(k + 1) * P],
                                           lambda s: wa[:, 1 - r, s, e, :], e == 0, e == GRP - 1)
                    ins.then_inc(o_mult, 1)

            def group(pair, r, first, last):
                for q in range(GRP):
                    ahead(turn, pair, r, q, first, last)
                    activations(pair, r, q, first)
                    if not (first and r == 0):
                        outputs(pair, r, q, first)

            turn(0, 0, 0, True)
            pairs(pe, group)
            for q in range(GRP):
                outputs(NG // 2, 0, q, False)

        @block.scalar
        def _(act):
            def round_u(pair, r, q, first):
                n = pair * (2 * GRP) + (r * GRP + q)
                act.wait_ge(u_turned, n + 1)
                if not (first and r == 0):
                    act.wait_ge(a_mult, n - 1)
                for b in range(2):
                    nc.scalar.copy(ut[:, q, 0, b * BANK:(b + 1) * BANK], m.ps[:, 2 * q + b, :]).then_inc(u_rounded, 1)

            def group(pair, r, first, last):
                for q in range(GRP):
                    n = pair * (2 * GRP) + (r * GRP + q)
                    ahead(round_u, pair, r, q, first, last)
                    if q == 0:
                        act.wait_ge(v_ins[r], pair * 16 + 16)
                        if not first:
                            act.wait_ge(o_mult, pair * (2 * KD) + (r - 1) * KD)
                    ins = nc.scalar.copy(vr[r][:, 0, q], vs[r][:, q, :])
                    if q == GRP - 1:
                        ins.then_inc(v_rounded, 1)
                    act.wait_ge(a_mult, n + 1)
                    if not (first and r == 0):
                        act.wait_ge(weighted, n - 1)
                    nc.scalar.activation(ga[:, q, :], m.ps[:, 4 + q, 0:T], ACT.Gelu_apprx_tanh).then_inc(gelu_done, 1)

            round_u(0, 0, 0, True)
            pairs(act, group)

        @block.vector
        def _(dve):
            def add_out(pair, r, q):
                for k in range(KO * q, KO * q + KO):
                    dve.wait_ge(o_mult, pair * (2 * KD) + ((r - 1) * KD + k + 1))
                    nc.vector.tensor_tensor(acc[:, k, :], acc[:, k, :], m.ps[:, 6 + k % 2, 0:T], ALU.add).then_inc(o_out, 1)

            def rest_u(pair, r, q, first):
                n = pair * (2 * GRP) + (r * GRP + q)
                for b in range(2):
                    dve.wait_ge(u_rounded, n * 2 + (b + 1))
                    ins = nc.vector.tensor_tensor(ut[:, q, 1, b * BANK:(b + 1) * BANK], m.ps[:, 2 * q + b, :],
                                                  ut[:, q, 0, b * BANK:(b + 1) * BANK].bitcast(F32), ALU.subtract)
                ins.then_inc(u_rested, 1)

            def weigh(pair, r, q, first):
                n = pair * (2 * GRP) + (r * GRP + q)
                if q == 0:
                    dve.wait_ge(w_ins[r], pair * 16 + 16)
                    if not first:
                        dve.wait_ge(o_mult, pair * (2 * KD) + (r - 1) * KD)
                dve.wait_ge(gelu_done, n + 1)
                nc.vector.tensor_tensor(wf[:, q, :], ga[:, q, :], ws[r][:, q, :], ALU.mult).then_inc(weighted, 1)
                dve.wait_ge(weighted, n + 1)
                nc.vector.tensor_copy(wa[:, r, 0, q, :], wf[:, q, :]).then_inc(wa_rounded, 1)
                dve.wait_ge(wa_rounded, n + 1)
                nc.vector.tensor_tensor(wa[:, r, 1, q, :], wf[:, q, :], wa[:, r, 0, q, :].bitcast(F32), ALU.subtract
                                        ).then_inc(wa_done, 1)

            def group(pair, r, first, last):
                for q in range(GRP):
                    ahead(rest_u, pair, r, q, first, last)
                    weigh(pair, r, q, first)
                    if not (first and r == 0):
                        add_out(pair, r, q)

            own = Chain(dve, dve_own)
            own.link(nc.vector.memset(acc[:, :, :], 0.0))
            rest_u(0, 0, 0, True)
            pairs(dve, group)
            for q in range(GRP):
                add_out(NG // 2, 0, q)
            dve.wait_ge(o_out, NG * KD)
            for k in range(KD):
                for kind, lo, hi in halves:
                    nc.vector.scalar_tensor_tensor(
                        out=m.resid[:, k, lo:hi], in0=acc[:, k, lo - t0:hi - t0],
                        scalar=m.mod[:, 5 * KD + k, kind:kind + 1], in1=m.resid[:, k, lo:hi], op0=ALU.mult, op1=ALU.add)


def store(nc, m, out):
    with ExitStack() as ctx:
        tok = ctx.enter_context(sbuf(nc, "tok", [P, 2, D], F32))
        block, turned, copied, stored = ctx.enter_context(stage(nc, "turned", "copied", "stored"))

        @block.tensor
        def _(pe):
            for b in range(2):
                for k in range(KD):
                    ins = nc.tensor.transpose(m.ps[:, 2 * b + k // 4, (k % 4) * P:(k % 4 + 1) * P],
                                              m.resid[:, k, CTX + b * P:CTX + (b + 1) * P], m.sq[:, C_ID, :])
                    if k % 4 == 3:
                        ins.then_inc(turned, 1)

        @block.scalar
        def _(act):
            for i in range(4):
                act.wait_ge(turned, i + 1)
                nc.scalar.copy(tok[:, i // 2, (i % 2) * 512:(i % 2) * 512 + 512], m.ps[:, i, :]).then_inc(copied, 1)

        @block.sync
        def _(sp):
            sp.wait_ge(copied, 4)
            sp.dma_start(out[0].rearrange("(b p) n -> p b n", p=P), tok[:, :, :]).then_inc(stored, 16)
            sp.wait_ge(stored, 16)


def build(nc, d, out, upto=None, tap=None):
    NUMBER[:] = [0, 0]
    wd = nc.dram_tensor("peer_w", (NK, NK, TOK), F32, kind="Internal").ap()
    m = Mem()
    t = Mem()
    with ExitStack() as ctx:
        sb = lambda name, shape: ctx.enter_context(sbuf(nc, name, shape, F32))
        m.ps = ctx.enter_context(nc.psum_tensor("ps", [P, BANKS, BANK], F32))
        m.sq = sb("squares", [P, C_N, P])
        m.resid = sb("resid", [P, KD, TOK])
        m.cond = sb("cond", [P, KD, 2])
        m.vec = sb("vec", [P, V_ROWS])
        m.mod = sb("mod", [P, 6 * KD, 2])
        setup(nc, m, d)
        for l in range(LAYERS):
            last = l == LAYERS - 1
            own0 = CTX if last else 0
            modulation(nc, m, d, l)
            with sbuf(nc, "h_split", [P, 2, KD, TOK], F32R) as hs:
                mod_norm(nc, m, hs, 0, 0)
                with ExitStack() as inner:
                    tb = lambda name, shape: inner.enter_context(sbuf(nc, name, shape, F32))
                    t.yT = tb("yT", [P, N_BRANCH, 2, TOK])
                    with ExitStack() as branch:
                        tb = lambda name, shape: branch.enter_context(sbuf(nc, name, shape, F32))
                        t.ckv, t.kpe, t.cq = tb("ckv", [P, TOK]), tb("kpe", [P, TOK]), tb("cq", [P, 2, TOK])
                        t.gq, t.gk, t.gv = tb("gq", [P, 2, TOK]), tb("gk", [P, TOK]), tb("gv", [P, NB, P])
                        t.mq, t.mk = tb("mq", [P, 2, TOK]), tb("mk", [P, 2, TOK])
                        t.mvo, t.mg = tb("mvo", [P, NB, 2 * ML_W]), tb("mg", [P, NB, 4 * ML_H])
                        t.hy = tb("hy", [P, 6, TOK])
                        input_projection(nc, m, d, hs, t, l, own0)
                        with sbuf(nc, "qm", [P, MLA_H, TOK], F32) as t.qm, \
                                sbuf(nc, "km", [P, MLA_H, TOK], F32) as t.km, \
                                sbuf(nc, "vm", [P, NB, MLA_H * MLA_V], F32) as t.vm:
                            attention_heads(nc, m, d, t, l, own0)
                            attention(nc, m, t, range(own0 // P, NB))
                        mlstm(nc, m, t, range(own0 // P, NB))
                        hyena(nc, m, d, t, l, (1,) if last else (0, 1))
                    if tap:
                        tap(f"yT{l}", t.yT)
                    merge(nc, m, d, hs, t, l, own0)
                mod_norm(nc, m, hs, 3 * KD, own0)
                if tap:
                    tap(f"xm{l}", m.resid)
                with sbuf(nc, "sel", [P, 3, TOK], F32) as sel:
                    peer_select(nc, m, d, hs, sel, l, own0)
                    if tap:
                        tap(f"sel{l}", sel)
                    peer_weights(nc, m, sel, wd, own0)
                peer_experts(nc, m, d, hs, wd, l, own0)
            if tap:
                tap(f"x{l}", m.resid)
            if upto == l:
                break
        store(nc, m, out)



_INS = ["x", "c", "ctx", "c_ctx", "ada_w", "ada_b", "norm1", "norm2", "w_in", "mla_q_norm", "mla_kv_norm",
        "mla_w_uq", "mla_w_ukv", "mla_qk_norm_q", "mla_qk_norm_k", "gqa_qk_norm_q", "gqa_qk_norm_k", "ml_gate_b",
        "ml_norm", "hy_conv", "hy_w1", "hy_b1", "hy_freq", "hy_w2", "hy_b2", "hy_w3", "hy_bias", "w_branch", "w_out",
        "peer_wq", "peer_subkeys", "peer_u", "peer_v"]


def _constants():
    import math

    import numpy as np

    f = np.float32
    r, c = np.arange(P)[:, None], np.arange(P)[None, :]
    rot = {}
    for name, base, half, n in (("m", MLA_NOPE, 8, 2), ("g", 0, 16, 4)):
        a = np.zeros((P, P), f)
        for s in range(n):
            for j in range(half):
                lo = base + s * 2 * half + j
                a[lo + half, lo] = -1
                a[lo, lo + half] = 1
        rot[name] = a
    square = np.concatenate([
        r == c, np.ones((P, P)), r // HD == c // HD, r <= c, r >= c, r > c, r < c,
        np.where(c > r, -1e30, 0), np.where(c < r, -1e30, 0), rot["m"], rot["g"], np.broadcast_to(c, (P, P))]).astype(f)
    grid_w = 64
    pos = (np.arange(LAT) // grid_w, np.arange(LAT) % grid_w)
    rope = np.zeros((4, P, TOK), f)
    rope[0::2] = 1
    for i, (base, half, reps) in enumerate(((MLA_NOPE, 8, 1), (0, 16, 2))):
        inv = (f(10000.0) ** (-np.arange(0, 2 * half, 2, dtype=f) / f(2 * half))).astype(f)
        for rep in range(reps):
            for ax in range(2):
                ang = (pos[ax].astype(f)[:, None] * inv).T
                for side in range(2):
                    at = base + rep * HD + ax * 2 * half + side * half
                    rope[2 * i, at:at + half, CTX:] = np.cos(ang)
                    rope[2 * i + 1, at:at + half, CTX:] = np.sin(ang)
    n = np.arange(SEQ)
    ang = 2 * np.pi * np.outer(n, n + 0.5) / (2 * SEQ)
    dft = np.stack([np.cos(ang), -np.sin(ang), np.cos(ang).T / SEQ, -np.sin(ang).T / SEQ]).astype(f)
    tt = np.arange(SEQ, dtype=f) / f(SEQ)
    a2 = f(2.0 * math.pi) * tt[:, None] * np.arange(1, 17, dtype=f)
    feat = np.concatenate([tt[:, None], np.sin(a2), np.cos(a2)], axis=1).T.astype(f)
    lt = math.log(1e-2)
    alpha = np.linspace(-lt / 1.5, -lt / 0.3, HY_W, dtype=f)
    decay = np.exp(-tt[:, None] * alpha).astype(f)
    return {"k_square": square, "k_rope": rope.reshape(4 * P, TOK), "k_dft": dft, "k_feat": feat, "k_decay": decay}


def kernel(**inputs):
    import numpy as _np
    import concourse.bacc as _bacc
    from concourse.bass_utils import run_bass_kernel_spmd as _run

    nc = _bacc.Bacc("TRN2", target_bir_lowering=False, num_devices=1)
    arrays, d = {}, {}
    for name, a in [(n, inputs[n]) for n in _INS] + list(_constants().items()):
        a = _np.ascontiguousarray(a)
        arrays[f"in_{name}"] = a
        d[name] = nc.dram_tensor(f"in_{name}", a.shape, mybir.dt.from_np(a.dtype), kind="ExternalInput").ap()
    out = nc.dram_tensor("out", (1, LAT, D), F32, kind="ExternalOutput").ap()
    build(nc, d, out)
    r = _run(nc, [arrays], core_ids=[0])
    return r.results[0]["out"]
```

```python
from contextlib import ExitStack, contextmanager

import concourse.bass as bass
from concourse import mybir

F32 = mybir.dt.float32
F32R = mybir.dt.float32r
U32 = mybir.dt.uint32
ALU = mybir.AluOpType
ACT = mybir.ActivationFunctionType
AX = mybir.AxisListType

P = 128
D = 1024
KD = D // P
CTX = 256
LAT = 256
TOK = CTX + LAT
NB = TOK // P
LAYERS = 2
EPS = 1e-6
BANK = 512
BANKS = 8

MLA_Q, MLA_KV, MLA_PE, MLA_NOPE, MLA_V, MLA_H = 256, 128, 32, 64, 64, 4
MLA_QK = MLA_NOPE + MLA_PE
GQA_Q, GQA_KV, HD = 4, 2, 64
ML_H = 4
ML_W = ML_H * HD
HY_W = 256
O_GQA = MLA_Q + MLA_KV + MLA_PE
O_ML = O_GQA + (GQA_Q + 2 * GQA_KV) * HD
O_HY = O_ML + 4 * ML_W + 4 * ML_H
O_GATE = O_HY + 3 * HY_W
N_BRANCH = 4

PH, NK, TOPK = 8, 128, 16
HC = 2 * PH

V_ADAB, V_N1, V_N2, V_CONV, V_HYB = 0, 48, 56, 64, 82
V_MQ, V_MKV, V_MLN, V_QKQ, V_QKK, V_GQ, V_GK = 86, 88, 89, 91, 92, 93, 94
V_B1, V_B2, V_FREQ, V_ROWS = 95, 96, 97, 99

(C_ID, C_ONES, C_BONES, C_TRI_F, C_TRI_B, C_STR_F, C_STR_B, C_NEG_F, C_NEG_B, C_ROT_M, C_ROT_G, C_IOTA,
 C_N) = range(13)


NUMBER = [0, 0]


@contextmanager
def stage(nc, *names):
    NUMBER[0] += 1
    sems = [nc.alloc_semaphore(f"{n}_{NUMBER[0]}") for n in names]
    with nc.Block() as block:
        yield (block, *sems)
    nc.clear_and_free_semaphores(sems)
    nc.all_engine_barrier()


def sbuf(nc, name, shape, dtype):
    NUMBER[1] += 1
    return nc.sbuf_tensor(f"{name}_{NUMBER[1]}", shape, dtype)


class Chain:

    def __init__(self, eng, sem):
        self.eng, self.sem, self.n = eng, sem, 0

    def step(self, ins):
        self.n += 1
        ins.then_inc(self.sem, 1)

    def meet(self):
        self.eng.wait_ge(self.sem, self.n)

    def link(self, ins):
        self.step(ins)
        self.meet()


def split_matmul(nc, out, left, right, first, last):
    nc.tensor.matmul(out, left(0), right(0), start=first, stop=False)
    nc.tensor.matmul(out, left(0), right(1), start=False, stop=False)
    return nc.tensor.matmul(out, left(1), right(0), start=False, stop=last)


class Mem:
    pass


@contextmanager
def weight_ring(nc, width):
    ring = Mem()
    with ExitStack() as ctx:
        ring.raw = ctx.enter_context(sbuf(nc, "ring_raw", [P, 2, KD, width], F32))
        ring.split = [ctx.enter_context(sbuf(nc, f"ring_split{r}", [P, 2, KD, width], F32R)) for r in range(2)]
        yield ring


def columns(weights, bounds):
    w = weights.rearrange("(k p) n -> p k n", p=P)
    return [w[:, :, lo:hi] for lo, hi in zip(bounds, bounds[1:])]




def setup(nc, m, d):
    with ExitStack() as ctx:
        tok = ctx.enter_context(sbuf(nc, "tok", [P, NB, D], F32))
        crow = ctx.enter_context(sbuf(nc, "crow", [2 * KD, P], F32))
        craw = ctx.enter_context(sbuf(nc, "craw", [P, 2 * KD], F32))
        cexp = ctx.enter_context(sbuf(nc, "cexp", [P, 2 * KD], F32))
        (block, consts_in, tok_in, c_in, tok_turned, c_turned, resid_by_act, c_exp, c_copied, dve_own, act_own) = (
            ctx.enter_context(stage(nc, "consts_in", "tok_in", "c_in", "tok_turned", "c_turned", "resid_by_act",
                                    "c_exp", "c_copied", "dve_own", "act_own")))

        @block.sync
        def _(sp):
            sp.dma_start(m.sq[:, :, :], d["k_square"].rearrange("(c p) n -> p c n", p=P)).then_inc(consts_in, 16)
            sp.dma_start(tok[:, 0:2, :], d["ctx"][0].rearrange("(b p) n -> p b n", p=P)).then_inc(tok_in, 16)
            sp.dma_start(tok[:, 2:4, :], d["x"][0].rearrange("(b p) n -> p b n", p=P)).then_inc(tok_in, 16)
            sp.dma_start(crow[0:KD, :], d["c"].rearrange("o (k p) -> (o k) p", p=P)).then_inc(c_in, 16)
            sp.dma_start(crow[KD:, :], d["c_ctx"].rearrange("(k p) -> k p", p=P)).then_inc(c_in, 16)

        @block.tensor
        def _(pe):
            pe.wait_ge(consts_in, 16)
            pe.wait_ge(c_in, 32)
            nc.tensor.transpose(m.ps[:, 7, 0:2 * KD], crow[:, :], m.sq[0:2 * KD, C_ID, 0:2 * KD]).then_inc(c_turned, 1)
            pe.wait_ge(tok_in, 32)
            for k in range(KD):
                if k >= 4:
                    pe.wait_ge(resid_by_act, k - 3)
                for b in range(NB):
                    ins = nc.tensor.transpose(m.ps[:, k % 4, b * P:(b + 1) * P], tok[:, b, k * P:(k + 1) * P],
                                              m.sq[:, C_ID, :])
                ins.then_inc(tok_turned, 1)

        @block.scalar
        def _(act):
            act.wait_ge(c_turned, 1)
            act.wait_ge(c_copied, 1)
            nc.scalar.activation(cexp[:, :], craw[:, :], ACT.Exp, scale=-1.0).then_inc(c_exp, 1)
            for k in range(KD):
                act.wait_ge(tok_turned, k + 1)
                nc.scalar.copy(m.resid[:, k, :], m.ps[:, k % 4, :]).then_inc(resid_by_act, 1)

        @block.vector
        def _(dve):
            own = Chain(dve, dve_own)
            own.step(nc.vector.memset(m.eps[:, :], EPS))
            dve.wait_ge(c_turned, 1)
            nc.vector.tensor_copy(craw[:, :], m.ps[:, 7, 0:2 * KD]).then_inc(c_copied, 1)
            dve.wait_ge(c_copied, 1)
            dve.wait_ge(c_exp, 1)
            own.link(nc.vector.tensor_scalar(cexp[:, :], cexp[:, :], 1.0, None, ALU.add))
            own.link(nc.vector.reciprocal(cexp[:, :], cexp[:, :]))
            own.link(nc.vector.tensor_tensor(m.cond[:, :, :].rearrange("p k r -> p r k"),
                                             craw[:, :].rearrange("p (r k) -> p r k", r=2),
                                             cexp[:, :].rearrange("p (r k) -> p r k", r=2), ALU.mult))



MCH = 256


class SideModulation:

    def __init__(self, nc, m, weights, lo, hi, raw, row, banks, turned_bank, ins, passed, mult, out, turned):
        self.nc, self.m, self.lo, self.n = nc, m, lo, (hi - lo) // MCH
        self.weights = weights.rearrange("(k p) n -> p k n", p=P)
        self.raw, self.row, self.banks, self.turned_bank = raw, row, banks, turned_bank
        self.ins, self.passed, self.mult, self.out, self.turned = ins, passed, mult, out, turned

    def load(self, sp, j):
        if j >= 2:
            sp.wait_ge(self.mult, j - 1)
        at = self.lo + j * MCH
        sp.dma_start(self.raw[:, j % 2, :, :], self.weights[:, :, at:at + MCH]).then_inc(self.ins[j % 2], 16)

    def multiply(self, pe, j):
        nc, m = self.nc, self.m
        pe.wait_ge(self.ins[j % 2], 16 * ((self.passed + j) // 2 + 1))
        if j >= 2:
            pe.wait_ge(self.out, j - 1)
        for k in range(KD):
            ins = nc.tensor.matmul(m.ps[0:2, self.banks[j % 2], 0:MCH], m.cond[:, k, :], self.raw[:, j % 2, k, :],
                                   start=(k == 0), stop=(k == KD - 1))
        ins.then_inc(self.mult, 1)
        if j >= 1:
            self.turn(pe, j - 1)

    def turn(self, pe, j):
        nc, m = self.nc, self.m
        pe.wait_ge(self.out, j + 1)
        for q in range(MCH // P):
            at = 2 * (j * (MCH // P) + q)
            ins = nc.tensor.transpose(m.ps[:, self.turned_bank, at:at + 2], self.row[:, j % 2, q * P:(q + 1) * P],
                                      m.sq[0:2, C_ID, 0:2])
        ins.then_inc(self.turned, 1)

    def copy(self, act, j):
        nc, m = self.nc, self.m
        act.wait_ge(self.mult, j + 1)
        if j >= 2:
            act.wait_ge(self.turned, j - 1)
        nc.scalar.copy(self.row[:, j % 2, :], m.ps[0:2, self.banks[j % 2], 0:MCH]).then_inc(self.out, 1)


def finish_modulation(nc, m, own, mod, products, lo, hi):
    own.link(nc.vector.tensor_tensor(
        mod[:, lo:hi, :], products.rearrange("p (j r) -> p j r", r=2),
        m.vec[:, V_ADAB + lo:V_ADAB + hi].unsqueeze(2).to_broadcast([P, hi - lo, 2]), ALU.add))
    for v, at in ((V_N1, KD), (V_N2, 4 * KD)):
        if lo <= at < hi:
            own.link(nc.vector.tensor_scalar(mod[:, at:at + KD, :], mod[:, at:at + KD, :], 1.0, None, ALU.add))
            own.link(nc.vector.tensor_tensor(mod[:, at:at + KD, :], mod[:, at:at + KD, :],
                                             m.vec[:, v:v + KD].unsqueeze(2).to_broadcast([P, KD, 2]), ALU.mult))


def small_vectors(d, l):
    return [
        (V_ADAB, 48, P, d["ada_b"][l].rearrange("(k p) -> k p", p=P), 0),
        (V_N1, 8, P, d["norm1"][l].rearrange("(k p) -> k p", p=P), 0),
        (V_N2, 8, P, d["norm2"][l].rearrange("(k p) -> k p", p=P), 0),
        (V_CONV, 18, P, d["hy_conv"][l].rearrange("j (k p) -> (j k) p", p=P), 0),
        (V_HYB, 4, P, d["hy_bias"][l].rearrange("j (k p) -> (j k) p", p=P), 0),
        (V_MQ, 2, P, d["mla_q_norm"][l].rearrange("(k p) -> k p", p=P), 0),
        (V_MKV, 1, P, d["mla_kv_norm"][l].rearrange("(k p) -> k p", p=P), 0),
        (V_MLN, 2, P, d["ml_norm"][l].rearrange("(a b) e -> a (b e)", b=2), 0),
        (V_QKQ, 1, MLA_QK, d["mla_qk_norm_q"][l:l + 1, :], 0),
        (V_QKK, 1, MLA_QK, d["mla_qk_norm_k"][l:l + 1, :], 0),
        (V_GQ, 1, HD, d["gqa_qk_norm_q"][l:l + 1, :], 0),
        (V_GQ, 1, HD, d["gqa_qk_norm_q"][l:l + 1, :], HD),
        (V_GK, 1, HD, d["gqa_qk_norm_k"][l:l + 1, :], 0),
        (V_GK, 1, HD, d["gqa_qk_norm_k"][l:l + 1, :], HD),
        (V_B1, 1, HD, d["hy_b1"][l:l + 1, :], 0),
        (V_B2, 1, HD, d["hy_b2"][l:l + 1, :], 0),
        (V_FREQ, 2, HD, d["hy_freq"][l], 0),
    ]


def modulation(nc, m, d):
    CH = 512
    NCH = 2 * D // CH
    RING = 3
    vecs = small_vectors(d, 0)
    with ExitStack() as ctx:
        vrow = ctx.enter_context(sbuf(nc, "vrow", [P, P], F32))
        wada = ctx.enter_context(sbuf(nc, "wada", [P, RING, KD, CH], F32))
        mrow = ctx.enter_context(sbuf(nc, "mrow", [2, 2 * D], F32))
        (block, zeroed, vecs_in, chunk_mult, row_out, vecs_turned, mods_turned, dve_own, *w_ins) = (
            ctx.enter_context(stage(nc, "zeroed", "vecs_in", "chunk_mult", "row_out", "vecs_turned",
                                    "mods_turned", "dve_own", *[f"w_in{r}" for r in range(RING)])))

        @block.sync
        def _(sp):
            for c in range(NCH):
                if c >= RING:
                    sp.wait_ge(chunk_mult, c - RING + 1)
                sp.dma_start(wada[:, c % RING, :, :],
                             d["ada_w"][0].rearrange("(k p) n -> p k n", p=P)[:, :, c * CH:(c + 1) * CH]
                             ).then_inc(w_ins[c % RING], 16)
            sp.wait_ge(zeroed, 1)
            for at, n, w, src, c0 in vecs[:len(vecs) // 2]:
                sp.dma_start(vrow[at:at + n, c0:c0 + w], src).then_inc(vecs_in, 16)

        @block.scalar
        def _(act):
            act.wait_ge(zeroed, 1)
            for at, n, w, src, c0 in vecs[len(vecs) // 2:]:
                act.dma_start(vrow[at:at + n, c0:c0 + w], src).then_inc(vecs_in, 16)
            for c in range(NCH):
                act.wait_ge(chunk_mult, c + 1)
                nc.scalar.copy(mrow[:, c * CH:(c + 1) * CH], m.ps[0:2, c % 2, :]).then_inc(row_out, 1)

        @block.tensor
        def _(pe):
            def turn(c):
                pe.wait_ge(row_out, c + 1)
                for q in range(CH // P):
                    j = c * (CH // P) + q
                    ins = nc.tensor.transpose(m.ps[:, 7, 2 * j:2 * j + 2], mrow[:, j * P:(j + 1) * P],
                                              m.sq[0:2, C_ID, 0:2])
                ins.then_inc(mods_turned, 1)

            for c in range(NCH):
                pe.wait_ge(w_ins[c % RING], 16 * (c // RING + 1))
                if c >= 2:
                    pe.wait_ge(row_out, c - 1)
                for k in range(KD):
                    ins = nc.tensor.matmul(m.ps[0:2, c % 2, :], m.cond[:, k, :], wada[:, c % RING, k, :],
                                           start=(k == 0), stop=(k == KD - 1))
                ins.then_inc(chunk_mult, 1)
                if c >= 1:
                    turn(c - 1)
            turn(NCH - 1)
            pe.wait_ge(vecs_in, 16 * len(vecs))
            nc.tensor.transpose(m.ps[:, 6, 0:P], vrow[:, :], m.sq[:, C_ID, :]).then_inc(vecs_turned, 1)

        @block.vector
        def _(dve):
            own = Chain(dve, dve_own)
            nc.vector.memset(vrow[:, :], 0.0).then_inc(zeroed, 1)
            dve.wait_ge(vecs_turned, 1)
            own.link(nc.vector.tensor_copy(m.vec[:, :], m.ps[:, 6, 0:V_ROWS]))
            dve.wait_ge(mods_turned, NCH)
            finish_modulation(nc, m, own, m.mod, m.ps[:, 7, 0:4 * KD], 0, 2 * KD)


def mod_norm(nc, m, hs, at, t0, ring, chunks):
    T = TOK - t0
    halves = [(kind, lo, hi) for kind, lo, hi in ((1, 0, CTX), (0, CTX, TOK)) if lo >= t0]
    with ExitStack() as ctx:
        sq = ctx.enter_context(sbuf(nc, "sq", [P, 3, TOK], F32))
        rs = ctx.enter_context(sbuf(nc, "rs", [P, TOK], F32))
        xn = ctx.enter_context(sbuf(nc, "xn", [P, TOK], F32))
        h = ctx.enter_context(sbuf(nc, "h", [P, 3, TOK], F32))
        (block, squared, summed, scaled, rooted, normed, rounded, rested, dve_own, w_in0, w_in1, w_rounded
         ) = ctx.enter_context(stage(nc, "squared", "summed", "scaled", "rooted", "normed", "rounded", "rested",
                                     "dve_own", "w_in0", "w_in1", "w_rounded"))
        w_ins = (w_in0, w_in1)
        width = chunks[0].shape[2]
        raw = [ring.raw[:, c, :, 0:width] for c in range(2)]
        split = [ring.split[c][:, :, :, 0:width] for c in range(2)]

        @block.sync
        def _(sp):
            for c in range(2):
                sp.dma_start(raw[c], chunks[c]).then_inc(w_ins[c], 16)

        @block.scalar
        def _(act):
            for k in range(KD):
                if k >= 3:
                    act.wait_ge(summed, k - 2)
                nc.scalar.activation(sq[:, k % 3, t0:], m.resid[:, k, t0:], ACT.Square).then_inc(squared, 1)
            act.wait_ge(scaled, 1)
            nc.scalar.activation(rs[:, t0:], rs[:, t0:], ACT.Sqrt).then_inc(rooted, 1)
            for c in range(2):
                act.wait_ge(w_ins[c], 16)
                nc.scalar.copy(split[c][:, 0], raw[c]).then_inc(w_rounded, 1)
            for k in range(KD):
                act.wait_ge(normed, k + 1)
                nc.scalar.copy(hs[:, 0, k, t0:], h[:, k % 3, t0:]).then_inc(rounded, 1)

        @block.gpsimd
        def _(pool):
            pool.wait_ge(w_rounded, 1)
            nc.gpsimd.tensor_tensor(split[0][:, 1], raw[0], split[0][:, 0].bitcast(F32), ALU.subtract)
            for k in range(KD):
                pool.wait_ge(rounded, k + 1)
                nc.gpsimd.tensor_tensor(hs[:, 1, k, t0:], h[:, k % 3, t0:], hs[:, 0, k, t0:].bitcast(F32),
                                        ALU.subtract).then_inc(rested, 1)

        @block.tensor
        def _(pe):
            for k in range(KD):
                pe.wait_ge(squared, k + 1)
                nc.tensor.matmul(m.ps[:, 0, 0:T], m.sq[:, C_ONES, :], sq[:, k % 3, t0:], start=(k == 0),
                                 stop=(k == KD - 1)).then_inc(summed, 1)

        @block.vector
        def _(dve):
            own = Chain(dve, dve_own)

            dve.wait_ge(summed, KD)
            nc.vector.tensor_scalar(rs[:, t0:], m.ps[:, 0, 0:T], 1.0 / D, EPS, ALU.mult, ALU.add).then_inc(scaled, 1)
            dve.wait_ge(rooted, 1)
            own.link(nc.vector.reciprocal(rs[:, t0:], rs[:, t0:]))
            for k in range(KD):
                if k >= 1:
                    dve.wait_ge(normed, k)
                own.link(nc.vector.tensor_tensor(xn[:, t0:], m.resid[:, k, t0:], rs[:, t0:], ALU.mult))
                if k >= 3:
                    dve.wait_ge(rested, k - 2)
                for kind, lo, hi in halves:
                    ins = nc.vector.tensor_scalar(h[:, k % 3, lo:hi], xn[:, lo:hi],
                                                  m.mod[:, at + KD + k, kind:kind + 1],
                                                  m.mod[:, at + k, kind:kind + 1], ALU.mult, ALU.add)
                ins.then_inc(normed, 1)




CW = 272


def input_projection(nc, m, d, hs, t, l, q0, ring):
    wide = lambda dst: [(dst, slice(0, P))]
    chunks = [
        (0, 256, [(P * g, wide(t.cq[:, g, :]), q0) for g in range(2)], []),
        (256, 256, [
            (256, wide(t.ckv[:, :]), 0),
            (384, [(t.kpe[64:96, :], slice(0, MLA_PE))], 0)], []),
        (O_GQA, 256, [
            (O_GQA, [(t.gq[0:64, 0, :], slice(0, 64)), (t.gq[0:64, 1, :], slice(64, P))], q0),
            (O_GQA + P, [(t.gq[64:128, 0, :], slice(0, 64)), (t.gq[64:128, 1, :], slice(64, P))], q0)], []),
        (O_GQA + 256, 256, [(O_GQA + 256, wide(t.gk[:, :]), 0)], [(O_GQA + 384, P, t.gv[:, :, :], False)]),
        (O_ML, 256, [(O_ML + P * g, wide(t.mq[:, g, :]), q0) for g in range(2)], []),
        (O_ML + 256, 256, [(O_ML + 256 + P * g, wide(t.mk[:, g, :]), 0) for g in range(2)], []),
        (O_ML + 512, 256, [], [(O_ML + 512, ML_W, t.mvo[:, :, 0:ML_W], False)]),
        (O_ML + 768, 272, [], [
            (O_ML + 768, ML_W, t.mvo[:, :, ML_W:], False),
            (O_ML + 1024, 16, t.mg[:, :, :], True)]),
    ] + [(O_HY + 256 * c, 256, [(O_HY + P * g, wide(t.hy[:, g, :]), q0) for g in (2 * c, 2 * c + 1)], [])
         for c in range(3)]
    groups = []
    for c, (_, _, fm, tm) in enumerate(chunks):
        groups += [(c, "fm", g, None) for g in fm]
        groups += [(c, "tm", g, b) for b in range(NB) for g in tm]
    last_of = {c: max(i for i, g in enumerate(groups) if g[0] == c) + 1 for c in range(len(chunks))}
    with ExitStack() as ctx:
        raw, w = ring.raw, ring.split
        gbias = ctx.enter_context(sbuf(nc, "gbias", [1, 16], F32))
        (block, heads_in, bias_in, group_mult, act_out, dve_out, w_rounded, w_rested, w_in0, w_in1) = ctx.enter_context(
            stage(nc, "heads_in", "bias_in", "group_mult", "act_out", "dve_out", "w_rounded", "w_rested", "w_in0", "w_in1"))
        w_ins = (w_in0, w_in1)

        @block.sync
        def _(sp):
            sp.dma_start(gbias[:, :], d["ml_gate_b"][l:l + 1].rearrange("o a h -> o (a h)")).then_inc(bias_in, 16)
            for c, (c0, n, _, _) in list(enumerate(chunks))[2:]:
                if c >= 3:
                    sp.wait_ge(w_rested, c - 2)
                sp.dma_start(raw[:, c % 2, :, 0:n], d["w_in"][l].rearrange("(k p) n -> p k n", p=P)[:, :, c0:c0 + n]
                             ).then_inc(w_ins[c % 2], 16)
            sp.dma_start(t.wuq[:, :, :], d["mla_w_uq"][l].rearrange("(k p) n -> p k n", p=P)).then_inc(heads_in, 16)
            sp.dma_start(t.wukv[:, :], d["mla_w_ukv"][l]).then_inc(heads_in, 16)
            sp.dma_start(t.rope[:, :, :], d["k_rope"].rearrange("(c p) n -> p c n", p=P)).then_inc(heads_in, 16)
            sp.wait_ge(heads_in, 48)

        @block.gpsimd
        def _(pool):
            for c, (_, n, _, _) in list(enumerate(chunks))[1:]:
                if c >= 2:
                    pool.wait_ge(w_rounded, c - 1)
                nc.gpsimd.tensor_tensor(w[c % 2][:, 1, :, 0:n], raw[:, c % 2, :, 0:n],
                                        w[c % 2][:, 0, :, 0:n].bitcast(F32), ALU.subtract).then_inc(w_rested, 1)

        @block.tensor
        def _(pe):
            pe.wait_ge(bias_in, 16)
            seen = 0
            for i, (c, kind, grp, b) in enumerate(groups):
                if c > seen:
                    seen = c
                    pe.wait_ge(w_rested, c)
                if i >= BANKS:
                    pe.wait_ge(dve_out if i % 2 else act_out, (i - BANKS) // 2 + 1)
                at = grp[0] - chunks[c][0]
                if kind == "fm":
                    t0 = grp[2]
                    out = m.ps[:, i % BANKS, 0:TOK - t0]
                    for k in range(KD):
                        ins = split_matmul(nc, out, lambda r: w[c % 2][:, r, k, at:at + P],
                                           lambda r: hs[:, r, k, t0:], k == 0, k == KD - 1)
                else:
                    _, n, _, biased = grp
                    out = m.ps[:, i % BANKS, 0:n]
                    for k in range(KD):
                        ins = split_matmul(nc, out, lambda r: hs[:, r, k, b * P:(b + 1) * P],
                                           lambda r: w[c % 2][:, r, k, at:at + n], k == 0,
                                           k == KD - 1 and not biased)
                    if biased:
                        ins = nc.tensor.matmul(out, m.sq[0:1, C_ONES, :], gbias[:, :], start=False, stop=True)
                ins.then_inc(group_mult, 1)

        def out_of(i):
            _, kind, grp, b = groups[i]
            if kind == "tm":
                return [(grp[2][:, b, :], m.ps[:, i % BANKS, 0:grp[1]])]
            _, dsts, t0 = grp
            return [(x[:, t0:], m.ps[rows, i % BANKS, 0:TOK - t0]) for x, rows in dsts]

        @block.scalar
        def _(act):
            def round_chunk(c):
                act.wait_ge(w_ins[c % 2], 16 * (c // 2))
                act.wait_ge(group_mult, last_of[c - 2])
                nc.scalar.copy(w[c % 2][:, 0, :, 0:chunks[c][1]], raw[:, c % 2, :, 0:chunks[c][1]]).then_inc(w_rounded, 1)

            nxt = 2
            for i in range(0, len(groups), 2):
                act.wait_ge(group_mult, i + 1)
                for dst, src in out_of(i):
                    ins = nc.scalar.copy(dst, src)
                ins.then_inc(act_out, 1)
                while nxt < len(chunks) and last_of[nxt - 2] <= i + 2:
                    round_chunk(nxt)
                    nxt += 1

        @block.vector
        def _(dve):
            for i in range(1, len(groups), 2):
                dve.wait_ge(group_mult, i + 1)
                for dst, src in out_of(i):
                    ins = nc.vector.tensor_copy(dst, src)
                ins.then_inc(dve_out, 1)




def attention_heads(nc, m, d, t, l, q0):
    with ExitStack() as ctx:
        wuq, wukv, rope = t.wuq, t.wukv, t.rope
        lat = ctx.enter_context(sbuf(nc, "lat", [P, 3, TOK], F32))
        sq = ctx.enter_context(sbuf(nc, "sq", [P, 3, TOK], F32))
        rs = ctx.enter_context(sbuf(nc, "rs", [P, 3, TOK], F32))
        xn = ctx.enter_context(sbuf(nc, "xn", [P, 2, TOK], F32))
        xc = ctx.enter_context(sbuf(nc, "xc", [P, 2, TOK], F32))
        m_raw = ctx.enter_context(sbuf(nc, "ada_w", [P, 2, KD, MCH], F32))
        m_row = ctx.enter_context(sbuf(nc, "mod_row", [2, 2, MCH], F32))
        (block, lat_sq, lat_sum, lat_scaled, lat_root, lat_done, up_mult, up_out, v_out, x_sq, x_sum,
         x_root, x_normed, x_rot, x_cos, x_sin, x_done, dve_own, m_in0, m_in1, m_mult, m_out, m_turned) = ctx.enter_context(stage(
            nc, "lat_sq", "lat_sum", "lat_scaled", "lat_root", "lat_done", "up_mult", "up_out", "v_out",
            "x_sq", "x_sum", "x_root", "x_normed", "x_rot", "x_cos", "x_sin", "x_done", "dve_own",
            "m_in0", "m_in1", "m_mult", "m_out", "m_turned"))
        lats = [(t.cq[:, 0, :], V_MQ, q0), (t.cq[:, 1, :], V_MQ + 1, q0), (t.ckv[:, :], V_MKV, 0)]
        tiles = ([(t.qm[0:MLA_QK, h, :], MLA_QK, V_QKQ, q0, 0, C_ROT_M) for h in range(MLA_H)]
                 + [(t.km[0:MLA_QK, h, :], MLA_QK, V_QKK, 0, 0, C_ROT_M) for h in range(MLA_H)]
                 + [(t.gq[:, a, :], P, V_GQ, q0, 2, C_ROT_G) for a in range(2)]
                 + [(t.gk[:, :], P, V_GK, 0, 2, C_ROT_G)])
        sums = (0, 1, 4)
        side = SideModulation(nc, m, d["ada_w"][l], 2 * D, 6 * D, m_raw, m_row, (5, 6), 7, (m_in0, m_in1), 0, m_mult,
                              m_out, m_turned)
        share = lambda i: range(i * side.n // len(tiles), (i + 1) * side.n // len(tiles)) if l == 0 else ()

        @block.sync
        def _(sp):
            for i in range(len(tiles)):
                for j in share(i):
                    side.load(sp, j)

        @block.scalar
        def _(act):
            for i, (x, _, t0) in enumerate(lats):
                nc.scalar.activation(sq[:, i, t0:], x[:, t0:], ACT.Square).then_inc(lat_sq, 1)
            for i, t0 in ((0, q0), (1, 0)):
                act.wait_ge(lat_scaled, i + 1)
                nc.scalar.activation(rs[:, i, t0:], rs[:, i, t0:], ACT.Sqrt).then_inc(lat_root, 1)
            for h in range(MLA_H):
                nc.scalar.copy(t.km[64:96, h, :], t.kpe[64:96, :])
            for h in range(MLA_H):
                act.wait_ge(up_mult, 2 * h + 1)
                nc.scalar.copy(t.qm[0:MLA_QK, h, q0:], m.ps[0:MLA_QK, 2 + 2 * (h % 2), q0 - q0:TOK - q0])
                act.wait_ge(up_mult, 2 * h + 2)
                nc.scalar.copy(t.km[0:MLA_NOPE, h, :], m.ps[0:MLA_NOPE, 3 + 2 * (h % 2), :]).then_inc(up_out, 1)
            act.wait_ge(up_out, MLA_H)
            act.wait_ge(lat_sum, 3)
            act.wait_ge(lat_done, 3)

            def square(i):
                x, rows, _, t0, _, _ = tiles[i]
                if i >= 3:
                    act.wait_ge(x_sum, i - 2)
                nc.scalar.activation(sq[0:rows, i % 3, t0:], x[:, t0:], ACT.Square).then_inc(x_sq, 1)

            square(0)
            square(1)
            for i, (x, rows, _, t0, _, _) in enumerate(tiles):
                if i + 2 < len(tiles):
                    square(i + 2)
                act.wait_ge(x_sum, i + 1)
                if i >= 3:
                    act.wait_ge(x_normed, i - 2)
                nc.scalar.activation(rs[0:rows, i % 3, t0:], m.ps[0:rows, sums[i % 3], 0:TOK - t0], ACT.Sqrt,
                                     scale=1.0 / (MLA_QK if rows == MLA_QK else HD), bias=m.eps[0:rows, :]
                                     ).then_inc(x_root, 1)
                for j in share(i):
                    side.copy(act, j)

        @block.gpsimd
        def _(pool):
            for i, (x, rows, _, t0, table, _) in enumerate(tiles):
                pool.wait_ge(x_normed, i + 1)
                nc.gpsimd.tensor_tensor(x[:, t0:], xn[0:rows, i % 2, t0:], rope[0:rows, table, t0:], ALU.mult
                                        ).then_inc(x_cos, 1)
                pool.wait_ge(x_cos, i + 1)
                pool.wait_ge(x_sin, i + 1)
                nc.gpsimd.tensor_tensor(x[:, t0:], x[:, t0:], xc[0:rows, i % 2, t0:], ALU.add).then_inc(x_done, 1)

        @block.tensor
        def _(pe):
            pe.wait_ge(lat_sq, 2)
            for i in range(2):
                nc.tensor.matmul(m.ps[:, 0, 0:TOK - q0], m.sq[:, C_ONES, :], sq[:, i, q0:], start=(i == 0),
                                 stop=(i == 1)).then_inc(lat_sum, 1)
            pe.wait_ge(lat_sq, 3)
            nc.tensor.matmul(m.ps[:, 1, :], m.sq[:, C_ONES, :], sq[:, 2, :], start=True, stop=True).then_inc(lat_sum, 1)
            pe.wait_ge(lat_done, 3)
            W = MLA_NOPE + MLA_V
            for h in range(MLA_H):
                if h >= 2:
                    pe.wait_ge(up_out, h - 1)
                for k in range(2):
                    ins = nc.tensor.matmul(m.ps[0:MLA_QK, 2 + 2 * (h % 2), 0:TOK - q0],
                                           wuq[:, k, h * MLA_QK:(h + 1) * MLA_QK], lat[:, k, q0:], start=(k == 0),
                                           stop=(k == 1))
                ins.then_inc(up_mult, 1)
                nc.tensor.matmul(m.ps[0:MLA_NOPE, 3 + 2 * (h % 2), :], wukv[:, h * W:h * W + MLA_NOPE],
                                 lat[:, 2, :], start=True, stop=True).then_inc(up_mult, 1)
            vcols = wukv[:, :].rearrange("p (h c) -> p h c", h=MLA_H)[:, :, MLA_NOPE:]
            for b in range(NB):
                if b >= 2:
                    pe.wait_ge(v_out, b - 1)
                nc.tensor.matmul(m.ps[:, 6 + b % 2, 0:MLA_H * MLA_V], lat[:, 2, b * P:(b + 1) * P], vcols,
                                 start=True, stop=True).then_inc(up_mult, 1)

            def rotate(i):
                x, rows, _, t0, _, rot = tiles[i]
                pe.wait_ge(x_normed, i + 1)
                nc.tensor.matmul(m.ps[0:rows, 2 + i % 2, 0:TOK - t0], m.sq[0:rows, rot, 0:rows], xn[0:rows, i % 2, t0:],
                                 start=True, stop=True).then_inc(x_rot, 1)

            def total(i):
                x, rows, _, t0, _, rot = tiles[i]
                pe.wait_ge(x_sq, i + 1)
                if i >= 3:
                    pe.wait_ge(x_root, i - 2)
                ones = m.sq[0:rows, C_BONES if rows == P else C_ONES, 0:rows]
                nc.tensor.matmul(m.ps[0:rows, sums[i % 3], 0:TOK - t0], ones, sq[0:rows, i % 3, t0:], start=True,
                                 stop=True).then_inc(x_sum, 1)

            total(0)
            total(1)
            pe.wait_ge(v_out, NB)
            for i in range(len(tiles)):
                if i + 2 < len(tiles):
                    total(i + 2)
                for j in share(i):
                    side.multiply(pe, j)
                rotate(i)
            if l == 0:
                side.turn(pe, side.n - 1)

        @block.vector
        def _(dve):
            own = Chain(dve, dve_own)
            for i, (n, t0, width) in enumerate(((2, q0, MLA_Q), (3, 0, MLA_KV))):
                dve.wait_ge(lat_sum, n)
                nc.vector.tensor_scalar(rs[:, i, t0:], m.ps[:, i, 0:TOK - t0], 1.0 / width, EPS, ALU.mult,
                                        ALU.add).then_inc(lat_scaled, 1)
            for i, t0 in ((0, q0), (1, 0)):
                dve.wait_ge(lat_root, i + 1)
                own.link(nc.vector.reciprocal(rs[:, i, t0:], rs[:, i, t0:]))
            for i, (x, v, t0) in enumerate(lats):
                nc.vector.scalar_tensor_tensor(out=lat[:, i, t0:], in0=x[:, t0:], scalar=m.vec[:, v:v + 1],
                                               in1=rs[:, i // 2, t0:], op0=ALU.mult, op1=ALU.mult
                                               ).then_inc(lat_done, 1)
            for b in range(NB):
                dve.wait_ge(up_mult, 2 * MLA_H + b + 1)
                nc.vector.tensor_copy(t.vm[:, b, :], m.ps[:, 6 + b % 2, 0:MLA_H * MLA_V]).then_inc(v_out, 1)

            def sine(i):
                _, rows, _, t0, table, _ = tiles[i]
                dve.wait_ge(x_rot, i + 1)
                if i >= 2:
                    dve.wait_ge(x_done, i - 1)
                nc.vector.tensor_tensor(xc[0:rows, i % 2, t0:], m.ps[0:rows, 2 + i % 2, 0:TOK - t0],
                                        rope[0:rows, table + 1, t0:], ALU.mult).then_inc(x_sin, 1)

            for i, (x, rows, v, t0, table, _) in enumerate(tiles):
                dve.wait_ge(x_root, i + 1)
                own.link(nc.vector.reciprocal(rs[0:rows, i % 3, t0:], rs[0:rows, i % 3, t0:]))
                if i >= 2:
                    dve.wait_ge(x_cos, i - 1)
                nc.vector.scalar_tensor_tensor(out=xn[0:rows, i % 2, t0:], in0=x[:, t0:], scalar=m.vec[0:rows, v:v + 1],
                                               in1=rs[0:rows, i % 3, t0:], op0=ALU.mult, op1=ALU.mult
                                               ).then_inc(x_normed, 1)
                if i >= 1:
                    sine(i - 1)
            sine(len(tiles) - 1)
            if l == 0:
                dve.wait_ge(m_turned, side.n)
                finish_modulation(nc, m, own, m.mod, m.ps[:, 7, 0:8 * KD], 2 * KD, 6 * KD)




def attention(nc, m, t, blocks):
    SC = {0: MLA_QK ** -0.5, 1: HD ** -0.5}
    units = []
    for h in range(4):
        half = 64 * (h % 2)
        for b in blocks:
            qs = slice(b * P, (b + 1) * P)
            units.append((0, t.qm[0:MLA_QK, h, qs], lambda n, h=h: t.km[0:MLA_QK, h, 0:n],
                          lambda kb, h=h: t.vm[:, kb, h * HD:(h + 1) * HD], t.yT[half:half + 64, 0, h // 2, qs], b, half))
    for h in range(4):
        half, kv = 64 * (h % 2), h // 2
        for b in blocks:
            qs = slice(b * P, (b + 1) * P)
            units.append((1, t.gq[64 * kv:64 * kv + 64, h % 2, qs],
                          lambda n, kv=kv: t.gk[64 * kv:64 * kv + 64, 0:n],
                          lambda kb, kv=kv: t.gv[:, kb, kv * HD:(kv + 1) * HD],
                          t.yT[half:half + 64, 1, h // 2, qs], b, half))
    N = len(units)
    nkeys = lambda b: CTX if b < CTX // P else TOK
    with ExitStack() as ctx:
        pr = ctx.enter_context(sbuf(nc, "probs", [P, 2, TOK], F32))
        pt = ctx.enter_context(sbuf(nc, "probsT", [P, 2, TOK], F32))
        st = ctx.enter_context(sbuf(nc, "stat", [P, 3, N], F32))
        (block, scored, maxed, exped, normed, turned, turn_out, summed, y_out, dve_own) = ctx.enter_context(stage(
            nc, "scored", "maxed", "exped", "normed", "turned", "turn_out", "summed", "y_out", "dve_own"))

        @block.tensor
        def _(pe):
            def score(u):
                _, q, k, _, _, b, _ = units[u]
                if u >= 3:
                    pe.wait_ge(exped, u - 2)
                nc.tensor.matmul(m.ps[:, u % 3, 0:nkeys(b)], q, k(nkeys(b)), start=True, stop=True).then_inc(scored, 1)

            def turn(u):
                b = units[u][5]
                pe.wait_ge(normed, u + 1)
                if u >= 2:
                    pe.wait_ge(turn_out, u - 1)
                for kb in range(nkeys(b) // P):
                    ins = nc.tensor.transpose(m.ps[:, 3 + u % 2, kb * P:(kb + 1) * P], pr[:, u % 2, kb * P:(kb + 1) * P],
                                              m.sq[:, C_ID, :])
                ins.then_inc(turned, 1)

            def values(u):
                _, _, _, v, _, b, half = units[u]
                pe.wait_ge(turn_out, u + 1)
                if u >= 2:
                    pe.wait_ge(y_out, u - 1)
                n = nkeys(b) // P
                for kb in range(n):
                    ins = nc.tensor.matmul(m.ps[half:half + 64, 5 + u % 2, 0:P], v(kb), pt[:, u % 2, kb * P:(kb + 1) * P],
                                           start=(kb == 0), stop=(kb == n - 1))
                ins.then_inc(summed, 1)

            score(0)
            score(1)
            for u in range(N):
                if u + 2 < N:
                    score(u + 2)
                turn(u)
                if u >= 1:
                    values(u - 1)
            values(N - 1)

        @block.scalar
        def _(act):
            def y_copy(u):
                act.wait_ge(summed, u + 1)
                nc.scalar.copy(units[u][4], m.ps[units[u][6]:units[u][6] + 64, 5 + u % 2, 0:P]).then_inc(y_out, 1)

            def t_copy(u):
                n = nkeys(units[u][5])
                act.wait_ge(turned, u + 1)
                if u >= 2:
                    act.wait_ge(summed, u - 1)
                nc.scalar.copy(pt[:, u % 2, 0:n], m.ps[:, 3 + u % 2, 0:n]).then_inc(turn_out, 1)

            for u, (br, _, _, _, _, b, _) in enumerate(units):
                n = nkeys(b)
                act.wait_ge(maxed, u + 1)
                if u >= 2:
                    act.wait_ge(turned, u - 1)
                nc.scalar.activation(pr[:, u % 2, 0:n], m.ps[:, u % 3, 0:n], ACT.Exp, bias=st[:, 0, u:u + 1],
                                     scale=SC[br], accum_out=st[:, 1, u:u + 1]).then_inc(exped, 1)
                if u >= 1:
                    t_copy(u - 1)
                if u >= 2:
                    y_copy(u - 2)
            t_copy(N - 1)
            y_copy(N - 2)
            y_copy(N - 1)

        @block.vector
        def _(dve):
            own = Chain(dve, dve_own)

            def top(u):
                br, b = units[u][0], units[u][5]
                dve.wait_ge(scored, u + 1)
                own.link(nc.vector.reduce_max(st[:, 2, u:u + 1], m.ps[:, u % 3, 0:nkeys(b)], axis=AX.X))
                nc.vector.tensor_scalar(st[:, 0, u:u + 1], st[:, 2, u:u + 1], -SC[br], None, ALU.mult).then_inc(maxed, 1)

            top(0)
            top(1)
            for u, unit in enumerate(units):
                n = nkeys(unit[5])
                dve.wait_ge(exped, u + 1)
                own.link(nc.vector.reciprocal(st[:, 1, u:u + 1], st[:, 1, u:u + 1]))
                nc.vector.tensor_scalar(pr[:, u % 2, 0:n], pr[:, u % 2, 0:n], st[:, 1, u:u + 1], None,
                                        ALU.mult).then_inc(normed, 1)
                if u + 2 < N:
                    top(u + 2)



ORDER = {0: (0, 1, 2, 3), 1: (1, 0, 3, 2)}


def mlstm(nc, m, d, t, l, q_at):
    units = [(dr, h, p) for dr in range(2) for h in range(ML_H) for p in q_at]
    N = len(units)
    SCALE = HD ** -0.5
    with ExitStack() as ctx:
        lf = ctx.enter_context(sbuf(nc, "logf", [P, NB, 2 * ML_H], F32))
        af = ctx.enter_context(sbuf(nc, "absf", [P, NB, 2 * ML_H], F32))
        ft = ctx.enter_context(sbuf(nc, "ftot", [P, 2, NB, ML_H], F32))
        same = ctx.enter_context(sbuf(nc, "same", [P, 2, NB, P], F32))
        fb = ctx.enter_context(sbuf(nc, "fbcast", [P, 2, NB, P], F32))
        below = ctx.enter_context(sbuf(nc, "below", [P, NB, P], F32))
        w = ctx.enter_context(sbuf(nc, "w", [P, 2, TOK], F32))
        a = ctx.enter_context(sbuf(nc, "a", [P, 2, TOK], F32))
        at = ctx.enter_context(sbuf(nc, "aT", [P, 2, TOK], F32))
        st = ctx.enter_context(sbuf(nc, "stat", [P, 6, N], F32))
        hh = ctx.enter_context(sbuf(nc, "h", [P, NB, ML_W], F32))
        h2 = ctx.enter_context(sbuf(nc, "h2", [P, NB, ML_W], F32))
        og = ctx.enter_context(sbuf(nc, "og", [P, NB, ML_W], F32))
        nr = ctx.enter_context(sbuf(nc, "nr", [P, NB, ML_H], F32))
        (block, f_abs, f_exp, f_exp1, f_ln, f_done, f_tot, tot_out, built, decayed, scored, maxed, exped, den_exp,
         weighed, turned, turn_out, summed, h_done, o_gate, n_scaled, n_root, y_done, y_turned, y_out, dve_own, pool_own, spread_out, hy_in
         ) = ctx.enter_context(stage(
             nc, "f_abs", "f_exp", "f_exp1", "f_ln", "f_done", "f_tot", "tot_out", "built", "decayed", "scored",
             "maxed", "exped", "den_exp", "weighed", "turned", "turn_out", "summed", "h_done", "o_gate", "n_scaled",
             "n_root", "y_done", "y_turned", "y_out", "dve_own", "pool_own", "spread_out", "hy_in"))
        qb = sorted({ORDER[0][p] for p in q_at})
        b0, b1 = qb[0], qb[-1] + 1
        tri = (C_TRI_F, C_TRI_B)
        strict = (C_STR_F, C_STR_B)
        neg = (C_NEG_F, C_NEG_B)
        heads = [(dr, h) for dr in range(2) for h in range(ML_H)]

        @block.sync
        def _(sp):
            sp.dma_start(t.feat[:, :], d["k_feat"]).then_inc(hy_in, 16)
            sp.dma_start(t.w1[:, :], d["hy_w1"][l]).then_inc(hy_in, 16)
            sp.dma_start(t.w2[:, :], d["hy_w2"][l]).then_inc(hy_in, 16)
            sp.dma_start(t.w3[:, :], d["hy_w3"][l]).then_inc(hy_in, 16)
            sp.dma_start(t.dec[:, :, :], d["k_decay"].rearrange("(a p) n -> p a n", p=P)).then_inc(hy_in, 16)
            sp.wait_ge(hy_in, 80)

        @block.gpsimd
        def _(pool):
            own = Chain(pool, pool_own)
            pool.wait_ge(f_done, 1)
            for i, (dr, h) in enumerate(heads):
                if i >= 2:
                    pool.wait_ge(decayed, (i - 1) * len(q_at))
                for b in range(NB):
                    gate = t.mg[:, b, dr * ML_H + h:dr * ML_H + h + 1]
                    log_f = lf[:, b, dr * ML_H + h:dr * ML_H + h + 1]
                    own.step(nc.gpsimd.tensor_scalar(same[:, i % 2, b, :], m.sq[:, C_ID, :], gate, None, ALU.mult))
                    own.step(nc.gpsimd.tensor_scalar(below[:, b, :], m.sq[:, strict[dr], :], log_f, None, ALU.mult))
                own.meet()
                nc.gpsimd.tensor_tensor(same[:, i % 2, :, :], same[:, i % 2, :, :], below[:, :, :], ALU.add
                                        ).then_inc(built, 1)
                pool.wait_ge(built, i + 1)

        @block.scalar
        def _(act):
            act.wait_ge(f_abs, 1)
            nc.scalar.activation(af[:, :, :], af[:, :, :], ACT.Exp, scale=-1.0).then_inc(f_exp, 1)
            act.wait_ge(f_exp1, 1)
            nc.scalar.activation(af[:, :, :], af[:, :, :], ACT.Ln).then_inc(f_ln, 1)
            nc.scalar.activation(og[:, b0:b1, :], t.mvo[:, b0:b1, ML_W:], ACT.Sigmoid).then_inc(o_gate, 1)

            def spread(i):
                dr, h = heads[i]
                if i >= 2:
                    act.wait_ge(decayed, (i - 1) * len(q_at))
                for b in range(NB):
                    ins = nc.scalar.activation(fb[:, i % 2, b, :], m.sq[:, C_ONES, :], ACT.Copy,
                                               scale=lf[:, b, dr * ML_H + h:dr * ML_H + h + 1])
                ins.then_inc(spread_out, 1)

            def t_copy(u):
                n = (units[u][2] + 1) * P
                act.wait_ge(turned, u + 1)
                if u >= 2:
                    act.wait_ge(summed, u - 1)
                nc.scalar.copy(at[:, u % 2, 0:n], m.ps[:, 5, 0:n]).then_inc(turn_out, 1)

            act.wait_ge(f_done, 1)
            spread(0)
            spread(1)
            for u, (dr, h, p) in enumerate(units):
                n = (p + 1) * P
                act.wait_ge(maxed, u + 1)
                if u >= 2:
                    act.wait_ge(weighed, u - 1)
                nc.scalar.activation(w[:, u % 2, 0:n], m.ps[:, u % 3, 0:n], ACT.Exp, bias=st[:, 1, u:u + 1]
                                     ).then_inc(exped, 1)
                nc.scalar.activation(st[:, 2, u:u + 1], st[:, 1, u:u + 1], ACT.Exp).then_inc(den_exp, 1)
                if u >= 1:
                    t_copy(u - 1)
                i = (u + 1) // len(q_at)
                if (u + 1) % len(q_at) == len(q_at) - 1 and i + 2 < len(heads):
                    spread(i + 2)
            t_copy(N - 1)
            act.wait_ge(n_scaled, 1)
            nc.scalar.activation(nr[:, b0:b1, :], nr[:, b0:b1, :], ACT.Sqrt).then_inc(n_root, 1)

        @block.tensor
        def _(pe):
            pe.wait_ge(f_done, 1)
            for dr in range(2):
                for p in range(NB):
                    blk = ORDER[dr]
                    for j in range(p + 1):
                        ins = nc.tensor.matmul(m.ps[:, 6, (dr * NB + p) * ML_H:(dr * NB + p + 1) * ML_H],
                                               m.sq[:, tri[dr] if j == p else C_ONES, :],
                                               lf[:, blk[j], dr * ML_H:(dr + 1) * ML_H], start=(j == 0), stop=(j == p))
            ins.then_inc(f_tot, 1)

            def decay(u):
                dr, h, p = units[u]
                blk, hd = ORDER[dr], heads.index((dr, h)) % 2
                pe.wait_ge(built, heads.index((dr, h)) + 1)
                pe.wait_ge(spread_out, heads.index((dr, h)) + 1)
                if u >= 3:
                    pe.wait_ge(exped, u - 2)
                ones = m.sq[:, C_ONES, :]
                for j in range(p + 1):
                    out = m.ps[:, u % 3, j * P:(j + 1) * P]
                    if j == p:
                        nc.tensor.matmul(out, m.sq[:, tri[dr], :], same[:, hd, blk[p], :], start=True, stop=False)
                        ins = nc.tensor.matmul(out, m.sq[:, C_ID, :], m.sq[:, neg[dr], :], start=False, stop=True)
                        continue
                    nc.tensor.matmul(out, ones, same[:, hd, blk[j], :], start=True, stop=False)
                    for i in range(j + 1, p):
                        nc.tensor.matmul(out, ones, fb[:, hd, blk[i], :], start=False, stop=False)
                    nc.tensor.matmul(out, m.sq[:, tri[dr], :], fb[:, hd, blk[p], :], start=False, stop=True)
                ins.then_inc(decayed, 1)

            def score(u):
                dr, h, p = units[u]
                blk, half = ORDER[dr], 64 * (h % 2)
                if u >= 2:
                    pe.wait_ge(weighed, u - 1)
                for j in range(p + 1):
                    ins = nc.tensor.matmul(m.ps[:, 3 + u % 2, j * P:(j + 1) * P],
                                           t.mq[half:half + 64, h // 2, blk[p] * P:(blk[p] + 1) * P],
                                           t.mk[half:half + 64, h // 2, blk[j] * P:(blk[j] + 1) * P],
                                           start=True, stop=True)
                ins.then_inc(scored, 1)

            def turn(u):
                pe.wait_ge(weighed, u + 1)
                if u >= 1:
                    pe.wait_ge(turn_out, u)
                for j in range(units[u][2] + 1):
                    ins = nc.tensor.transpose(m.ps[:, 5, j * P:(j + 1) * P], a[:, u % 2, j * P:(j + 1) * P],
                                              m.sq[:, C_ID, :])
                ins.then_inc(turned, 1)

            def values(u):
                dr, h, p = units[u]
                pe.wait_ge(turn_out, u + 1)
                if u == 0:
                    pe.wait_ge(tot_out, 1)
                if u >= 2:
                    pe.wait_ge(h_done, u - 1)
                for j in range(p + 1):
                    ins = nc.tensor.matmul(m.ps[:, 6 + u % 2, 0:HD], at[:, u % 2, j * P:(j + 1) * P],
                                           t.mvo[:, ORDER[dr][j], h * HD:(h + 1) * HD], start=(j == 0), stop=(j == p))
                ins.then_inc(summed, 1)

            decay(0)
            decay(1)
            score(0)
            for u in range(N):
                if u + 2 < N:
                    decay(u + 2)
                if u + 1 < N:
                    score(u + 1)
                turn(u)
                if u >= 1:
                    values(u - 1)
            values(N - 1)
            pe.wait_ge(y_done, 1)
            for i, b in enumerate(range(b0, b1)):
                if i >= 2:
                    pe.wait_ge(y_out, i - 1)
                for g in range(2):
                    ins = nc.tensor.transpose(m.ps[:, i % 2, g * P:(g + 1) * P], hh[:, b, g * P:(g + 1) * P],
                                              m.sq[:, C_ID, :])
                ins.then_inc(y_turned, 1)

        @block.vector
        def _(dve):
            own = Chain(dve, dve_own)
            nc.vector.scalar_tensor_tensor(out=af[:, :, :], in0=t.mg[:, :, 2 * ML_H:], scalar=-1.0,
                                           in1=t.mg[:, :, 2 * ML_H:], op0=ALU.mult, op1=ALU.max).then_inc(f_abs, 1)
            own.link(nc.vector.tensor_scalar(lf[:, :, :], t.mg[:, :, 2 * ML_H:], 0.0, None, ALU.min))
            dve.wait_ge(f_exp, 1)
            nc.vector.tensor_scalar(af[:, :, :], af[:, :, :], 1.0, None, ALU.add).then_inc(f_exp1, 1)
            dve.wait_ge(f_ln, 1)
            nc.vector.tensor_tensor(lf[:, :, :], lf[:, :, :], af[:, :, :], ALU.subtract).then_inc(f_done, 1)
            dve.wait_ge(f_done, 1)
            dve.wait_ge(f_tot, 1)
            nc.vector.tensor_copy(ft[:, :, :, :].rearrange("p a b c -> p (a b c)"),
                                  m.ps[:, 6, 0:2 * NB * ML_H]).then_inc(tot_out, 1)
            dve.wait_ge(tot_out, 1)

            def top(u):
                dr, h, p = units[u]
                dve.wait_ge(decayed, u + 1)
                own.link(nc.vector.reduce_max(st[:, 0, u:u + 1], m.ps[:, u % 3, 0:(p + 1) * P], axis=AX.X))
                nc.vector.tensor_scalar(st[:, 1, u:u + 1], st[:, 0, u:u + 1], ft[:, dr, p, h:h + 1], -1.0, ALU.max,
                                        ALU.mult).then_inc(maxed, 1)

            def output(u):
                dr, h, p = units[u]
                b = ORDER[dr][p]
                dve.wait_ge(den_exp, u + 1)
                own.link(nc.vector.scalar_tensor_tensor(out=st[:, 4, u:u + 1], in0=st[:, 3, u:u + 1], scalar=-1.0,
                                                        in1=st[:, 3, u:u + 1], op0=ALU.mult, op1=ALU.max))
                own.link(nc.vector.tensor_tensor(st[:, 4, u:u + 1], st[:, 4, u:u + 1], st[:, 2, u:u + 1], ALU.max))
                own.link(nc.vector.reciprocal(st[:, 5, u:u + 1], st[:, 4, u:u + 1]))
                dve.wait_ge(summed, u + 1)
                out, got = hh[:, b, h * HD:(h + 1) * HD], m.ps[:, 6 + u % 2, 0:HD]
                if dr == 0:
                    ins = nc.vector.tensor_scalar(out, got, st[:, 5, u:u + 1], None, ALU.mult)
                else:
                    ins = nc.vector.scalar_tensor_tensor(out=out, in0=got, scalar=st[:, 5, u:u + 1], in1=out,
                                                         op0=ALU.mult, op1=ALU.add)
                ins.then_inc(h_done, 1)

            top(0)
            top(1)
            for u, (dr, h, p) in enumerate(units):
                n = (p + 1) * P
                dve.wait_ge(exped, u + 1)
                dve.wait_ge(scored, u + 1)
                if u >= 2:
                    dve.wait_ge(turned, u - 1)
                nc.vector.tensor_tensor_reduce(a[:, u % 2, 0:n], w[:, u % 2, 0:n], m.ps[:, 3 + u % 2, 0:n], SCALE, 0.0,
                                               ALU.mult, ALU.add, st[:, 3, u:u + 1]).then_inc(weighed, 1)
                dve.wait_ge(weighed, u + 1)
                if u >= 1:
                    output(u - 1)
                if u + 2 < N:
                    top(u + 2)
            output(N - 1)
            dve.wait_ge(h_done, N)
            own.link(nc.vector.tensor_tensor(h2[:, b0:b1, :], hh[:, b0:b1, :], hh[:, b0:b1, :], ALU.mult))
            own.link(nc.vector.tensor_reduce(nr[:, b0:b1, :], h2[:, b0:b1, :].rearrange("p b (h e) -> p b h e", h=ML_H),
                                             axis=AX.X, op=ALU.add))
            nc.vector.tensor_scalar(nr[:, b0:b1, :], nr[:, b0:b1, :], 1.0 / HD, EPS, ALU.mult, ALU.add
                                    ).then_inc(n_scaled, 1)
            dve.wait_ge(o_gate, 1)
            own.link(nc.vector.tensor_tensor(hh[:, b0:b1, :], hh[:, b0:b1, :], og[:, b0:b1, :], ALU.mult))
            dve.wait_ge(n_root, 1)
            own.link(nc.vector.reciprocal(nr[:, b0:b1, :], nr[:, b0:b1, :]))
            for b in range(b0, b1):
                ins = nc.vector.tensor_tensor(
                    hh[:, b, :].rearrange("p (h e) -> p h e", h=ML_H), hh[:, b, :].rearrange("p (h e) -> p h e", h=ML_H),
                    nr[:, b, :].unsqueeze(2).to_broadcast([P, ML_H, HD]), ALU.mult)
                own.step(ins)
            own.meet()
            dve.sem_inc(y_done, 1)
            for i, b in enumerate(range(b0, b1)):
                dve.wait_ge(y_turned, i + 1)
                for g in range(2):
                    ins = nc.vector.tensor_scalar(t.yT[:, 2, g, b * P:(b + 1) * P], m.ps[:, i % 2, g * P:(g + 1) * P],
                                                  m.vec[:, V_MLN + g:V_MLN + g + 1], None, ALU.mult)
                ins.then_inc(y_out, 1)



SEQ = 256
KF = SEQ // P
TWO_PI_HI = 6.28125
TWO_PI_LO = 6.283185307179586 - 6.28125
ROUND = 1.5 * 2.0 ** 23
PI = 3.1415925


def hyena(nc, m, d, t, l, streams, ring):
    S = len(streams)
    s0, C2 = streams[0], 2 * HY_W
    with ExitStack() as ctx:
        sb = lambda name, shape: ctx.enter_context(sbuf(nc, name, shape, F32))
        dft = sb("dft", [P, 4, KF, SEQ])
        dec, feat, w1, w2, w3 = t.dec, t.feat, t.w1, t.w2, t.w3
        hid, arg, rnd = sb("hid", [64, SEQ]), sb("arg", [64, SEQ]), sb("rnd", [64, SEQ])
        filt = sb("filt", [P, KF, 2, 2, HY_W])
        fsq = sb("fsq", [P, KF, 2 * C2])
        frs = sb("frs", [P, C2])
        comb = sb("comb", [P, 2, KF, C2])
        spec = sb("spec", [P, 2, KF, C2])
        cv = sb("cv", [P, 6, TOK])
        z = sb("z", [P, KF, 2, HY_W])
        zf = sb("zf", [P, 2, KF, S * HY_W])
        yf = sb("yf", [P, 2, KF, S * HY_W])
        tmp = fsq[:, :, 0:S * HY_W]
        zt = sb("zt", [P, 2, TOK])
        (block, k_in, h_mult, arg_done, sine_done, f_mult, f_out, f_sq, f_sum, f_scaled, f_root, comb_done, s_mult,
         s_out, conv_done, z_turned, z_out, z_mult, zf_out, yf_done, y_mult, y_out, dve_own, wg_in0, wg_in1, wg_rounded) = ctx.enter_context(stage(
             nc, "k_in", "h_mult", "arg_done", "sine_done", "f_mult", "f_out", "f_sq", "f_sum", "f_scaled", "f_root",
             "comb_done", "s_mult", "s_out", "conv_done", "z_turned", "z_out", "z_mult", "zf_out", "yf_done",
             "y_mult", "y_out", "dve_own", "wg_in0", "wg_in1", "wg_rounded"))
        wg_ins = (wg_in0, wg_in1)
        flat = lambda x: x.rearrange("p k i n -> p (k i n)")

        @block.gpsimd
        def _(pool):
            pool.wait_ge(wg_rounded, 1)
            nc.gpsimd.tensor_tensor(flat(ring.split[0][:, 1]), flat(ring.raw[:, 0]), flat(ring.split[0][:, 0]).bitcast(F32),
                                    ALU.subtract)

        @block.sync
        def _(sp):
            sp.dma_start(dft[:, :, :, :], d["k_dft"].rearrange("c (a p) n -> p c a n", p=P)).then_inc(k_in, 16)
            for c in range(2):
                load_gates(sp, d, l, ring, c, wg_ins)
            sp.wait_ge(wg_in1, 32)

        @block.tensor
        def _(pe):
            nc.tensor.matmul(m.ps[0:64, 0, 0:SEQ], w1[:, :], feat[:, :], start=True, stop=True).then_inc(h_mult, 1)
            pe.wait_ge(sine_done, 1)
            nc.tensor.matmul(m.ps[0:64, 1, 0:SEQ], w2[:, :], hid[:, :], start=True, stop=True).then_inc(h_mult, 1)
            pe.wait_ge(sine_done, 2)
            for a in range(KF):
                for o in range(2):
                    nc.tensor.matmul(m.ps[:, 2 + 2 * a + o, :], hid[:, a * P:(a + 1) * P], w3[:, o * C2:(o + 1) * C2],
                                     start=True, stop=True).then_inc(f_mult, 1)
            pe.wait_ge(f_sq, 1)
            for o in range(2):
                for i in range(2 * KF):
                    a, r = i % KF, i // KF
                    ins = nc.tensor.matmul(m.ps[:, 0, o * HY_W:(o + 1) * HY_W], m.sq[:, C_ONES, :],
                                           fsq[:, a, o * C2 + r * HY_W:o * C2 + (r + 1) * HY_W], start=(i == 0),
                                           stop=(i == 2 * KF - 1))
            ins.then_inc(f_sum, 1)

            def spectra(order):
                src = cv if order == 0 else zt
                for a in range(KF):
                    for i, s in enumerate(streams):
                        for c in range(2):
                            ins = nc.tensor.transpose(m.ps[:, 2 + a, i * HY_W + c * P:i * HY_W + (c + 1) * P],
                                                      src[:, c, s * SEQ + a * P:s * SEQ + (a + 1) * P], m.sq[:, C_ID, :])
                    ins.then_inc(z_turned, 1)
                pe.wait_ge(z_out, 2 * (order + 1))
                for r in range(2):
                    for kt in range(KF):
                        for a in range(KF):
                            ins = nc.tensor.matmul(m.ps[:, 4 + 2 * r + kt, 0:S * HY_W], dft[:, r, a, kt * P:(kt + 1) * P],
                                                   z[:, a, 0:S, :].rearrange("p s c -> p (s c)"), start=(a == 0),
                                                   stop=(a == KF - 1))
                        ins.then_inc(z_mult, 1)

            def back(order):
                for r in range(2):
                    pe.wait_ge(yf_done, 2 * order + r + 1)
                    for i in range(S):
                        for c in range(2):
                            for kt in range(KF):
                                ins = nc.tensor.matmul(m.ps[:, 2 * i + c, 0:SEQ],
                                                       yf[:, r, kt, i * HY_W + c * P:i * HY_W + (c + 1) * P],
                                                       dft[:, 2 + r, kt, :], start=(r == 0 and kt == 0),
                                                       stop=(r == 1 and kt == KF - 1))
                            if r == 1:
                                ins.then_inc(y_mult, 1)

            pe.wait_ge(k_in, 16)
            pe.wait_ge(conv_done, 1)
            spectra(0)
            pe.wait_ge(comb_done, 1)
            pe.wait_ge(zf_out, 4)
            for r in range(2):
                for kt in range(KF):
                    for a in range(KF):
                        ins = nc.tensor.matmul(m.ps[:, 4 + 2 * r + kt, :], dft[:, r, a, kt * P:(kt + 1) * P],
                                               comb[:, r, a, :], start=(a == 0), stop=(a == KF - 1))
                    ins.then_inc(s_mult, 1)
            back(0)
            pe.wait_ge(s_out, 4)
            pe.wait_ge(y_out, 2 * S)
            spectra(1)
            back(1)

        @block.scalar
        def _(act):
            for i in range(2):
                act.wait_ge(arg_done, i + 1)
                nc.scalar.activation(hid[:, :], arg[:, :], ACT.Sin).then_inc(sine_done, 1)
            act.wait_ge(wg_in0, 32)
            nc.scalar.copy(flat(ring.split[0][:, 0]), flat(ring.raw[:, 0])).then_inc(wg_rounded, 1)
            act.wait_ge(f_scaled, 1)
            nc.scalar.activation(frs[:, :], frs[:, :], ACT.Sqrt).then_inc(f_root, 1)
            for order in range(2):
                for a in range(KF):
                    act.wait_ge(z_turned, 2 * order + a + 1)
                    nc.scalar.copy(z[:, a, 0:S, :].rearrange("p s c -> p (s c)"), m.ps[:, 2 + a, 0:S * HY_W]
                                   ).then_inc(z_out, 1)
                if order == 1:
                    act.wait_ge(yf_done, 2)
                for i in range(4):
                    act.wait_ge(z_mult, 4 * order + i + 1)
                    nc.scalar.copy(zf[:, i // 2, i % 2, :], m.ps[:, 4 + i, 0:S * HY_W]).then_inc(zf_out, 1)
                if order == 0:
                    for i in range(4):
                        act.wait_ge(s_mult, i + 1)
                        nc.scalar.copy(spec[:, i // 2, i % 2, :], m.ps[:, 4 + i, :]).then_inc(s_out, 1)

        @block.vector
        def _(dve):
            own = Chain(dve, dve_own)

            def short(tiles):
                tap = lambda j, g: m.vec[:, V_CONV + 6 * j + g:V_CONV + 6 * j + g + 1]
                u = lambda g, lo, hi: t.hy[:, g, s0 * SEQ:].rearrange("p (s n) -> p s n", n=SEQ)[:, :, lo:hi]
                o = lambda g, lo, hi: cv[:, g, s0 * SEQ:].rearrange("p (s n) -> p s n", n=SEQ)[:, :, lo:hi]
                for g in tiles:
                    own.step(nc.vector.tensor_scalar(o(g, 0, SEQ), u(g, 0, SEQ), tap(1, g), None, ALU.mult))
                own.meet()
                for g in tiles:
                    own.step(nc.vector.scalar_tensor_tensor(out=o(g, 1, SEQ), in0=u(g, 0, SEQ - 1), scalar=tap(0, g),
                                                            in1=o(g, 1, SEQ), op0=ALU.mult, op1=ALU.add))
                own.meet()
                for g in tiles:
                    own.step(nc.vector.scalar_tensor_tensor(out=o(g, 0, SEQ - 1), in0=u(g, 1, SEQ), scalar=tap(2, g),
                                                            in1=o(g, 0, SEQ - 1), op0=ALU.mult, op1=ALU.add))
                own.meet()

            for i, vb in enumerate((V_B1, V_B2)):
                if i == 1:
                    short((0, 1))
                    dve.sem_inc(conv_done, 1)
                dve.wait_ge(h_mult, i + 1)
                if i == 1:
                    dve.wait_ge(sine_done, 1)
                own.link(nc.vector.tensor_scalar(arg[:, :], m.ps[0:64, i, 0:SEQ], m.vec[0:64, vb:vb + 1],
                                                 m.vec[0:64, V_FREQ + i:V_FREQ + i + 1], ALU.add, ALU.mult))
                own.link(nc.vector.tensor_scalar(rnd[:, :], arg[:, :], 1.0 / (TWO_PI_HI + TWO_PI_LO), ROUND, ALU.mult,
                                                 ALU.add))
                own.link(nc.vector.tensor_scalar(rnd[:, :], rnd[:, :], -ROUND, None, ALU.add))
                for part in (TWO_PI_HI, TWO_PI_LO):
                    own.link(nc.vector.scalar_tensor_tensor(out=arg[:, :], in0=rnd[:, :], scalar=-part, in1=arg[:, :],
                                                            op0=ALU.mult, op1=ALU.add))
                nc.vector.tensor_scalar(arg[:, :], arg[:, :], PI, -PI, ALU.min, ALU.max).then_inc(arg_done, 1)
            for a in range(KF):
                for o in range(2):
                    dve.wait_ge(f_mult, 2 * a + o + 1)
                    own.step(nc.vector.tensor_tensor(
                        filt[:, a, o, :, :], m.ps[:, 2 + 2 * a + o, :].rearrange("p (r c) -> p r c", r=2),
                        dec[:, a:a + 1, :].to_broadcast([P, 2, HY_W]), ALU.mult))
            own.meet()
            nc.vector.tensor_tensor(fsq[:, :, :], filt[:, :, :, :, :].rearrange("p a o r c -> p a (o r c)"),
                                    filt[:, :, :, :, :].rearrange("p a o r c -> p a (o r c)"), ALU.mult).then_inc(f_sq, 1)
            short((2, 3, 4, 5))
            dve.wait_ge(f_sum, 1)
            nc.vector.tensor_scalar(frs[:, :], m.ps[:, 0, :], EPS, None, ALU.add).then_inc(f_scaled, 1)
            dve.wait_ge(f_root, 1)
            own.link(nc.vector.reciprocal(frs[:, :], frs[:, :]))
            for a in range(KF):
                for r in range(2):
                    own.step(nc.vector.tensor_tensor(filt[:, a, :, r, :], filt[:, a, :, r, :],
                                                     frs[:, :].rearrange("p (o c) -> p o c", o=2), ALU.mult))
            own.meet()
            own.link(nc.vector.memset(filt[0:1, 0, :, 1, :], 0.0))
            for a in range(KF):
                view = lambda x: x.rearrange("p (o c) -> p o c", o=2)
                own.step(nc.vector.tensor_tensor(view(comb[:, 0, a, :]), filt[:, a, :, 0, :], filt[:, a, :, 1, :], ALU.add))
                own.step(nc.vector.tensor_tensor(view(comb[:, 1, a, :]), filt[:, a, :, 0, :], filt[:, a, :, 1, :],
                                                 ALU.subtract))
            own.meet()
            dve.sem_inc(comb_done, 1)
            for order in range(2):
                src = cv if order == 0 else zt
                dve.wait_ge(zf_out, 4 * (order + 1))
                dve.wait_ge(s_out, 4)
                bc = lambda r: spec[:, r, :, order * HY_W:(order + 1) * HY_W].unsqueeze(2).to_broadcast(
                    [P, KF, S, HY_W])
                vw = lambda x: x.rearrange("p k (s c) -> p k s c", s=S)
                if order == 1:
                    dve.wait_ge(y_mult, 2 * S)
                for r in range(2):
                    for kt in range(KF):
                        kk = slice(kt, kt + 1)
                        own.step(nc.vector.tensor_tensor(vw(yf[:, r, kk, :]), vw(zf[:, 0, kk, :]), bc(r)[:, kk], ALU.mult))
                        own.step(nc.vector.tensor_tensor(vw(tmp[:, kk, :]), vw(zf[:, 1, kk, :]), bc(1 - r)[:, kk],
                                                         ALU.mult))
                    own.meet()
                    nc.vector.tensor_tensor(yf[:, r, :, :], yf[:, r, :, :], tmp[:, :, :],
                                            ALU.add if r else ALU.subtract).then_inc(yf_done, 1)
                    dve.wait_ge(yf_done, 2 * order + r + 1)
                for i, s in enumerate(streams):
                    for c in range(2):
                        dve.wait_ge(y_mult, 2 * S * order + 2 * i + c + 1)
                        tk = slice(s * SEQ, (s + 1) * SEQ)
                        vb = m.vec[:, V_HYB + 2 * order + c:V_HYB + 2 * order + c + 1]
                        own.link(nc.vector.scalar_tensor_tensor(out=zt[:, c, tk], in0=src[:, c, tk], scalar=vb,
                                                                in1=m.ps[:, 2 * i + c, 0:SEQ], op0=ALU.mult,
                                                                op1=ALU.add))
                        out = zt[:, c, tk] if order == 0 else t.yT[:, 3, c, tk]
                        nc.vector.tensor_tensor(out, zt[:, c, tk], cv[:, 2 + 2 * order + c, tk], ALU.mult
                                                ).then_inc(y_out, 1)
                if order == 0:
                    dve.wait_ge(y_out, 2 * S)




GATE_STEPS = [(k, i) for k in range(KD) for i in range(N_BRANCH)]


def load_gates(sp, d, l, ring, c, wg_ins):
    k, i = GATE_STEPS[2 * c]
    gates = d["w_in"][l].rearrange("(k p) n -> p k n", p=P)[:, :, O_GATE:].rearrange("p k (i n) -> p k i n", i=N_BRANCH)
    for j in range(2):
        sp.dma_start(ring.raw[:, c % 2, :, j, :], gates[:, :, i + j, k * P:(k + 1) * P]).then_inc(wg_ins[c % 2], 16)


def merge(nc, m, d, hs, t, l, t0, ring):
    T = TOK - t0
    halves = [(kind, lo, hi) for kind, lo, hi in ((1, 0, CTX), (0, CTX, TOK)) if lo >= t0]
    steps = GATE_STEPS
    PAIRS = len(steps) // 2
    with ExitStack() as ctx:
        raw, wg = ring.raw, [ring.split[0], ctx.enter_context(sbuf(nc, "wg_split1", [P, 2, KD, 2, P], F32R))]
        wb = ctx.enter_context(sbuf(nc, "w_branch", [P, 2, N_BRANCH * 2, P], F32))
        wo = ctx.enter_context(sbuf(nc, "w_out", [P, 2, KD, P], F32))
        acc = ctx.enter_context(sbuf(nc, "merged", [P, KD, TOK], F32))
        sg = ctx.enter_context(sbuf(nc, "sig", [P, 2, TOK], F32))
        pr = ctx.enter_context(sbuf(nc, "prod", [P, 2, TOK], F32))
        (block, gate_mult, y_mult, sig_done, prod_done, acc_done, o_mult, o_out, rounded, rested, wg_in0, wg_in1,
         wb_in0, wb_in1, wo_in0, wo_in1) = ctx.enter_context(stage(
             nc, "gate_mult", "y_mult", "sig_done", "prod_done", "acc_done", "o_mult", "o_out", "rounded", "rested",
             "wg_in0", "wg_in1", "wb_in0", "wb_in1", "wo_in0", "wo_in1"))
        wg_ins, wb_ins, wo_ins = (wg_in0, wg_in1), (wb_in0, wb_in1), (wo_in0, wo_in1)

        @block.sync
        def _(sp):
            for c in range(PAIRS):
                k, i = steps[2 * c]
                if c >= 3:
                    sp.wait_ge(rested, c - 2)
                if c >= 2:
                    load_gates(sp, d, l, ring, c, wg_ins)
                if c % 2 == 0:
                    if k >= 2:
                        sp.wait_ge(y_mult, N_BRANCH * (k - 1))
                    sp.dma_start(wb[:, k % 2, :, :], d["w_branch"][l].rearrange("i (a p) n -> p (i a) n", p=P)[
                        :, :, k * P:(k + 1) * P]).then_inc(wb_ins[k % 2], 16)
            for k in range(KD):
                if k >= 2:
                    sp.wait_ge(o_mult, k - 1)
                sp.dma_start(wo[:, k % 2, :, :], d["w_out"][l].rearrange("(k p) n -> p k n", p=P)[
                    :, :, k * P:(k + 1) * P]).then_inc(wo_ins[k % 2], 16)

        @block.gpsimd
        def _(pool):
            for c in range(1, PAIRS):
                pool.wait_ge(rounded, c)
                flat = lambda x: x.rearrange("p k i n -> p (k i n)")
                nc.gpsimd.tensor_tensor(flat(wg[c % 2][:, 1]), flat(raw[:, c % 2]), flat(wg[c % 2][:, 0]).bitcast(F32),
                                        ALU.subtract).then_inc(rested, 1)

        @block.tensor
        def _(pe):
            for n, (k, i) in enumerate(steps):
                if n % 2 == 0 and n >= 2:
                    pe.wait_ge(rested, n // 2)
                if n >= 2:
                    pe.wait_ge(sig_done, n - 1)
                w = wg[n // 2 % 2]
                for kk in range(KD):
                    ins = split_matmul(nc, m.ps[:, n % 2, 0:T], lambda r: w[:, r, kk, i % 2, :],
                                       lambda r: hs[:, r, kk, t0:], kk == 0, kk == KD - 1)
                ins.then_inc(gate_mult, 1)
                if i == 0:
                    pe.wait_ge(wb_ins[k % 2], 16 * (k // 2 + 1))
                if n >= 2:
                    pe.wait_ge(prod_done, n - 1)
                for a in range(2):
                    ins = nc.tensor.matmul(m.ps[:, 2 + n % 2, 0:T], wb[:, k % 2, 2 * i + a, :],
                                           t.yT[:, i, a, t0:], start=(a == 0), stop=(a == 1))
                ins.then_inc(y_mult, 1)
            pe.wait_ge(acc_done, len(steps))
            for k in range(KD):
                pe.wait_ge(wo_ins[k % 2], 16 * (k // 2 + 1))
                if k >= 4:
                    pe.wait_ge(o_out, k - 3)
                for kk in range(KD):
                    ins = nc.tensor.matmul(m.ps[:, 4 + k % 4, 0:T], wo[:, k % 2, kk, :], acc[:, kk, t0:],
                                           start=(kk == 0), stop=(kk == KD - 1))
                ins.then_inc(o_mult, 1)

        @block.scalar
        def _(act):
            def round_pair(c):
                if c >= 2:
                    act.wait_ge(wg_ins[c % 2], 32 * (c // 2))
                    act.wait_ge(gate_mult, 2 * (c - 1))
                flat = lambda x: x.rearrange("p k i n -> p (k i n)")
                nc.scalar.copy(flat(wg[c % 2][:, 0]), flat(raw[:, c % 2])).then_inc(rounded, 1)

            round_pair(1)
            for n in range(len(steps)):
                act.wait_ge(gate_mult, n + 1)
                if n >= 2:
                    act.wait_ge(prod_done, n - 1)
                nc.scalar.activation(sg[:, n % 2, t0:], m.ps[:, n % 2, 0:T], ACT.Sigmoid).then_inc(sig_done, 1)
                if n % 2 == 1 and n // 2 + 2 < PAIRS:
                    round_pair(n // 2 + 2)

        @block.vector
        def _(dve):
            for n, (k, i) in enumerate(steps):
                dve.wait_ge(y_mult, n + 1)
                dve.wait_ge(sig_done, n + 1)
                if n >= 2:
                    dve.wait_ge(acc_done, n - 1)
                if i == 0:
                    nc.vector.tensor_tensor(acc[:, k, t0:], sg[:, n % 2, t0:], m.ps[:, 2 + n % 2, 0:T], ALU.mult
                                            ).then_inc(prod_done, 1)
                    dve.wait_ge(prod_done, n + 1)
                    dve.sem_inc(acc_done, 1)
                    continue
                nc.vector.tensor_tensor(pr[:, n % 2, t0:], sg[:, n % 2, t0:], m.ps[:, 2 + n % 2, 0:T], ALU.mult
                                        ).then_inc(prod_done, 1)
                dve.wait_ge(prod_done, n + 1)
                dve.wait_ge(acc_done, n)
                nc.vector.tensor_tensor(acc[:, k, t0:], acc[:, k, t0:], pr[:, n % 2, t0:], ALU.add).then_inc(acc_done, 1)
            for k in range(KD):
                dve.wait_ge(o_mult, k + 1)
                for kind, lo, hi in halves:
                    ins = nc.vector.scalar_tensor_tensor(
                        out=m.resid[:, k, lo:hi], in0=m.ps[:, 4 + k % 4, lo - t0:hi - t0],
                        scalar=m.mod[:, 2 * KD + k, kind:kind + 1], in1=m.resid[:, k, lo:hi], op0=ALU.mult, op1=ALU.add)
                ins.then_inc(o_out, 1)




QCH = 2 * P


def peer_select(nc, m, d, hs, sel, l, t0, ring):
    T = TOK - t0
    tb0 = t0 // P
    nb = NB - tb0
    with ExitStack() as ctx:
        sb = lambda name, shape, dt=F32: ctx.enter_context(sbuf(nc, name, shape, dt))
        raw, wq = ring.raw, ring.split
        m_raw = sb("ada_w", [P, 2, KD, MCH])
        m_row = sb("mod_row", [2, 2, MCH])
        vrow = sb("vrow", [P, P])
        qT = sb("qT", [P, 2, 2, TOK])
        sk = sb("subkeys", [P, HC, P])
        skT = sb("subkeysT", [P, HC, P])
        sc = sb("scores", [P, 2, 2, nb, P])
        s2 = sb("scores2", [P, 2, nb, P])
        sv = sb("sv", [P, 2, nb, TOPK])
        si = sb("si", [P, 2, nb, TOPK], U32)
        sif = sb("sif", [P, 2, 2, nb, TOPK])
        cand = sb("cand", [P, nb, TOPK * TOPK])
        cand2 = sb("cand2", [P, nb, TOPK * TOPK])
        best = sb("best", [P, nb, TOPK])
        pos = sb("pos", [P, nb, TOPK], U32)
        part = sb("part", [P, 2, nb, TOPK], U32)
        partf = sb("partf", [P, 2, nb, TOPK])
        eq = sb("eq", [P, 2, nb, TOPK, TOPK])
        pick = sb("pick", [P, nb, 3, P])
        dn = sb("dn", [P, nb, PH])
        (block, sk_in, sk_turned, sk_out, q_mult, q_out, s_mult, s_out, s_used, diffed, g_exp, picked, p_turned,
         p_out, dve_own, rounded, rested, wq_in0, wq_in1, m_in0, m_in1, m_mult, m_out, m_turned,
         zeroed, vecs_in, vecs_turned, vecs_out, products_out, placed, keyed) = ctx.enter_context(
             stage(nc, "sk_in", "sk_turned", "sk_out", "q_mult", "q_out", "s_mult", "s_out", "s_used", "diffed",
                   "g_exp", "picked", "p_turned", "p_out", "dve_own", "rounded", "rested", "wq_in0", "wq_in1",
                   "m_in0", "m_in1", "m_mult", "m_out", "m_turned", "zeroed", "vecs_in", "vecs_turned", "vecs_out",
                   "products_out", "placed", "keyed"))
        wq_ins = (wq_in0, wq_in1)
        side = l + 1 < LAYERS and SideModulation(nc, m, d["ada_w"][l + 1], 0, 6 * D, m_raw, m_row, (6, 7), 2,
                                                 (m_in0, m_in1), 0, m_mult, m_out, m_turned)
        vecs = small_vectors(d, l + 1) if side else []
        share = lambda h: range(h * side.n // PH, (h + 1) * side.n // PH) if side else ()
        LOW = -3.0e38

        @block.sync
        def _(sp):
            def load_wq(c):
                if c >= 3:
                    sp.wait_ge(rested, c - 2)
                sp.dma_start(raw[:, c % 2, :, :], d["peer_wq"][l].rearrange("(k p) n -> p k n", p=P)[
                    :, :, c * QCH:(c + 1) * QCH]).then_inc(wq_ins[c % 2], 16)

            sp.dma_start(sk[:, :, :], d["peer_subkeys"][l].rearrange("h c n d -> n (h c) d")).then_inc(sk_in, 16)
            load_wq(2)
            for h in range(PH):
                if h + 3 < PH:
                    load_wq(h + 3)
                for j in share(h):
                    side.load(sp, j)
            if side:
                sp.wait_ge(zeroed, 1)
                for at, n, w, src, c0 in vecs:
                    sp.dma_start(vrow[at:at + n, c0:c0 + w], src).then_inc(vecs_in, 16)

        @block.gpsimd
        def _(pool):
            def rest(c):
                if c >= 2:
                    pool.wait_ge(rounded, c - 1)
                nc.gpsimd.tensor_tensor(wq[c % 2][:, 1], raw[:, c % 2], wq[c % 2][:, 0].bitcast(F32), ALU.subtract
                                        ).then_inc(rested, 1)

            rest(1)
            for h in range(PH):
                if h + 2 < PH:
                    rest(h + 2)
                pool.wait_ge(placed, h + 1)
                for c in range(2):
                    nc.gpsimd.tensor_tensor(eq[:, c, :, :, :], eq[:, c, :, :, :],
                                            sif[:, h % 2, c, :, :].unsqueeze(2).to_broadcast([P, nb, TOPK, TOPK]),
                                            ALU.mult).then_inc(keyed, 1)

        @block.tensor
        def _(pe):
            def queries(h):
                if h >= 1:
                    pe.wait_ge(rested, h)
                w = wq[h % 2]
                for c in range(2):
                    if h >= 1:
                        pe.wait_ge(q_out, 2 * (h - 1) + c + 1)
                    for k in range(KD):
                        ins = split_matmul(nc, m.ps[:, c, 0:T], lambda r: w[:, r, k, c * P:(c + 1) * P],
                                           lambda r: hs[:, r, k, t0:], k == 0, k == KD - 1)
                    ins.then_inc(q_mult, 1)

            def scores(h):
                for c in range(2):
                    pe.wait_ge(q_out, 2 * h + c + 1)
                    if h >= 1:
                        pe.wait_ge(s_out, 2 * (h - 1) + c + 1)
                    for n in range(nb):
                        at = (tb0 + n) * P
                        ins = nc.tensor.matmul(m.ps[:, 4 + c, n * P:(n + 1) * P], qT[:, h % 2, c, at:at + P],
                                               skT[:, 2 * h + c, :], start=True, stop=True)
                    ins.then_inc(s_mult, 1)

            queries(0)
            pe.wait_ge(sk_in, 16)
            for q in range(4):
                if q >= 2:
                    pe.wait_ge(sk_out, q - 1)
                for i in range(4):
                    ins = nc.tensor.transpose(m.ps[:, 2 + q % 2, i * P:(i + 1) * P], sk[:, 4 * q + i, :], m.sq[:, C_ID, :])
                ins.then_inc(sk_turned, 1)
            pe.wait_ge(sk_out, 4)
            for h in range(PH):
                scores(h)
                if h + 1 < PH:
                    queries(h + 1)
                for j in share(h):
                    side.multiply(pe, j)
            if side:
                side.turn(pe, side.n - 1)
                pe.wait_ge(vecs_in, 16 * len(vecs))
                nc.tensor.transpose(m.ps[:, 3, 0:P], vrow[:, :], m.sq[:, C_ID, :]).then_inc(vecs_turned, 1)
            pe.wait_ge(picked, 1)
            for n in range(nb):
                if n >= 2:
                    pe.wait_ge(p_out, n - 1)
                for i in range(3):
                    ins = nc.tensor.transpose(m.ps[:, n % 2, i * P:(i + 1) * P], pick[:, n, i, :], m.sq[:, C_ID, :])
                ins.then_inc(p_turned, 1)

        @block.scalar
        def _(act):
            def copy_queries(h):
                for c in range(2):
                    act.wait_ge(q_mult, 2 * h + c + 1)
                    if h >= 2:
                        act.wait_ge(s_mult, 2 * (h - 2) + c + 1)
                    nc.scalar.copy(qT[:, h % 2, c, t0:], m.ps[:, c, 0:T]).then_inc(q_out, 1)
                if h + 2 < PH:
                    act.wait_ge(wq_ins[h % 2], 16 * (h // 2 + 1))
                    act.wait_ge(q_mult, 2 * (h + 1))
                    nc.scalar.copy(wq[h % 2][:, 0], raw[:, h % 2]).then_inc(rounded, 1)

            copy_queries(0)
            for q in range(4):
                act.wait_ge(sk_turned, q + 1)
                nc.scalar.copy(skT[:, 4 * q:4 * q + 4, :].rearrange("p a b -> p (a b)"), m.ps[:, 2 + q % 2, :]
                               ).then_inc(sk_out, 1)
            for h in range(PH):
                for c in range(2):
                    act.wait_ge(s_mult, 2 * h + c + 1)
                    if h >= 2:
                        act.wait_ge(s_used, h - 1)
                    nc.scalar.copy(sc[:, h % 2, c, :, :].rearrange("p a b -> p (a b)"), m.ps[:, 4 + c, 0:T]
                                   ).then_inc(s_out, 1)
                if h + 1 < PH:
                    copy_queries(h + 1)
                for j in share(h):
                    side.copy(act, j)
            if side:
                act.wait_ge(m_turned, side.n)
                nc.scalar.copy(m.products[:, :, :].rearrange("p j r -> p (j r)"), m.ps[:, 2, 0:12 * KD]
                               ).then_inc(products_out, 1)
                act.wait_ge(vecs_turned, 1)
                nc.scalar.copy(m.vec[:, :], m.ps[:, 3, 0:V_ROWS]).then_inc(vecs_out, 1)
            act.wait_ge(diffed, PH)
            nc.scalar.activation(pick[:, :, 2, :], pick[:, :, 2, :], ACT.Exp).then_inc(g_exp, 1)
            for n in range(nb):
                act.wait_ge(p_turned, n + 1)
                at = (tb0 + n) * P
                nc.scalar.copy(sel[:, :, at:at + P], m.ps[:, n % 2, 0:3 * P].rearrange("p (a b) -> p a b", a=3)
                               ).then_inc(p_out, 1)

        @block.vector
        def _(dve):
            own = Chain(dve, dve_own)

            def top16(rows, val, idx, src, src2):
                for r in rows:
                    own.step(nc.vector.max(val(r, 0), src(r)))
                own.meet()
                for r in rows:
                    own.step(nc.vector.max_index(idx(r, 0), val(r, 0), src(r)))
                    own.step(nc.vector.match_replace(src2(r), val(r, 0), src(r), LOW))
                own.meet()
                for r in rows:
                    own.step(nc.vector.max(val(r, 1), src2(r)))
                own.meet()
                for r in rows:
                    own.step(nc.vector.max_index(idx(r, 1), val(r, 1), src2(r)))
                own.meet()

            def keys(h):
                for c in range(2):
                    dve.wait_ge(keyed, 2 * h + c + 1)
                    own.step(nc.vector.tensor_reduce(pick[:, :, c, h * TOPK:(h + 1) * TOPK], eq[:, c, :, :, :],
                                                     axis=AX.X, op=ALU.add))
                own.meet()

            if side:
                nc.vector.memset(vrow[:, :], 0.0).then_inc(zeroed, 1)
            for h in range(PH):
                choices = slice(h * TOPK, (h + 1) * TOPK)
                dve.wait_ge(s_out, 2 * (h + 1))
                top16([(c, n) for c in range(2) for n in range(nb)],
                      lambda r, j: sv[:, r[0], r[1], 8 * j:8 * j + 8], lambda r, j: si[:, r[0], r[1], 8 * j:8 * j + 8],
                      lambda r: sc[:, h % 2, r[0], r[1], :], lambda r: s2[:, r[0], r[1], :])
                dve.sem_inc(s_used, 1)
                if h >= 1:
                    keys(h - 1)
                own.step(nc.vector.tensor_copy(sif[:, h % 2, :, :, :], si[:, :, :, :]))
                own.link(nc.vector.tensor_tensor(
                    cand[:, :, :].rearrange("p n (a b) -> p n a b", a=TOPK),
                    sv[:, 0, :, :].unsqueeze(3).to_broadcast([P, nb, TOPK, TOPK]),
                    sv[:, 1, :, :].unsqueeze(2).to_broadcast([P, nb, TOPK, TOPK]), ALU.add))
                top16(range(nb), lambda r, j: best[:, r, 8 * j:8 * j + 8], lambda r, j: pos[:, r, 8 * j:8 * j + 8],
                      lambda r: cand[:, r, :], lambda r: cand2[:, r, :])
                nc.vector.tensor_tensor(pick[:, :, 2, choices], best[:, :, :],
                                        best[:, :, 0:1].to_broadcast([P, nb, TOPK]), ALU.subtract).then_inc(diffed, 1)
                own.step(nc.vector.tensor_scalar(part[:, 0, :, :], pos[:, :, :], 4, None, ALU.logical_shift_right))
                own.step(nc.vector.tensor_scalar(part[:, 1, :, :], pos[:, :, :], 15, None, ALU.bitwise_and))
                own.meet()
                own.link(nc.vector.tensor_copy(partf[:, :, :, :], part[:, :, :, :]))
                for c in range(2):
                    ins = nc.vector.tensor_tensor(
                        eq[:, c, :, :, :].rearrange("p n a b -> p (n a) b"),
                        partf[:, c, :, :].rearrange("p n k -> p (n k)").unsqueeze(2).to_broadcast([P, nb * TOPK, TOPK]),
                        m.sq[:, C_IOTA:C_IOTA + 1, 0:TOPK].to_broadcast([P, nb * TOPK, TOPK]), ALU.is_equal)
                ins.then_inc(placed, 1)
            keys(PH - 1)
            dve.wait_ge(g_exp, 1)
            if side:
                dve.wait_ge(products_out, 1)
                dve.wait_ge(vecs_out, 1)
                finish_modulation(nc, m, own, m.products, m.products[:, :, :].rearrange("p j r -> p (j r)"), 0, 6 * KD)
            weights = pick[:, :, 2, :].rearrange("p n (h k) -> p n h k", h=PH)
            own.link(nc.vector.tensor_reduce(dn[:, :, :], weights, axis=AX.X, op=ALU.add))
            own.link(nc.vector.reciprocal(dn[:, :, :], dn[:, :, :]))
            nc.vector.tensor_tensor(weights, weights, dn[:, :, :].unsqueeze(3).to_broadcast([P, nb, PH, TOPK]), ALU.mult
                                    ).then_inc(picked, 1)


def peer_weights(nc, m, sel, wd, t0):
    GRP = 4
    STEP = 16
    TURNS = P // STEP
    G = STEP // GRP
    BY_POOL = tuple(range(STEP // 2))
    done = lambda who, g: len([s for s in who if s < (g + 1) * GRP])
    blocks = list(range(t0 // P, NB))
    with ExitStack() as ctx:
        ia = ctx.enter_context(sbuf(nc, "hot_i", [P, STEP, P], F32))
        ib = ctx.enter_context(sbuf(nc, "hot_j", [P, STEP, P], F32))
        wsb = ctx.enter_context(sbuf(nc, "w_block", [P, 2, P, P], F32))
        keys = ctx.enter_context(sbuf(nc, "keys", [P, STEP], F32))
        (block, slots_seen, keys_in, hot_i, hot_j, w_mult, w_out, w_stored0, w_stored1) = ctx.enter_context(
            stage(nc, "slots_seen", "keys_in", "hot_i", "hot_j", "w_mult", "w_out", "w_stored0", "w_stored1"))
        w_stored = (w_stored0, w_stored1)

        @block.vector
        def _(dve):
            dve.sem_inc(w_mult, G)
            for n, b in enumerate(blocks):
                with dve.Fori(0, TURNS) as i:
                    for s in range(STEP):
                        if s % GRP == 0:
                            dve.wait_ge(w_mult, i * G + (n * TURNS * G + s // GRP + 1))
                        tok = i * STEP + (b * P + s)
                        if s % GRP == 0 and s not in BY_POOL:
                            nc.vector.tensor_tensor(
                                ib[:, s:s + GRP, :], m.sq[:, C_IOTA:C_IOTA + 1, :].to_broadcast([P, GRP, P]),
                                sel[:, 1, bass.ds(tok, GRP)].unsqueeze(2).to_broadcast([P, GRP, P]), ALU.is_equal)
                        nc.vector.tensor_scalar(ia[:, s, :], m.sq[:, C_IOTA, :], sel[:, 0, bass.ds(tok, 1)],
                                                sel[:, 2, bass.ds(tok, 1)], ALU.is_equal, ALU.mult).then_inc(hot_i, 1)

        @block.gpsimd
        def _(pool):
            for n, b in enumerate(blocks):
                with pool.Fori(0, TURNS) as i:
                    nc.gpsimd.tensor_copy(keys[:, :], sel[:, 1, bass.ds(i * STEP + b * P, STEP)]).then_inc(keys_in, 1)
                    pool.wait_ge(keys_in, i + (n * TURNS + 1))
                    for s in BY_POOL:
                        if s % GRP == 0:
                            pool.wait_ge(w_mult, i * G + (n * TURNS * G + s // GRP + 1))
                            pool.sem_inc(slots_seen, 1)
                        nc.gpsimd.tensor_scalar(ib[:, s, :], m.sq[:, C_IOTA, :], keys[:, s:s + 1], None,
                                                ALU.is_equal).then_inc(hot_j, 1)
                    pool.wait_ge(hot_j, i * len(BY_POOL) + (n * TURNS + 1) * len(BY_POOL))

        @block.tensor
        def _(pe):
            for n, b in enumerate(blocks):
                with pe.Fori(0, TURNS) as i:
                    for g in range(G):
                        pe.wait_ge(hot_i, i * STEP + (n * P + (g + 1) * GRP))
                        pe.wait_ge(hot_j, i * len(BY_POOL) + (n * TURNS * len(BY_POOL) + done(BY_POOL, g)))
                        pe.wait_ge(w_out, i * G + (n * TURNS * G + g + 1))
                        for s in range(GRP):
                            ins = nc.tensor.matmul(m.ps[:, g, s * P:(s + 1) * P], ib[:, g * GRP + s, :],
                                                   ia[:, g * GRP + s, :], start=True, stop=True)
                        ins.then_inc(w_mult, 1)

        @block.scalar
        def _(act):
            act.sem_inc(w_out, G)
            for n, b in enumerate(blocks):
                if n >= 2:
                    act.wait_ge(w_stored[n % 2], 16 * (n // 2))
                with act.Fori(0, TURNS) as i:
                    for g in range(G):
                        act.wait_ge(w_mult, i * G + ((n * TURNS + 1) * G + g + 1))
                        nc.scalar.copy(wsb[:, n % 2, :, bass.ds(i * STEP + g * GRP, GRP)],
                                       m.ps[:, g, :].rearrange("p (s i) -> p i s", s=GRP)).then_inc(w_out, 1)

        @block.sync
        def _(sp):
            for n, b in enumerate(blocks):
                sp.wait_ge(w_out, (n + 1) * TURNS * G + G)
                sp.dma_start(wd.rearrange("i j t -> j i t")[:, :, b * P:(b + 1) * P], wsb[:, n % 2, :, :]
                             ).then_inc(w_stored[n % 2], 16)
            for n in range(max(0, len(blocks) - 2), len(blocks)):
                sp.wait_ge(w_stored[n % 2], 16 * (n // 2 + 1))


def peer_experts(nc, m, d, hs, wd, l, t0):
    T = TOK - t0
    GRP = 2
    NG = NK // GRP
    KO = KD // GRP
    halves = [(kind, lo, hi) for kind, lo, hi in ((1, 0, CTX), (0, CTX, TOK)) if lo >= t0]
    ug = d["peer_u"][l].rearrange("(g q j) n -> g j q n", q=GRP, j=P)
    vg = d["peer_v"][l].rearrange("(g q j) n -> g j q n", q=GRP, j=P)
    wg = wd.rearrange("(g q) j t -> g j q t", q=GRP)
    with ExitStack() as ctx:
        sb = lambda name, shape, dt=F32: ctx.enter_context(sbuf(nc, name, shape, dt))
        us = [sb(f"u{i}", [P, GRP, D]) for i in range(2)]
        vs = [sb(f"v{i}", [P, GRP, D]) for i in range(2)]
        vr = [sb(f"v_split{i}", [P, 2, GRP, D], F32R) for i in range(2)]
        ws = [sb(f"w{i}", [P, GRP, T]) for i in range(2)]
        ut = sb("uT", [P, 2, 2, KD * P], F32R)
        ga = sb("gelu", [P, 2, T])
        wf = sb("weighted", [P, 2, T])
        wa = sb("w_split", [P, 2, 2, GRP, T], F32R)
        acc = sb("experts_out", [P, KD, T])
        (block, u_in0, u_in1, v_in0, v_in1, w_in0, w_in1, u_turned, u_rounded, u_rested, v_rounded, v_rested, a_mult,
         gelu_done, weighted, wa_rounded, wa_done, o_mult, o_out, dve_own) = ctx.enter_context(stage(
             nc, "u_in0", "u_in1", "v_in0", "v_in1", "w_in0", "w_in1", "u_turned", "u_rounded", "u_rested",
             "v_rounded", "v_rested", "a_mult", "gelu_done", "weighted", "wa_rounded", "wa_done", "o_mult", "o_out",
             "dve_own"))
        u_ins, v_ins, w_ins = (u_in0, u_in1), (v_in0, v_in1), (w_in0, w_in1)

        def ahead(work, pair, r, q, first, last):
            if q + 1 < GRP:
                work(pair, r, q + 1, first)
            elif r == 0:
                work(pair, 1, 0, first)
            elif not last:
                work(pair + 1, 0, 0, False)

        def pairs(engine, group):
            group(0, 0, True, False)
            group(0, 1, True, False)
            with engine.Fori(1, NG // 2 - 1) as i:
                group(i, 0, False, False)
                group(i, 1, False, False)
            group(NG // 2 - 1, 0, False, True)
            group(NG // 2 - 1, 1, False, True)

        @block.sync
        def _(sp):
            def pair(i, first):
                for r in range(2):
                    g = 2 * i + r
                    if not first:
                        sp.wait_ge(u_turned, i * (2 * GRP) + (r - 1) * GRP)
                    sp.dma_start(us[r][:, :, :], ug[g]).then_inc(u_ins[r], 16)
                    if not first:
                        sp.wait_ge(wa_done, i * (2 * GRP) + (r - 1) * GRP)
                    sp.dma_start(ws[r][:, :, :], wg[g][:, :, t0:]).then_inc(w_ins[r], 16)
                    if not first:
                        sp.wait_ge(v_rested, i * 2 + (r - 1))
                    sp.dma_start(vs[r][:, :, :], vg[g]).then_inc(v_ins[r], 16)

            pair(0, True)
            with sp.Fori(1, NG // 2) as i:
                pair(i, False)

        @block.gpsimd
        def _(pool):
            def pair(i):
                for r in range(2):
                    pool.wait_ge(v_rounded, i * 2 + (r + 1))
                    nc.gpsimd.tensor_tensor(vr[r][:, 1], vs[r][:, :, :], vr[r][:, 0].bitcast(F32), ALU.subtract
                                            ).then_inc(v_rested, 1)

            pair(0)
            with pool.Fori(1, NG // 2) as i:
                pair(i)

        @block.tensor
        def _(pe):
            def turn(pair, r, q, first):
                n = pair * (2 * GRP) + (r * GRP + q)
                if q == 0:
                    pe.wait_ge(u_ins[r], pair * 16 + 16)
                if not (first and r == 0):
                    pe.wait_ge(u_rested, n - 1)
                for k in range(KD):
                    ins = nc.tensor.transpose(m.ps[:, 2 * q + k // 4, (k % 4) * P:(k % 4 + 1) * P],
                                              us[r][:, q, k * P:(k + 1) * P], m.sq[:, C_ID, :])
                ins.then_inc(u_turned, 1)

            def activations(pair, r, q, first):
                n = pair * (2 * GRP) + (r * GRP + q)
                pe.wait_ge(u_rested, n + 1)
                if not (first and r == 0):
                    pe.wait_ge(gelu_done, n - 1)
                for k in range(KD):
                    ins = split_matmul(nc, m.ps[:, 4 + q, 0:T], lambda s: ut[:, q, s, k * P:(k + 1) * P],
                                       lambda s: hs[:, s, k, t0:], k == 0, k == KD - 1)
                ins.then_inc(a_mult, 1)

            def outputs(pair, r, q, first):
                if q == 0:
                    pe.wait_ge(wa_done, pair * (2 * GRP) + r * GRP)
                    pe.wait_ge(v_rested, pair * 2 + r)
                for k in range(KO * q, KO * q + KO):
                    if not (first and r == 1 and k < 2):
                        pe.wait_ge(o_out, pair * (2 * KD) + ((r - 1) * KD + k - 1))
                    for e in range(GRP):
                        ins = split_matmul(nc, m.ps[:, 6 + k % 2, 0:T], lambda s: vr[1 - r][:, s, e, k * P:(k + 1) * P],
                                           lambda s: wa[:, 1 - r, s, e, :], e == 0, e == GRP - 1)
                    ins.then_inc(o_mult, 1)

            def group(pair, r, first, last):
                for q in range(GRP):
                    ahead(turn, pair, r, q, first, last)
                    activations(pair, r, q, first)
                    if not (first and r == 0):
                        outputs(pair, r, q, first)

            turn(0, 0, 0, True)
            pairs(pe, group)
            for q in range(GRP):
                outputs(NG // 2, 0, q, False)

        @block.scalar
        def _(act):
            def round_u(pair, r, q, first):
                n = pair * (2 * GRP) + (r * GRP + q)
                act.wait_ge(u_turned, n + 1)
                if not (first and r == 0):
                    act.wait_ge(a_mult, n - 1)
                for b in range(2):
                    nc.scalar.copy(ut[:, q, 0, b * BANK:(b + 1) * BANK], m.ps[:, 2 * q + b, :]).then_inc(u_rounded, 1)

            def group(pair, r, first, last):
                for q in range(GRP):
                    n = pair * (2 * GRP) + (r * GRP + q)
                    ahead(round_u, pair, r, q, first, last)
                    if q == 0:
                        act.wait_ge(v_ins[r], pair * 16 + 16)
                        if not first:
                            act.wait_ge(o_mult, pair * (2 * KD) + (r - 1) * KD)
                    ins = nc.scalar.copy(vr[r][:, 0, q], vs[r][:, q, :])
                    if q == GRP - 1:
                        ins.then_inc(v_rounded, 1)
                    act.wait_ge(a_mult, n + 1)
                    if not (first and r == 0):
                        act.wait_ge(weighted, n - 1)
                    nc.scalar.activation(ga[:, q, :], m.ps[:, 4 + q, 0:T], ACT.Gelu_apprx_tanh).then_inc(gelu_done, 1)

            round_u(0, 0, 0, True)
            pairs(act, group)

        @block.vector
        def _(dve):
            def add_out(pair, r, q):
                for k in range(KO * q, KO * q + KO):
                    dve.wait_ge(o_mult, pair * (2 * KD) + ((r - 1) * KD + k + 1))
                    nc.vector.tensor_tensor(acc[:, k, :], acc[:, k, :], m.ps[:, 6 + k % 2, 0:T], ALU.add).then_inc(o_out, 1)

            def rest_u(pair, r, q, first):
                n = pair * (2 * GRP) + (r * GRP + q)
                for b in range(2):
                    dve.wait_ge(u_rounded, n * 2 + (b + 1))
                    ins = nc.vector.tensor_tensor(ut[:, q, 1, b * BANK:(b + 1) * BANK], m.ps[:, 2 * q + b, :],
                                                  ut[:, q, 0, b * BANK:(b + 1) * BANK].bitcast(F32), ALU.subtract)
                ins.then_inc(u_rested, 1)

            def weigh(pair, r, q, first):
                n = pair * (2 * GRP) + (r * GRP + q)
                if q == 0:
                    dve.wait_ge(w_ins[r], pair * 16 + 16)
                    if not first:
                        dve.wait_ge(o_mult, pair * (2 * KD) + (r - 1) * KD)
                dve.wait_ge(gelu_done, n + 1)
                nc.vector.tensor_tensor(wf[:, q, :], ga[:, q, :], ws[r][:, q, :], ALU.mult).then_inc(weighted, 1)
                dve.wait_ge(weighted, n + 1)
                nc.vector.tensor_copy(wa[:, r, 0, q, :], wf[:, q, :]).then_inc(wa_rounded, 1)
                dve.wait_ge(wa_rounded, n + 1)
                nc.vector.tensor_tensor(wa[:, r, 1, q, :], wf[:, q, :], wa[:, r, 0, q, :].bitcast(F32), ALU.subtract
                                        ).then_inc(wa_done, 1)

            def group(pair, r, first, last):
                for q in range(GRP):
                    ahead(rest_u, pair, r, q, first, last)
                    if not (first and r == 0):
                        add_out(pair, r, q)
                    weigh(pair, r, q, first)

            own = Chain(dve, dve_own)
            own.link(nc.vector.memset(acc[:, :, :], 0.0))
            rest_u(0, 0, 0, True)
            pairs(dve, group)
            for q in range(GRP):
                add_out(NG // 2, 0, q)
            dve.wait_ge(o_out, NG * KD)
            for k in range(KD):
                for kind, lo, hi in halves:
                    nc.vector.scalar_tensor_tensor(
                        out=m.resid[:, k, lo:hi], in0=acc[:, k, lo - t0:hi - t0],
                        scalar=m.mod[:, 5 * KD + k, kind:kind + 1], in1=m.resid[:, k, lo:hi], op0=ALU.mult, op1=ALU.add)


def store(nc, m, out):
    with ExitStack() as ctx:
        tok = ctx.enter_context(sbuf(nc, "tok", [P, 2, D], F32))
        block, turned, copied, stored = ctx.enter_context(stage(nc, "turned", "copied", "stored"))

        @block.tensor
        def _(pe):
            for b in range(2):
                for k in range(KD):
                    ins = nc.tensor.transpose(m.ps[:, 2 * b + k // 4, (k % 4) * P:(k % 4 + 1) * P],
                                              m.resid[:, k, CTX + b * P:CTX + (b + 1) * P], m.sq[:, C_ID, :])
                    if k % 4 == 3:
                        ins.then_inc(turned, 1)

        @block.scalar
        def _(act):
            for i in range(4):
                act.wait_ge(turned, i + 1)
                nc.scalar.copy(tok[:, i // 2, (i % 2) * 512:(i % 2) * 512 + 512], m.ps[:, i, :]).then_inc(copied, 1)

        @block.sync
        def _(sp):
            sp.wait_ge(copied, 4)
            sp.dma_start(out[0].rearrange("(b p) n -> p b n", p=P), tok[:, :, :]).then_inc(stored, 16)
            sp.wait_ge(stored, 16)


def build(nc, d, out):
    NUMBER[:] = [0, 0]
    wd = nc.dram_tensor("peer_w", (NK, NK, TOK), F32, kind="Internal").ap()
    m = Mem()
    t = Mem()
    with ExitStack() as ctx:
        sb = lambda name, shape: ctx.enter_context(sbuf(nc, name, shape, F32))
        m.ps = ctx.enter_context(nc.psum_tensor("ps", [P, BANKS, BANK], F32))
        m.sq = sb("squares", [P, C_N, P])
        m.resid = sb("resid", [P, KD, TOK])
        m.cond = sb("cond", [P, KD, 2])
        m.vec = sb("vec", [P, V_ROWS])
        m.mod = sb("mod", [P, 6 * KD, 2])
        m.products = sb("mod_products", [P, 6 * KD, 2])
        m.eps = sb("eps", [P, 1])
        setup(nc, m, d)
        for l in range(LAYERS):
            last = l == LAYERS - 1
            own0 = CTX if last else 0
            if l == 0:
                modulation(nc, m, d)
            with sbuf(nc, "h_split", [P, 2, KD, TOK], F32R) as hs:
                with ExitStack() as inner:
                    tb = lambda name, shape: inner.enter_context(sbuf(nc, name, shape, F32))
                    t.yT, t.hy = tb("yT", [P, N_BRANCH, 2, TOK]), tb("hy", [P, 6, TOK])
                    t.dec, t.feat = tb("decay", [P, KF, HY_W]), tb("feat", [33, SEQ])
                    t.w1, t.w2, t.w3 = tb("w1", [33, 64]), tb("w2", [64, 64]), tb("w3", [64, 4 * HY_W])
                    with ExitStack() as branch:
                        tb = lambda name, shape: branch.enter_context(sbuf(nc, name, shape, F32))
                        t.ckv, t.kpe, t.cq = tb("ckv", [P, TOK]), tb("kpe", [P, TOK]), tb("cq", [P, 2, TOK])
                        t.gq, t.gk, t.gv = tb("gq", [P, 2, TOK]), tb("gk", [P, TOK]), tb("gv", [P, NB, P])
                        t.mq, t.mk = tb("mq", [P, 2, TOK]), tb("mk", [P, 2, TOK])
                        t.mvo, t.mg = tb("mvo", [P, NB, 2 * ML_W]), tb("mg", [P, NB, 4 * ML_H])
                        with ExitStack() as heads:
                            tb = lambda name, shape: heads.enter_context(sbuf(nc, name, shape, F32))
                            t.wuq, t.wukv = tb("wuq", [P, 2, MLA_H * MLA_QK]), tb("wukv", [P, MLA_H * (MLA_NOPE + MLA_V)])
                            t.rope = tb("rope", [P, 4, TOK])
                            with weight_ring(nc, CW) as ring:
                                mod_norm(nc, m, hs, 0, 0, ring, columns(d["w_in"][l], (0, 256, 512)))
                                input_projection(nc, m, d, hs, t, l, own0, ring)
                            t.qm, t.km = tb("qm", [P, MLA_H, TOK]), tb("km", [P, MLA_H, TOK])
                            t.vm = tb("vm", [P, NB, MLA_H * MLA_V])
                            attention_heads(nc, m, d, t, l, own0)
                            attention(nc, m, t, range(own0 // P, NB))
                        mlstm(nc, m, d, t, l, range(own0 // P, NB))
                    ring = Mem()
                    ring.raw = inner.enter_context(sbuf(nc, "wg_raw", [P, 2, KD, 2, P], F32))
                    ring.split = [inner.enter_context(sbuf(nc, "wg_split0", [P, 2, KD, 2, P], F32R))]
                    hyena(nc, m, d, t, l, (1,) if last else (0, 1), ring)
                    merge(nc, m, d, hs, t, l, own0, ring)
                with sbuf(nc, "sel", [P, 3, TOK], F32) as sel:
                    with weight_ring(nc, QCH) as ring:
                        mod_norm(nc, m, hs, 3 * KD, own0, ring, columns(d["peer_wq"][l], (0, QCH, 2 * QCH)))
                        peer_select(nc, m, d, hs, sel, l, own0, ring)
                    peer_weights(nc, m, sel, wd, own0)
                peer_experts(nc, m, d, hs, wd, l, own0)
                m.mod, m.products = m.products, m.mod
        store(nc, m, out)



_INS = ["x", "c", "ctx", "c_ctx", "ada_w", "ada_b", "norm1", "norm2", "w_in", "mla_q_norm", "mla_kv_norm",
        "mla_w_uq", "mla_w_ukv", "mla_qk_norm_q", "mla_qk_norm_k", "gqa_qk_norm_q", "gqa_qk_norm_k", "ml_gate_b",
        "ml_norm", "hy_conv", "hy_w1", "hy_b1", "hy_freq", "hy_w2", "hy_b2", "hy_w3", "hy_bias", "w_branch", "w_out",
        "peer_wq", "peer_subkeys", "peer_u", "peer_v"]


def _constants():
    import math

    import numpy as np

    f = np.float32
    r, c = np.arange(P)[:, None], np.arange(P)[None, :]
    rot = {}
    for name, base, half, n in (("m", MLA_NOPE, 8, 2), ("g", 0, 16, 4)):
        a = np.zeros((P, P), f)
        for s in range(n):
            for j in range(half):
                lo = base + s * 2 * half + j
                a[lo + half, lo] = -1
                a[lo, lo + half] = 1
        rot[name] = a
    square = np.concatenate([
        r == c, np.ones((P, P)), r // HD == c // HD, r <= c, r >= c, r > c, r < c,
        np.where(c > r, -1e30, 0), np.where(c < r, -1e30, 0), rot["m"], rot["g"], np.broadcast_to(c, (P, P))]).astype(f)
    grid_w = 64
    pos = (np.arange(LAT) // grid_w, np.arange(LAT) % grid_w)
    rope = np.zeros((4, P, TOK), f)
    rope[0::2] = 1
    for i, (base, half, reps) in enumerate(((MLA_NOPE, 8, 1), (0, 16, 2))):
        inv = (f(10000.0) ** (-np.arange(0, 2 * half, 2, dtype=f) / f(2 * half))).astype(f)
        for rep in range(reps):
            for ax in range(2):
                ang = (pos[ax].astype(f)[:, None] * inv).T
                for side in range(2):
                    at = base + rep * HD + ax * 2 * half + side * half
                    rope[2 * i, at:at + half, CTX:] = np.cos(ang)
                    rope[2 * i + 1, at:at + half, CTX:] = np.sin(ang)
    n = np.arange(SEQ)
    ang = 2 * np.pi * np.outer(n, n + 0.5) / (2 * SEQ)
    dft = np.stack([np.cos(ang), -np.sin(ang), np.cos(ang).T / SEQ, -np.sin(ang).T / SEQ]).astype(f)
    tt = np.arange(SEQ, dtype=f) / f(SEQ)
    a2 = f(2.0 * math.pi) * tt[:, None] * np.arange(1, 17, dtype=f)
    feat = np.concatenate([tt[:, None], np.sin(a2), np.cos(a2)], axis=1).T.astype(f)
    lt = math.log(1e-2)
    alpha = np.linspace(-lt / 1.5, -lt / 0.3, HY_W, dtype=f)
    decay = np.exp(-tt[:, None] * alpha).astype(f)
    return {"k_square": square, "k_rope": rope.reshape(4 * P, TOK), "k_dft": dft, "k_feat": feat, "k_decay": decay}


def kernel(**inputs):
    import numpy as _np
    import concourse.bacc as _bacc
    from concourse.bass_utils import run_bass_kernel_spmd as _run

    nc = _bacc.Bacc("TRN2", target_bir_lowering=False, num_devices=1)
    arrays, d = {}, {}
    for name, a in [(n, inputs[n]) for n in _INS] + list(_constants().items()):
        a = _np.ascontiguousarray(a)
        arrays[f"in_{name}"] = a
        d[name] = nc.dram_tensor(f"in_{name}", a.shape, mybir.dt.from_np(a.dtype), kind="ExternalInput").ap()
    out = nc.dram_tensor("out", (1, LAT, D), F32, kind="ExternalOutput").ap()
    build(nc, d, out)
    r = _run(nc, [arrays], core_ids=[0])
    return r.results[0]["out"]
```
